# Optimizing a Trainium2 kernel written in Bass

```python
import math
import jax, jax.numpy as jnp
from jax import lax
import numpy as np
import jax
import jax.numpy as jnp

D_MODEL = 1024
BATCH = 1
SEQ = 1024
DEPTH = 1

HEAD_DIM = 64
HEADS_PER_GROUP = 8
DILATED_GROUPS = ((128, 1), (512, 4), (2048, 16))
N_GROUPS = len(DILATED_GROUPS)
N_ATTN_HEADS = N_GROUPS * HEADS_PER_GROUP
ATTN_W = N_ATTN_HEADS * HEAD_DIM
ATTN_OUT_W = HEADS_PER_GROUP * HEAD_DIM
BLOCK = 128
REL_BUCKETS = 32
REL_MAX_DISTANCE = 2048
CONV_CHANNELS = D_MODEL
CONV_WIDTH = 31
FFN_HIDDEN = -(-8 * D_MODEL // (3 * 256)) * 256
IN_W = 3 * ATTN_W + 2 * CONV_CHANNELS + 2 * D_MODEL
RMS_EPS = 1e-6
LN_EPS = 1e-5
NEG_INF = -1e30


def rms_norm(x, g):
    xf = x.astype(jnp.float32)
    y = xf * lax.rsqrt(jnp.mean(xf * xf, axis=-1, keepdims=True) + RMS_EPS)
    return (y * g.astype(jnp.float32)).astype(x.dtype)

def layer_norm(x, g, b):
    xf = x.astype(jnp.float32)
    mu = jnp.mean(xf, axis=-1, keepdims=True)
    xc = xf - mu
    y = xc * lax.rsqrt(jnp.mean(xc * xc, axis=-1, keepdims=True) + LN_EPS)
    return (y * g.astype(jnp.float32) + b.astype(jnp.float32)).astype(x.dtype)

def rel_bucket(dist):
    max_exact = REL_BUCKETS // 2
    d = jnp.maximum(dist, 0)
    df = jnp.maximum(d, 1).astype(jnp.float32)
    large = max_exact + (jnp.log(df / max_exact) / math.log(REL_MAX_DISTANCE / max_exact)
                         * (REL_BUCKETS - max_exact)).astype(jnp.int32)
    large = jnp.minimum(large, REL_BUCKETS - 1)
    return jnp.where(d < max_exact, d, large)

def dilated_group_attention(q, k, v, bias_tab, window, dilation):
    B, S, H, Dh = q.shape
    span = window // dilation
    L = S // dilation
    nb = -(-L // BLOCK)
    Lp = nb * BLOCK
    n_prev = -(-span // BLOCK)
    kb_len = (n_prev + 1) * BLOCK

    def to_sub(t, front):
        t = t.reshape(B, L, dilation, H, Dh).transpose(0, 2, 1, 3, 4)
        return jnp.pad(t, ((0, 0), (0, 0), (front, Lp - L), (0, 0), (0, 0)))

    qb = to_sub(q, 0).reshape(B, dilation, nb, BLOCK, H, Dh)

    def band(t):
        tb = to_sub(t, n_prev * BLOCK).reshape(B, dilation, nb + n_prev, BLOCK, H, Dh)
        return jnp.concatenate([tb[:, :, j:j + nb] for j in range(n_prev + 1)], axis=3)

    kb, vb = band(k), band(v)
    a = jnp.arange(BLOCK, dtype=jnp.int32)[:, None]
    c = jnp.arange(kb_len, dtype=jnp.int32)[None, :]
    offset = a - c + n_prev * BLOCK
    bias = bias_tab[rel_bucket(offset * dilation)].astype(jnp.float32).transpose(2, 0, 1)
    kj = (jnp.arange(nb, dtype=jnp.int32)[:, None, None] - n_prev) * BLOCK + c[None]
    valid = (offset >= 0) & (offset <= span) & (kj >= 0)

    s = jnp.einsum('brnqhd,brnkhd->brnhqk', qb, kb).astype(jnp.float32) * (Dh ** -0.5) + bias
    s = jnp.where(valid[:, None], s, NEG_INF)
    lse = jax.nn.logsumexp(s, axis=-1)
    p = jnp.exp(s - lse[..., None])
    o = jnp.einsum('brnhqk,brnkhd->brnqhd', p, vb.astype(jnp.float32))
    o = o.reshape(B, dilation, Lp, H, Dh)[:, :, :L].transpose(0, 2, 1, 3, 4).reshape(B, S, H, Dh)
    lse = lse.transpose(0, 1, 2, 4, 3).reshape(B, dilation, Lp, H)[:, :, :L]
    lse = lse.transpose(0, 2, 1, 3).reshape(B, S, H)
    return o, lse

def dilated_attention_mixer(q, k, v, rel_bias_table, w_attn_out):
    B, S = q.shape[0], q.shape[1]
    outs, lses = [], []
    for g, (window, dilation) in enumerate(DILATED_GROUPS):
        tab = rel_bias_table[:, g * HEADS_PER_GROUP:(g + 1) * HEADS_PER_GROUP]
        o_g, lse_g = dilated_group_attention(q[:, :, g], k[:, :, g], v[:, :, g], tab, window, dilation)
        outs.append(o_g)
        lses.append(lse_g)
    alpha = jax.nn.softmax(jnp.stack(lses, axis=0), axis=0)
    o = jnp.einsum('gbsh,gbshd->bshd', alpha, jnp.stack(outs, axis=0))
    o = o.reshape(B, S, ATTN_OUT_W).astype(w_attn_out.dtype)
    return o @ w_attn_out

def conformer_conv_mixer(glu_in, b_glu, w_dw, b_dw, g_ln, b_ln, w_conv_out, b_conv_out):
    h = glu_in + b_glu
    u, gate = jnp.split(h, 2, axis=-1)
    u = u * jax.nn.sigmoid(gate)
    u = lax.conv_general_dilated(
        u, w_dw.reshape(CONV_WIDTH, 1, CONV_CHANNELS).astype(u.dtype),
        window_strides=(1,), padding=[(CONV_WIDTH - 1, 0)],
        dimension_numbers=('NWC', 'WIO', 'NWC'),
        feature_group_count=CONV_CHANNELS) + b_dw
    u = jax.nn.silu(layer_norm(u, g_ln, b_ln))
    return u @ w_conv_out + b_conv_out

def swiglu_ffn(h, w_ffn_in, w_ffn_out):
    gate, up = jnp.split(h @ w_ffn_in, 2, axis=-1)
    return (jax.nn.silu(gate) * up) @ w_ffn_out

def first_inputs(seed: int = 0) -> dict:
    key = jax.random.key(seed)
    ks = jax.random.split(key, 20)
    f32 = jnp.float32

    def nrm(k, shape, scale):
        return jax.random.normal(k, shape, f32) * scale

    def gain(k, shape):
        return 1.0 + 0.05 * jax.random.normal(k, shape, f32)

    return {
        "x": jax.random.normal(ks[0], (BATCH, SEQ, D_MODEL), f32),
        "rel_bias_table": nrm(ks[1], (REL_BUCKETS, N_ATTN_HEADS), 0.2),
        "g_pre_mix": gain(ks[2], (DEPTH, D_MODEL)),
        "w_in": nrm(ks[3], (DEPTH, D_MODEL, IN_W), D_MODEL ** -0.5),
        "b_glu": nrm(ks[4], (DEPTH, 2 * CONV_CHANNELS), 0.02),
        "w_dw": nrm(ks[5], (DEPTH, CONV_WIDTH, CONV_CHANNELS), CONV_WIDTH ** -0.5),
        "b_dw": nrm(ks[6], (DEPTH, CONV_CHANNELS), 0.02),
        "g_conv_ln": gain(ks[7], (DEPTH, CONV_CHANNELS)),
        "b_conv_ln": nrm(ks[8], (DEPTH, CONV_CHANNELS), 0.02),
        "w_conv_out": nrm(ks[9], (DEPTH, CONV_CHANNELS, D_MODEL), CONV_CHANNELS ** -0.5),
        "b_conv_out": nrm(ks[10], (DEPTH, D_MODEL), 0.02),
        "w_attn_out": nrm(ks[11], (DEPTH, ATTN_OUT_W, D_MODEL), ATTN_OUT_W ** -0.5),
        "w_mix_out": nrm(ks[12], (DEPTH, D_MODEL, D_MODEL), D_MODEL ** -0.5),
        "g_post_mix": gain(ks[13], (DEPTH, D_MODEL)),
        "g_pre_ffn": gain(ks[14], (DEPTH, D_MODEL)),
        "w_ffn_in": nrm(ks[15], (DEPTH, D_MODEL, 2 * FFN_HIDDEN), D_MODEL ** -0.5),
        "w_ffn_out": nrm(ks[16], (DEPTH, FFN_HIDDEN, D_MODEL), FFN_HIDDEN ** -0.5),
        "g_post_ffn": gain(ks[17], (DEPTH, D_MODEL)),
    }

def first_block(x, rel_bias_table, g_pre_mix, w_in, b_glu, w_dw, b_dw, g_conv_ln, b_conv_ln,
              w_conv_out, b_conv_out, w_attn_out, w_mix_out, g_post_mix, g_pre_ffn,
              w_ffn_in, w_ffn_out, g_post_ffn):
    B, S, D = x.shape
    for l in range(DEPTH):
        h = rms_norm(x, g_pre_mix[l])
        z = h @ w_in[l]
        q, k, v, glu_in, z_ga, z_gc = jnp.split(
            z, np.cumsum([ATTN_W, ATTN_W, ATTN_W, 2 * CONV_CHANNELS, D_MODEL]).tolist(), axis=-1)
        shp = (B, S, N_GROUPS, HEADS_PER_GROUP, HEAD_DIM)
        y_attn = dilated_attention_mixer(q.reshape(shp), k.reshape(shp), v.reshape(shp),
                                         rel_bias_table, w_attn_out[l])
        y_conv = conformer_conv_mixer(glu_in, b_glu[l], w_dw[l], b_dw[l], g_conv_ln[l],
                                      b_conv_ln[l], w_conv_out[l], b_conv_out[l])
        merged = jax.nn.sigmoid(z_ga) * y_attn + jax.nn.sigmoid(z_gc) * y_conv
        x = x + rms_norm(merged @ w_mix_out[l], g_post_mix[l])
        h = rms_norm(x, g_pre_ffn[l])
        x = x + rms_norm(swiglu_ffn(h, w_ffn_in[l], w_ffn_out[l]), g_post_ffn[l])
    return x


GRID_W = 64
CTX_LEN = 256
DN_HEADS = 4
DN_HEAD_DIM = 128
DN_WIDTH = DN_HEADS * DN_HEAD_DIM
SHORT_CONV = 5
CHUNK = 64
POOL_GROUPS = 4
POOL_WINDOWS = (2, 4, 8, 16)
POOL_WIDTH = D_MODEL - DN_WIDTH
POOL_GROUP_DIM = POOL_WIDTH // POOL_GROUPS
MIX_WIDTH = DN_WIDTH + POOL_WIDTH
D_FF = 128 * ((8 * D_MODEL // 3 + 127) // 128)
FFN_CONV = 3
N_MOD = 6
NORM_EPS = 1e-6
Q_OFF = 0
K_OFF = DN_WIDTH
V_OFF = 2 * DN_WIDTH
Z_OFF = 3 * DN_WIDTH
GATE_OFF = 4 * DN_WIDTH
POOL_OFF = GATE_OFF + 4 * DN_HEADS
IN_COLS = POOL_OFF + POOL_WIDTH


def rms_norm_2(x, g):
    xf = x.astype(jnp.float32)
    y = xf * lax.rsqrt(jnp.mean(xf * xf, axis=-1, keepdims=True) + NORM_EPS)
    return (y * g.astype(jnp.float32)).astype(x.dtype)

def l2_normalize(x):
    xf = x.astype(jnp.float32)
    return xf * lax.rsqrt(jnp.sum(xf * xf, axis=-1, keepdims=True) + NORM_EPS)

def modulation(cond, w_mod, b_mod):
    m = jax.nn.silu(cond) @ w_mod + b_mod
    return jnp.split(m[..., None, :], N_MOD, axis=-1)

def depthwise_conv(x, w):
    pad = w.shape[0] // 2
    return lax.conv_general_dilated(x, w[:, None, :], window_strides=(1,), padding=[(pad, pad)],
                                    dimension_numbers=('NWC', 'WIO', 'NWC'),
                                    feature_group_count=x.shape[-1])

def split_heads(a):
    return a.reshape(*a.shape[:-1], -1, DN_HEAD_DIM)

def gated_delta_rule(q, k, v, g, beta, s0):
    bsz, t, nh, dk = k.shape
    n = t // CHUNK

    def to_chunks(a):
        a = a.astype(jnp.float32).reshape(bsz, n, CHUNK, nh, *a.shape[3:])
        return jnp.moveaxis(a, 3, 1)

    k_c, v_c = to_chunks(k), to_chunks(v)
    gcum = jnp.cumsum(to_chunks(g), axis=-1)
    b_c = to_chunks(beta)[..., None]
    incl = jnp.tril(jnp.ones((CHUNK, CHUNK), dtype=bool))
    strict = jnp.tril(jnp.ones((CHUNK, CHUNK), dtype=bool), k=-1)
    decay = jnp.exp(jnp.where(incl, gcum[..., :, None] - gcum[..., None, :], -jnp.inf))
    kb = k_c * b_c
    lower = jnp.where(strict, jnp.einsum('bhnid,bhnjd->bhnij', kb, k_c) * decay, 0.0)
    eye = jnp.eye(CHUNK, dtype=jnp.float32)
    t_inv = lax.linalg.triangular_solve(lower + eye, jnp.broadcast_to(eye, lower.shape),
                                        left_side=True, lower=True, unit_diagonal=True)
    u_c = jnp.einsum('bhnij,bhnjv->bhniv', t_inv, v_c * b_c)
    w_c = jnp.einsum('bhnij,bhnjk->bhnik', t_inv, kb * jnp.exp(gcum)[..., None])
    g_last = gcum[..., -1]
    k_dec = k_c * jnp.exp(g_last[..., None] - gcum)[..., None]

    def seq_first(a):
        return jnp.moveaxis(a, 2, 0)

    xs = [seq_first(a) for a in (u_c, w_c, k_dec, g_last)]
    with_out = q is not None
    if with_out:
        q_c = to_chunks(q) * dk ** -0.5
        attn = jnp.where(incl, jnp.einsum('bhnik,bhnjk->bhnij', q_c, k_c) * decay, 0.0)
        xs += [seq_first(q_c * jnp.exp(gcum)[..., None]), seq_first(attn)]

    def step(s, xs_n):
        u_n, w_n, kd_n, gl_n = xs_n[:4]
        v_new = u_n - jnp.einsum('bhck,bhkv->bhcv', w_n, s)
        s_new = s * jnp.exp(gl_n)[..., None, None] + jnp.einsum('bhck,bhcv->bhkv', kd_n, v_new)
        if not with_out:
            return s_new, None
        qd_n, a_n = xs_n[4:]
        o_n = (jnp.einsum('bhck,bhkv->bhcv', qd_n, s)
               + jnp.einsum('bhij,bhjv->bhiv', a_n, v_new))
        return s_new, o_n

    s_fin, o = lax.scan(step, s0, tuple(xs))
    if not with_out:
        return None, s_fin
    o = jnp.moveaxis(jnp.moveaxis(o, 0, 2), 1, 3).reshape(bsz, t, nh, -1)
    return o, s_fin

def dn_gates(p_gate, a_log, dt_bias):
    pf = p_gate.astype(jnp.float32)
    b_f, b_b, a_f, a_b = jnp.split(pf, 4, axis=-1)

    def log_decay(a, d):
        return -jnp.exp(a_log[d].astype(jnp.float32)) * jax.nn.softplus(a + dt_bias[d].astype(jnp.float32))

    return (log_decay(a_f, 0), jax.nn.sigmoid(b_f)), (log_decay(a_b, 1), jax.nn.sigmoid(b_b))

def bidirectional_delta(q, k, v, gates, s0_f, s0_b):
    (g_f, beta_f), (g_b, beta_b) = gates

    def flip(a):
        return None if a is None else jnp.flip(a, axis=1)

    o_f, s_f = gated_delta_rule(q, k, v, g_f, beta_f, s0_f)
    o_b, s_b = gated_delta_rule(flip(q), flip(k), flip(v), flip(g_b), flip(beta_b), s0_b)
    o = None if q is None else o_f + flip(o_b)
    return o, s_f, s_b

def box_mean(u, w, axis):
    n = u.shape[axis]
    left = w // 2
    right = w - 1 - left
    cs = jnp.cumsum(u, axis=axis)
    cs = jnp.concatenate([jnp.zeros_like(lax.slice_in_dim(cs, 0, 1, axis=axis)), cs], axis=axis)
    idx = jnp.arange(n)
    lo = jnp.clip(idx - left, 0, n)
    hi = jnp.clip(idx + right + 1, 0, n)
    total = jnp.take(cs, hi, axis=axis) - jnp.take(cs, lo, axis=axis)
    shape = [1] * u.ndim
    shape[axis] = n
    return total / (hi - lo).astype(u.dtype).reshape(shape)

def pool_mixer(u, pool_w, pool_scale, rows):
    bsz, t, _ = u.shape
    if rows is None:
        spatial, axes = (t,), (1,)
    else:
        spatial, axes = (rows, GRID_W), (1, 2)
    uf = u.astype(jnp.float32).reshape(bsz, *spatial, POOL_GROUPS, POOL_GROUP_DIM)
    diffs = []
    for gi, w in enumerate(POOL_WINDOWS):
        ug = uf[..., gi, :]
        m = ug
        for ax in axes:
            m = box_mean(m, w, ax)
        diffs.append(m - ug)
    d = jnp.stack(diffs, axis=-2).reshape(bsz, t, POOL_GROUPS, POOL_GROUP_DIM).astype(u.dtype)
    y = jnp.einsum('btgc,gcd->btgd', d, pool_w).reshape(bsz, t, POOL_WIDTH)
    return y * pool_scale

def token_mixers(h, rows, s0_f, s0_b, w_in, conv_qkv, a_log, dt_bias, o_norm, pool_w, pool_scale, w_out):
    p = h @ w_in
    qkv = jax.nn.silu(depthwise_conv(p[..., Q_OFF:Z_OFF], conv_qkv))
    q, k, v = (split_heads(a) for a in jnp.split(qkv, 3, axis=-1))
    gates = dn_gates(p[..., GATE_OFF:POOL_OFF], a_log, dt_bias)
    o, s_f, s_b = bidirectional_delta(l2_normalize(q), l2_normalize(k), v, gates, s0_f, s0_b)
    z = split_heads(p[..., Z_OFF:GATE_OFF]).astype(jnp.float32)
    o = rms_norm_2(o, o_norm) * jax.nn.silu(z)
    dn_out = o.reshape(*h.shape[:-1], DN_WIDTH).astype(h.dtype)
    pool_out = pool_mixer(p[..., POOL_OFF:], pool_w, pool_scale, rows)
    y = jnp.concatenate([dn_out, pool_out], axis=-1) @ w_out
    return y, s_f, s_b

def context_states(hc, w_in, conv_qkv, a_log, dt_bias):
    kv = jax.nn.silu(depthwise_conv(hc @ w_in[:, K_OFF:Z_OFF], conv_qkv[:, K_OFF:Z_OFF]))
    k, v = (split_heads(a) for a in jnp.split(kv, 2, axis=-1))
    gates = dn_gates(hc @ w_in[:, GATE_OFF:POOL_OFF], a_log, dt_bias)
    zeros = jnp.zeros((hc.shape[0], DN_HEADS, DN_HEAD_DIM, DN_HEAD_DIM), jnp.float32)
    _, s_f, s_b = bidirectional_delta(None, l2_normalize(k), v, gates, zeros, zeros)
    return s_f, s_b

def conv_glu_ffn(h, w_up, conv_w, w_down):
    gate, up = jnp.split(h @ w_up, 2, axis=-1)
    return (jax.nn.silu(depthwise_conv(gate, conv_w)) * up) @ w_down

def layer(x, ctx, c, c_ctx, rows, update_ctx, w_mod, b_mod, g_pre_mix, g_post_mix, g_pre_ffn,
          g_post_ffn, w_in, conv_qkv, a_log, dt_bias, o_norm, pool_w, pool_scale, w_out,
          w_up, conv_ffn, w_down):
    sh1, sc1, gt1, sh2, sc2, gt2 = modulation(c, w_mod, b_mod)
    csh1, csc1, cgt1, csh2, csc2, cgt2 = modulation(c_ctx, w_mod, b_mod)
    mix_params = (w_in, conv_qkv, a_log, dt_bias, o_norm, pool_w, pool_scale, w_out)
    hx = rms_norm_2(x, g_pre_mix) * (1 + sc1) + sh1
    hc = rms_norm_2(ctx, g_pre_mix) * (1 + csc1) + csh1
    if update_ctx:
        zeros = jnp.zeros((ctx.shape[0], DN_HEADS, DN_HEAD_DIM, DN_HEAD_DIM), jnp.float32)
        yc, s_f, s_b = token_mixers(hc, None, zeros, zeros, *mix_params)
    else:
        s_f, s_b = context_states(hc, w_in, conv_qkv, a_log, dt_bias)
    yx, _, _ = token_mixers(hx, rows, s_f, s_b, *mix_params)
    x = x + gt1 * rms_norm_2(yx, g_post_mix)
    hx = rms_norm_2(x, g_pre_ffn) * (1 + sc2) + sh2
    x = x + gt2 * rms_norm_2(conv_glu_ffn(hx, w_up, conv_ffn, w_down), g_post_ffn)
    if update_ctx:
        ctx = ctx + cgt1 * rms_norm_2(yc, g_post_mix)
        hc = rms_norm_2(ctx, g_pre_ffn) * (1 + csc2) + csh2
        ctx = ctx + cgt2 * rms_norm_2(conv_glu_ffn(hc, w_up, conv_ffn, w_down), g_post_ffn)
    return x, ctx

def second_inputs(seed: int = 0) -> dict:
    key = jax.random.key(seed)
    ks = jax.random.split(key, 21)
    f32 = jnp.float32

    def nrm(k, shape, scale):
        return jax.random.normal(k, shape, f32) * scale

    dt = jnp.exp(jax.random.uniform(ks[13], (DEPTH, 2, DN_HEADS), f32,
                                    minval=math.log(1e-3), maxval=math.log(1e-1)))
    return {
        'x': nrm(ks[0], (BATCH, SEQ, D_MODEL), 1.0),
        'c': nrm(ks[1], (BATCH, D_MODEL), 1.0),
        'ctx': nrm(ks[2], (BATCH, CTX_LEN, D_MODEL), 1.0),
        'c_ctx': nrm(ks[3], (D_MODEL,), 1.0),
        'w_mod': nrm(ks[4], (DEPTH, D_MODEL, N_MOD * D_MODEL), 0.5 * D_MODEL ** -0.5),
        'b_mod': nrm(ks[5], (DEPTH, N_MOD * D_MODEL), 0.02),
        'g_pre_mix': 1.0 + nrm(ks[6], (DEPTH, D_MODEL), 0.05),
        'g_post_mix': 1.0 + nrm(ks[7], (DEPTH, D_MODEL), 0.05),
        'g_pre_ffn': 1.0 + nrm(ks[8], (DEPTH, D_MODEL), 0.05),
        'g_post_ffn': 1.0 + nrm(ks[9], (DEPTH, D_MODEL), 0.05),
        'w_in': nrm(ks[10], (DEPTH, D_MODEL, IN_COLS), D_MODEL ** -0.5),
        'conv_qkv': nrm(ks[11], (DEPTH, SHORT_CONV, 3 * DN_WIDTH), SHORT_CONV ** -0.5),
        'a_log': jnp.log(jax.random.uniform(ks[12], (DEPTH, 2, DN_HEADS), f32, minval=1.0, maxval=16.0)),
        'dt_bias': jnp.log(jnp.expm1(dt)),
        'o_norm': 1.0 + nrm(ks[14], (DEPTH, DN_HEAD_DIM), 0.05),
        'pool_w': nrm(ks[15], (DEPTH, POOL_GROUPS, POOL_GROUP_DIM, POOL_GROUP_DIM), POOL_GROUP_DIM ** -0.5),
        'pool_scale': 1.0 + nrm(ks[16], (DEPTH, POOL_WIDTH), 0.05),
        'w_out': nrm(ks[17], (DEPTH, MIX_WIDTH, D_MODEL), MIX_WIDTH ** -0.5),
        'w_up': nrm(ks[18], (DEPTH, D_MODEL, 2 * D_FF), D_MODEL ** -0.5),
        'conv_ffn': nrm(ks[19], (DEPTH, FFN_CONV, D_FF), FFN_CONV ** -0.5),
        'w_down': nrm(ks[20], (DEPTH, D_FF, D_MODEL), D_FF ** -0.5),
    }

def second_block(x, c, ctx, c_ctx, w_mod, b_mod, g_pre_mix, g_post_mix, g_pre_ffn, g_post_ffn,
              w_in, conv_qkv, a_log, dt_bias, o_norm, pool_w, pool_scale, w_out, w_up,
              conv_ffn, w_down):
    rows = x.shape[1] // GRID_W
    for i in range(DEPTH):
        x, ctx = layer(x, ctx, c, c_ctx, rows, i < DEPTH - 1,
                       w_mod[i], b_mod[i], g_pre_mix[i], g_post_mix[i], g_pre_ffn[i],
                       g_post_ffn[i], w_in[i], conv_qkv[i], a_log[i], dt_bias[i], o_norm[i],
                       pool_w[i], pool_scale[i], w_out[i], w_up[i], conv_ffn[i], w_down[i])
    return x


def setup_inputs(seed=0):
    out = dict(first_inputs(seed))
    for name, value in second_inputs(seed + 1).items():
        if name != "x":
            out[name + "_2"] = value
    return out


def reference(
    x, rel_bias_table, g_pre_mix, w_in, b_glu, w_dw, b_dw, g_conv_ln, b_conv_ln, w_conv_out,
    b_conv_out, w_attn_out, w_mix_out, g_post_mix, g_pre_ffn, w_ffn_in, w_ffn_out, g_post_ffn,
    c_2, ctx_2, c_ctx_2, w_mod_2, b_mod_2, g_pre_mix_2, g_post_mix_2, g_pre_ffn_2, g_post_ffn_2,
    w_in_2, conv_qkv_2, a_log_2, dt_bias_2, o_norm_2, pool_w_2, pool_scale_2, w_out_2, w_up_2,
    conv_ffn_2, w_down_2,
):
    x = first_block(
        x, rel_bias_table, g_pre_mix, w_in, b_glu, w_dw, b_dw, g_conv_ln, b_conv_ln, w_conv_out,
        b_conv_out, w_attn_out, w_mix_out, g_post_mix, g_pre_ffn, w_ffn_in, w_ffn_out,
        g_post_ffn,
    )
    return second_block(
        x, c_2, ctx_2, c_ctx_2, w_mod_2, b_mod_2, g_pre_mix_2, g_post_mix_2, g_pre_ffn_2,
        g_post_ffn_2, w_in_2, conv_qkv_2, a_log_2, dt_bias_2, o_norm_2, pool_w_2, pool_scale_2,
        w_out_2, w_up_2, conv_ffn_2, w_down_2,
    )


_drawn_inputs = setup_inputs


def setup_inputs(seed=0):
    import zlib

    import numpy as np

    out = dict(_drawn_inputs(seed))
    spreads = {}
    factors = {'b_glu': 2.982,
     'b_conv_ln': 3.563,
     'ctx_2': 8.0,
     'c_ctx_2': 8.0,
     'b_mod_2': 3.167,
     'g_pre_mix_2': 5.62,
     'g_post_mix_2': 6.984,
     'g_pre_ffn_2': 4.368,
     'g_post_ffn_2': 6.555,
     'a_log_2': 5.176,
     'o_norm_2': 8.0,
     'pool_scale_2': 7.162}
    for name, (base, spread) in spreads.items():
        noise = np.random.default_rng([zlib.crc32(name.encode()), seed]).standard_normal(out[name].shape)
        drawn = base * np.exp(spread * noise) if base else spread * noise
        out[name] = jnp.asarray(drawn.astype(out[name].dtype))
    for name, factor in factors.items():
        out[name] = (out[name] * factor).astype(out[name].dtype)
    return out
```

```python
from contextlib import ExitStack

import numpy as np

import concourse.bass as bass
from concourse import mybir

F32 = mybir.dt.float32
F32R = mybir.dt.float32r
ALU = mybir.AluOpType
ACT = mybir.ActivationFunctionType
AX = mybir.AxisListType

P = 128
S = 1024
D = 1024
KD = D // P
HALF = 512
NT = S // P
HD = 64
NH = 8
DILATION = (1, 4, 16)
CLASSES = (1, 4, 8)
NG = 3
ATTN_W = NG * NH * HD
FFN = 2816
KF = FFN // P
TAPS = 31
RMS_EPS = 1e-6
LN_EPS = 1e-5
BUCKETS, MAX_DISTANCE = 32, 2048
TOEP = 384
GLU0 = 3 * ATTN_W
GA0 = GLU0 + 2 * D
GC0 = GA0 + D

CTX = 256
CT = CTX // P
DH = 4
DW = 512
CHUNK = 64
CONV5 = 5
GRID_W = 64
GRID_H = S // GRID_W
WINDOWS = (2, 4, 8, 16)
GATE0 = 4 * DW
POOL0 = GATE0 + 4 * DH
LEVELS = 6



def rel_buckets(distance):
    exact = BUCKETS // 2
    d = np.maximum(distance, 0)
    df = np.maximum(d, 1).astype(np.float32)
    large = exact + (np.log(df / np.float32(exact)) / np.float32(np.log(MAX_DISTANCE / exact))
                     * (BUCKETS - exact)).astype(np.int32)
    return np.where(d < exact, d, np.minimum(large, BUCKETS - 1))


def constants():
    offset = 255 - np.arange(TOEP)
    onehot = np.zeros((BUCKETS, NG, TOEP), np.float32)
    invalid = np.zeros((NG, TOEP), np.float32)
    for g, (dil, classes) in enumerate(zip(DILATION, CLASSES)):
        step = dil // classes
        valid = (offset >= 0) & (offset <= 128 * step) & (offset % step == 0)
        b = rel_buckets(offset * classes)
        onehot[b[valid], g, np.flatnonzero(valid)] = 1.0
        invalid[g] = np.where(valid, 0.0, -1e30)
    i = np.arange(P)
    same = (i[:, None] // CHUNK) == (i[None, :] // CHUNK)
    upper_in = same & (i[:, None] <= i[None, :])
    lower_in = same & (i[:, None] >= i[None, :])
    upper_ex = same & (i[:, None] < i[None, :])
    lower_ex = same & (i[:, None] > i[None, :])
    tri = np.stack([upper_in, lower_in, upper_ex, lower_ex, same], 1).astype(np.float32)
    levels = np.zeros((P, 2, LEVELS, P), np.float32)
    for lv in range(LEVELS):
        b = 1 << lv
        pair = (i[:, None] // (2 * b)) == (i[None, :] // (2 * b))
        levels[:, 0, lv] = pair & ((i[:, None] // b) > (i[None, :] // b))
        levels[:, 1, lv] = pair & ((i[:, None] // b) < (i[None, :] // b))
    inv = np.zeros((len(WINDOWS), S), np.float32)
    for w, win in enumerate(WINDOWS):
        left, right = win // 2, win - 1 - win // 2

        def count(n):
            j = np.arange(n)
            return (np.clip(j + right + 1, 0, n) - np.clip(j - left, 0, n)).astype(np.float32)
        inv[w] = (1.0 / (count(GRID_H)[:, None] * count(GRID_W)[None, :])).reshape(-1)
    return {
        "k_onehot": onehot.reshape(BUCKETS, NG * TOEP),
        "k_invalid": invalid,
        "k_ident": np.eye(P, dtype=np.float32),
        "k_tri": tri.reshape(P, 5 * P),
        "k_levels": levels.reshape(P, 2 * LEVELS * P),
        "k_pool": inv,
    }



class Lane:

    def __init__(self, sem):
        self.sem, self.count, self.ops, self.waited = sem, 0, [], {}

    def put(self, fn, after=(), mark=True):
        waits = []
        for token in flat(after):
            if self.waited.get(token[0], 0) < token[1]:
                self.waited[token[0]] = token[1]
                waits.append(token)
        waits = [w for n, w in enumerate(waits) if all(v[0] != w[0] for v in waits[n + 1:])]
        if mark:
            self.count += 1
        self.ops.append((waits, fn, (self.sem, 1) if mark else None))
        return (self.sem, self.count)

    def put_dma(self, fn, counter, after=()):
        counter.count += 16
        self.put(fn, after, mark=False)
        waits, fn, _ = self.ops.pop()
        self.ops.append((waits, fn, (counter.sem, 16)))
        return (counter.sem, counter.count)

    def last(self):
        return (self.sem, self.count)

    def play(self, eng):
        for waits, fn, inc in self.ops:
            for sem, value in waits:
                eng.wait_ge(sem, value)
            ins = fn(eng)
            if inc:
                ins.then_inc(*inc)


class Counter:
    def __init__(self, sem):
        self.sem, self.count = sem, 0

    def last(self):
        return (self.sem, self.count)


def flat(tokens):
    if tokens is None:
        return []
    if isinstance(tokens, tuple) and len(tokens) == 2 and isinstance(tokens[1], int):
        return [tokens] if tokens[1] > 0 else []
    out = []
    for t in tokens:
        out += flat(t)
    return out


class Ring:

    def __init__(self, slots, free=()):
        self.slots, self.at = slots, -1
        self.free = [list(flat(free)) for _ in slots]

    def next(self):
        self.at = (self.at + 1) % len(self.slots)
        return self.at, self.slots[self.at], self.free[self.at]


class Banks:

    def __init__(self, banks):
        self.banks, self.free, self.held, self.at = banks, [[] for _ in banks], [False] * len(banks), -1

    def take(self):
        for _ in self.banks:
            self.at = (self.at + 1) % len(self.banks)
            if not self.held[self.at]:
                self.held[self.at] = True
                return self.at
        raise ValueError("all banks are held")

    def release(self, b, tokens):
        self.held[b] = False
        self.free[b] = flat(tokens)


class Program:
    def __init__(self, nc, ctx, arg, scratch, out):
        self.nc, self.arg, self.scratch, self.out = nc, arg, scratch, out

        def sem(name):
            return ctx.enter_context(nc.semaphore(name))
        self.pe, self.act, self.dve = Lane(sem("s_pe")), Lane(sem("s_act")), Lane(sem("s_dve"))
        self.pool, self.sp = Lane(sem("s_pool")), Lane(sem("s_sp"))
        self.raw_counters = [Counter(sem(f"s_weights{i}")) for i in range(3)]
        self.queues = {lane: [0, [Counter(sem(f"s_{name}{i}")) for i in range(12)]]
                       for name, lane in (("dma_sp", self.sp), ("dma_pool", self.pool))}
        self.misc = [c for _, counters in self.queues.values() for c in counters]
        banks = [ctx.enter_context(nc.psum_tensor(f"bank{i}", [P, HALF], F32)) for i in range(8)]
        self.banks = Banks(banks)
        self.streams, self.turn_of = [], 0
        self.base = (nc.sbuf_base + 63) // 64 * 64
        self.limit = nc.sbuf_usable_end
        self.cursor = self.base
        self.phase = 0


    def place(self, name, shape, dtype=F32):
        size = int(np.prod(shape[1:])) * 4
        t = self.nc.alloc_sbuf_tensor_at(f"{name}_{self.phase}", shape, dtype, offset=self.cursor)
        self.cursor += (size + 31) // 32 * 32
        assert self.cursor <= self.limit, (name, self.cursor, self.limit)
        return t

    def begin_phase(self, floor):
        self.phase += 1
        self.cursor = floor
        return [x.last() for x in (self.pe, self.act, self.dve, self.pool, *self.misc)]


    def load(self, dst, src, after=(), lane=None):
        lane = lane or self.pool
        at, counters = self.queues[lane]
        c = counters[at]
        self.queues[lane][0] = (at + 1) % len(counters)
        return lane.put_dma(lambda e: e.dma_start(dst, src), c, after)

    store = load


    def weights_begin(self, plan):
        self.plan = plan
        self.raw_ring = Ring([self.place(f"raw{i}", [P, 1024]) for i in range(3)])
        self.split_ring = Ring([(self.place(f"whi{i}", [P, 1024], F32R), self.place(f"wlo{i}", [P, 1024], F32R))
                                for i in range(5)])
        self.ready, self.fetched, self.taken = [], 0, 0

    def fetch(self):
        name, src, k, n, split = self.plan[self.fetched]
        i, raw, free = self.raw_ring.next()
        view = raw[:, :k * n].rearrange("p (k n) -> p k n", k=k)
        landed = self.sp.put_dma(lambda e: e.dma_start(view, src), self.raw_counters[i], free)
        if not split:
            self.raw_ring.free[i] = None
            self.ready.append((name, view, None, landed, i))
        else:
            j, (hi, lo), sfree = self.split_ring.next()
            assert sfree is not None, name
            h, l = hi[:, :k * n], lo[:, :k * n]
            high = self.act.put(lambda e: e.activation(h, raw[:, :k * n], ACT.Copy), [landed, sfree])
            low = self.dve.put(lambda e: e.tensor_tensor(l, raw[:, :k * n], h.bitcast(F32), ALU.subtract),
                               [high, sfree])
            self.raw_ring.free[i] = [low]
            self.split_ring.free[j] = None
            self.ready.append((name, h.rearrange("p (k n) -> p k n", k=k),
                               l.rearrange("p (k n) -> p k n", k=k), [high, low], j))
        self.fetched += 1

    def weights_take(self, name):
        while self.fetched <= self.taken:
            self.fetch()
        self.prefetch()
        block = self.ready[self.taken]
        assert block[0] == name, (block[0], name)
        self.taken += 1
        return block

    def prefetch(self):
        while self.fetched < min(self.taken + 4, len(self.plan)):
            ring = self.raw_ring if not self.plan[self.fetched][4] else self.split_ring
            raw_next = self.raw_ring.free[(self.raw_ring.at + 1) % 3]
            if raw_next is None or ring.free[(ring.at + 1) % len(ring.slots)] is None:
                return
            self.fetch()

    def weights_done(self, block, token):
        ring = self.raw_ring if block[2] is None else self.split_ring
        ring.free[block[4]] = [token]


    def pump(self, n=1):
        for _ in range(n):
            busy = [x for x in self.streams if x]
            if not busy:
                return
            self.turn_of += 1
            work = busy[self.turn_of % len(busy)]
            if next(work[0], True):
                work.pop(0)

    def finish_background(self):
        while any(self.streams):
            self.pump()

    def next_slot(self, ring):
        while ring.free[(ring.at + 1) % len(ring.slots)] is None:
            self.pump()
        return ring.next()


    def product(self, out, terms, after=()):
        for n, (lhsT, rhs) in enumerate(terms):
            first, last = n == 0, n == len(terms) - 1
            token = self.pe.put(lambda e, a=lhsT, b=rhs, s=first, t=last: e.matmul(out, a, b, start=s, stop=t),
                                after if first else (), mark=last)
        return token

    def into_bank(self, shape, terms, after=()):
        b = self.banks.take()
        view = bank_view(self.banks.banks[b], shape)
        return b, view, self.product(view, terms, [self.banks.free[b], after])

    def split(self, src, hi, lo, after, free=()):
        high = self.act.put(lambda e: e.activation(hi, src, ACT.Copy), [after, free])
        low = self.dve.put(lambda e: e.tensor_tensor(lo, src, hi.bitcast(F32), ALU.subtract), [high, free])
        return [high, low]

    def transposes(self, pieces, after):
        b = self.banks.take()
        bank = self.banks.banks[b]
        for n, piece in enumerate(pieces):
            rows = piece.shape[0]
            width = int(np.prod(piece.shape[1:]))
            token = self.pe.put(
                lambda e, n=n, piece=piece, rows=rows, width=width: e.transpose(
                    bank[:width, n * P:n * P + rows], piece, self.ident[:rows, :rows]),
                [self.banks.free[b], after] if n == 0 else (), mark=n == len(pieces) - 1)
        return b, bank, token


    def inverse_root(self, dst, src, scale, eps, after):
        a = self.dve.put(lambda e: e.tensor_scalar(dst, src, scale, eps, ALU.mult, ALU.add), after)
        b = self.act.put(lambda e: e.activation(dst, dst, ACT.Sqrt), [a])
        return self.dve.put(lambda e: e.reciprocal(dst, dst), [b])

    def norm_to_columns(self, source, n_tiles, hi, lo, gain, shift, work, free, row_ready):
        done = []
        for t in range(n_tiles):
            rows, src, col, loaded = source(t)
            i, x, xfree = work["x"].next()
            landed = self.load(x[:rows, :], src, [xfree, loaded], lane=self.sp)
            j, st, sfree = work["stat"].next()
            junk = work["junk"]
            sq = self.act.put(lambda e, x=x, st=st, rows=rows: e.activation(
                junk[:rows, :], x[:rows, :], ACT.Square, accum_out=st[:rows, 0:1]), [landed, sfree, self.junk_free])
            self.junk_free = [sq]
            inv = self.inverse_root(st[:rows, 1:2], st[:rows, 0:1], 1.0 / D, RMS_EPS, [sq])
            ready = self.dve.put(lambda e, x=x, st=st, rows=rows: e.scalar_tensor_tensor(
                x[:rows, :], x[:rows, :], st[:rows, 1:2], gain[:rows, :], ALU.mult, ALU.mult), [inv, row_ready])
            if shift is not None:
                ready = self.dve.put(lambda e, x=x, rows=rows: e.tensor_tensor(
                    x[:rows, :], x[:rows, :], shift[:rows, :], ALU.add), [ready])
            work["stat"].free[j] = [ready]
            for h in range(2):
                b, bank, turned = self.transposes([x[:rows, (4 * h + k) * P:(4 * h + k + 1) * P] for k in range(4)],
                                                  [ready])
                src4 = bank[:, :].rearrange("p (k t) -> p k t", k=4)[:, :, :rows]
                parts = self.split(src4, hi[:, 4 * h:4 * h + 4, col:col + rows],
                                   lo[:, 4 * h:4 * h + 4, col:col + rows], [turned], free)
                self.banks.release(b, parts)
                done += parts
            work["x"].free[i] = [turned]
        return done

    def norm_work(self, free):
        self.junk_free = list(flat(free))
        return {"x": Ring([self.place(f"x{i}", [P, D]) for i in range(2)], free),
                "stat": Ring([self.place(f"stat{i}", [P, 2]) for i in range(2)], free),
                "junk": self.place("junk", [P, D])}


    def project_rows(self, name, x, k_all, x_ready):
        out = {}
        for c in range(2):
            held = [self.banks.take() for _ in range(4)]
            for k0 in range(0, k_all, 2):
                block = self.weights_take(name)
                _, whi, wlo, wready, _ = block
                for t in range(4):
                    tok = slice(t * P, (t + 1) * P)
                    bank = self.banks.banks[held[t]]
                    terms = []
                    for k in range(2):
                        terms += [(x[0][:, k0 + k, tok], whi[:, k, :]), (x[1][:, k0 + k, tok], whi[:, k, :]),
                                  (x[0][:, k0 + k, tok], wlo[:, k, :])]
                    for n, (a, w) in enumerate(terms):
                        first, last = k0 == 0 and n == 0, k0 == k_all - 2 and n == len(terms) - 1
                        token = self.pe.put(
                            lambda e, a=a, w=w, f=first, g=last, bank=bank: e.matmul(
                                bank[:, :], a, w, start=f, stop=g),
                            [wready, x_ready, self.banks.free[held[t]] if k0 == 0 else ()] if n == 0 else (),
                            mark=n == len(terms) - 1)
                    if k0 == k_all - 2:
                        out[(t, c)] = (held[t], token)
                self.weights_done(block, token)
                self.prefetch()
                self.pump()
        return out

    def add_residual(self, banks, source, target, gain, work, free, row_ready):
        stored = []
        for t in range(4):
            (b0, y0), (b1, y1) = banks[(t, 0)], banks[(t, 1)]
            bank0, bank1 = self.banks.banks[b0], self.banks.banks[b1]
            src, loaded = source(t)
            i, x, xfree = work["x"].next()
            landed = self.load(x[:, :], src, [xfree, loaded], lane=self.sp)
            j, st, sfree = work["stat"].next()
            junk, y = work["junk"], work["y"]
            s0 = self.act.put(lambda e, b=bank0, st=st: e.activation(junk[:, :HALF], b[:, :], ACT.Square,
                                                                     accum_out=st[:, 0:1]),
                              [y0, sfree, self.junk_free])
            s1 = self.act.put(lambda e, b=bank1, st=st: e.activation(junk[:, HALF:], b[:, :], ACT.Square,
                                                                     accum_out=st[:, 1:2]), [y1, self.junk_free])
            self.junk_free = [s1]
            both = self.dve.put(lambda e, st=st: e.tensor_tensor(st[:, 0:1], st[:, 0:1], st[:, 1:2], ALU.add), [s0, s1])
            inv = self.inverse_root(st[:, 2:3], st[:, 0:1], 1.0 / D, RMS_EPS, [both])
            for c, (b, bank) in enumerate(((b0, bank0), (b1, bank1))):
                cols = slice(c * HALF, (c + 1) * HALF)
                scaled = self.dve.put(lambda e, bank=bank, st=st, cols=cols: e.scalar_tensor_tensor(
                    y[:, cols], bank[:, :], st[:, 2:3], gain[:, cols], ALU.mult, ALU.mult), [inv, row_ready, free])
                self.banks.release(b, [scaled])
                added = self.dve.put(lambda e, x=x, cols=cols: e.tensor_tensor(
                    x[:, cols], x[:, cols], y[:, cols], ALU.add), [scaled, landed])
            work["stat"].free[j] = [added]
            out = self.store(target(t), x[:, :], [added])
            work["x"].free[i] = [out]
            stored.append(out)
        return stored

    def residual_work(self, free):
        self.junk_free = list(flat(free))
        return {"x": Ring([self.place(f"rx{i}", [P, D]) for i in range(2)], free),
                "stat": Ring([self.place(f"rstat{i}", [P, 3]) for i in range(2)], free),
                "junk": self.place("rjunk", [P, D]), "y": self.place("ry", [P, D])}


    def setup(self):
        a, nc = self.arg, self.nc
        self.ident = self.place("ident", [P, P])
        self.mean = self.place("mean", [P, P])
        ident_ready = self.load(self.ident[:, :], a["k_ident"])
        self.mean_ready = self.pool.put(lambda e: e.memset(self.mean[:, :], 1.0 / D))
        sources = [[a["b_glu"], a["b_dw"], a["g_conv_ln"], a["b_conv_ln"], a["b_conv_out"],
                    a["pool_scale_2"], a["c_2"], a["b_mod_2"]],
                   [a["w_dw"][0, 0:15, :]], [a["w_dw"][0, 15:31, :]], [a["conv_qkv_2"][0]]]
        self.vec = self.place("vec", [P, 4, P])
        self.vec_at = {}
        rows = self.place("vec_rows", [P, 4, P])
        floor = self.cursor
        counts = []
        for n, group in enumerate(sources):
            r = 0
            landed = []
            for src in group:
                flat_src = src.rearrange("a (j p) -> (a j) p", p=P)
                m = flat_src.shape[0]
                landed.append(self.load(rows[r:r + m, n, :], flat_src))
                counts.append((n, r, m))
                r += m
            if n == 0:
                c_ctx = a["c_ctx_2"].rearrange("(j p) -> j p", p=P)
                landed.append(self.load(rows[r:r + 8, n, :], c_ctx))
                counts.append((n, r, 8))
                r += 8
            b, bank, turned = self.transposes([rows[:r, n, :]], [landed, ident_ready])
            copied = self.dve.put(lambda e, bank=bank, n=n, r=r: e.tensor_copy(self.vec[:, n, :r], bank[:, :r]), [turned])
            self.banks.release(b, [copied])
            self.vec_ready = [copied]
        self.v_b_glu, self.v_b_dw, self.v_g_ln, self.v_b_ln, self.v_b_co, self.v_pool, self.v_c, self.v_b_mod, \
            self.v_c_ctx = (self.vec[:, 0, r:r + m] for _, r, m in counts[:9])
        return ident_ready

    def dw_tap(self, chunk, tap):
        n, t = (1, tap) if tap < 15 else (2, tap - 15)
        return self.vec[:, n, t * KD + chunk:t * KD + chunk + 1]

    def row_load(self, name, src, after):
        row = self.place(name, [P, src.shape[-1]])
        return row, self.load(row[:, :], broadcast(src, src.shape[-1]), after, lane=self.sp)


    def first_mix_projections(self, free):
        a, s = self.arg, self.scratch
        hi, lo = self.place("h_hi", [P, KD, S], F32R), self.place("h_lo", [P, KD, S], F32R)
        floor = self.cursor
        gain, gain_ready = self.row_load("gain", a["g_pre_mix"], free)
        work = self.norm_work(free)
        h_ready = self.norm_to_columns(lambda t: (P, a["x"][0, t * P:(t + 1) * P, :], t * P, ()), NT, hi, lo,
                                       gain, None, work, free, gain_ready)
        norm_done = [x.last() for x in (self.pe, self.act, self.dve)]
        self.phase += 1
        self.cursor = floor
        free = norm_done
        self.attention_setup(free)
        self.conv_setup(free)
        stage = Ring([self.place(f"stage{i}", [P, HALF]) for i in range(3)], free)
        v_sb = self.place("v", [P, NT, NH, HD + 1])
        ones = self.pool.put(lambda e: e.memset(v_sb[:, :, :, HD:HD + 1], 1.0), free)
        qk = Ring([(self.place(f"q{i}", [P, S]), self.place(f"k{i}", [P, S])) for i in range(2)], free)
        self.v_free = list(free)
        attention, convolution = [], []
        self.streams = [attention, convolution]
        self.gates_stored, self.conv_stored, self.u_stored = [], [], []
        h = (hi, lo)

        def glu(j):
            i, (up, acc), cfree = self.next_slot(self.conv_ring)
            gate = self.weights_take("glu_gate")
            main = self.weights_take("glu_u")
            landed = []
            for n in range(2):
                sl = slice(n * HALF, (n + 1) * HALF)
                b, y, done = self.into_bank([P, HALF], self.column_terms(gate, h, KD, sl), [gate[3], h_ready])
                k, sg, sfree = self.sig_ring.next()
                sig = self.act.put(lambda e, y=y, sg=sg: e.activation(
                    sg[:, :], y, ACT.Sigmoid, bias=self.v_b_glu[:, KD + j:KD + j + 1]), [done, sfree, self.vec_ready])
                self.banks.release(b, [sig])
                if n:
                    self.weights_done(gate, done)
                b, y, done = self.into_bank([P, HALF], self.column_terms(main, h, KD, sl), [main[3]])
                put = self.dve.put(lambda e, y=y, sg=sg, n=n, up=up: e.scalar_tensor_tensor(
                    up[:, TAPS - 1 + n * HALF:TAPS - 1 + (n + 1) * HALF], y, self.v_b_glu[:, j:j + 1], sg[:, :],
                    ALU.add, ALU.mult), [done, sig, cfree])
                self.banks.release(b, [put])
                self.sig_ring.free[k] = [put]
                landed.append(put)
                if n:
                    self.weights_done(main, done)
                self.prefetch()
                self.pump(2)
            self.conv_ring.free[i] = None
            convolution.append(self.convolve(j, i, up, acc, landed))

        def gates(name, slot, j):
            block = self.weights_take(name)
            for n in range(2):
                b, y, done = self.into_bank([P, HALF], self.column_terms(block, h, KD, slice(n * HALF, (n + 1) * HALF)),
                                            [block[3], h_ready])
                i, st, sfree = stage.next()
                sig = self.act.put(lambda e, y=y, st=st: e.activation(st[:, :], y, ACT.Sigmoid), [done, sfree])
                self.banks.release(b, [sig])
                out = self.store(s["gates"][slot, j, :, n * HALF:(n + 1) * HALF], st[:, :], [sig])
                stage.free[i] = [out]
                self.gates_stored.append(out)
                if n:
                    self.weights_done(block, done)
                self.prefetch()
                self.pump(2)

        glu(0)
        glu(1)
        for g in range(NG):
            blocks = [self.weights_take("v") for _ in range(4)]
            landed = []
            for t in range(NT):
                terms = []
                for k in range(KD):
                    _, whi, wlo, _, _ = blocks[k // 2]
                    xs = [group_tokens(x, k, g, t) for x in (hi, lo)]
                    terms += [(xs[0], whi[:, k % 2, :]), (xs[1], whi[:, k % 2, :]), (xs[0], wlo[:, k % 2, :])]
                b, y, done = self.into_bank([P, HALF], terms, [[x[3] for x in blocks], h_ready])
                eng = self.act if t % 2 else self.dve
                dst = v_sb[:, t, :, 0:HD]
                src = y.rearrange("p (h d) -> p h d", h=NH)
                if t % 2:
                    put = self.act.put(lambda e, dst=dst, src=src: e.activation(dst, src, ACT.Copy), [done, self.v_free])
                else:
                    put = self.dve.put(lambda e, dst=dst, src=src: e.tensor_copy(dst, src), [done, self.v_free])
                self.banks.release(b, [put])
                landed.append(put)
                if t >= NT - 1:
                    for x in blocks:
                        self.weights_done(x, done)
                self.pump()
            self.prefetch()
            v_ready = [landed, ones]
            for pair in range(NH // 2):
                i, (q, k), qfree = self.next_slot(qk)
                ready = []
                for name, dst, scale in (("q", q, HD ** -0.5), ("k", k, 1.0)):
                    block = self.weights_take(name)
                    for n in range(2):
                        b, y, done = self.into_bank([P, HALF],
                                                    self.column_terms(block, h, KD, slice(n * HALF, (n + 1) * HALF)),
                                                    [block[3], h_ready])
                        dv, sv = class_order(dst, y, g, n)
                        put = self.act.put(lambda e, dv=dv, sv=sv, scale=scale: e.activation(
                            dv, sv, ACT.Copy, scale=scale), [done, qfree])
                        self.banks.release(b, [put])
                        ready.append(put)
                        if n:
                            self.weights_done(block, done)
                        self.prefetch()
                        self.pump(2)
                qk.free[i] = None
                attention.append(self.attend(g, pair, q, k, v_sb, [ready, v_ready], (qk, i)))
                if pair % 2:
                    glu(2 + 2 * g + pair // 2)
            while attention:
                self.pump()
            self.v_free = [self.pe.last()]
        for j in range(KD):
            gates("gate_attn", 0, j)
            gates("gate_conv", 1, j)
        self.finish_background()

    def column_terms(self, block, x, k_all, sl):
        _, whi, wlo, _, _ = block
        terms = []
        for k in range(k_all):
            terms += [(whi[:, k, :], x[0][:, k, sl]), (whi[:, k, :], x[1][:, k, sl]), (wlo[:, k, :], x[0][:, k, sl])]
        return terms


    def conv_setup(self, free):
        self.conv_ring = Ring([(self.place(f"u{i}", [P, TAPS - 1 + S]), self.place(f"conv{i}", [P, S]))
                               for i in range(2)], free)
        self.sig_ring = Ring([self.place(f"sig{i}", [P, HALF]) for i in range(2)], free)
        for i, (up, _) in enumerate(self.conv_ring.slots):
            zero = self.dve.put(lambda e, up=up: e.memset(up[:, 0:TAPS - 1], 0.0), free)
            self.conv_ring.free[i] = [zero]

    def convolve(self, j, i, up, acc, ready):
        token = self.dve.put(lambda e: e.tensor_scalar(acc[:, :], up[:, 0:S], self.dw_tap(j, 0),
                                                       self.v_b_dw[:, j:j + 1], ALU.mult, ALU.add), ready)
        for tap in range(1, TAPS):
            token = self.dve.put(lambda e, tap=tap: e.scalar_tensor_tensor(
                acc[:, :], up[:, tap:tap + S], self.dw_tap(j, tap), acc[:, :], ALU.mult, ALU.add), [token])
            if tap % 3 == 2:
                yield
        out = self.store(self.scratch["conv"][j], acc[:, :], [token])
        self.conv_ring.free[i] = [out, token]
        self.conv_stored.append(out)


    def attention_setup(self, free):
        a, s = self.arg, self.scratch
        table = self.place("table", [BUCKETS, NG * NH])
        self.bias = Ring([self.place(f"bias{i}", [P, 2, 2 * P]) for i in range(2)], free)
        self.scores = Ring([self.place(f"scores{i}", [P, 2, 2 * P]) for i in range(2)], free)
        self.turned = Ring([self.place(f"turned{i}", [P, 2, 2, P]) for i in range(2)], free)
        self.u_ring = Ring([self.place(f"uo{i}", [P, NT, 2, HD + 2]) for i in range(2)], free)
        self.stats = Ring([self.place(f"astat{i}", [P, 4]) for i in range(4)], free)
        onehot = self.bias.slots[0][0:BUCKETS, :, :].rearrange("p a b -> p (a b)")[:, 0:TOEP]
        vec = self.scores.slots[0][0:NG * NH, :, :].rearrange("p a b -> p (a b)")[:, 0:TOEP]
        invalid = self.scores.slots[1][0:NG * NH, :, :].rearrange("p a b -> p (a b)")[:, 0:TOEP]
        landed = self.load(table[:, :], a["rel_bias_table"], free)
        stored = []
        for g in range(NG):
            hot = self.load(onehot, a["k_onehot"][:, g * TOEP:(g + 1) * TOEP], [free, self.pe.last()])
            bad = self.load(invalid, bass.AP(tensor=a["k_invalid"].tensor, offset=g * TOEP,
                                             ap=[[0, NG * NH], [1, TOEP]]), [free, self.dve.last()])
            b, y, done = self.into_bank([NG * NH, TOEP], [(table[:, :], onehot)], [landed, hot])
            add = self.dve.put(lambda e, y=y: e.tensor_tensor(vec, y, invalid, ALU.add), [done, bad, stored])
            self.banks.release(b, [add])
            own = slice(g * NH, (g + 1) * NH)
            stored.append(self.store(s["toeplitz"][own, :].rearrange("h (r j) -> h r j", j=TOEP),
                                     vec[own, :].unsqueeze(1).to_broadcast([NH, P, TOEP]), [add]))
        self.toeplitz_stored = stored
        self.bias.free[0] = [done]
        self.scores.free = [[stored], [add]]

    def attend(self, g, pair, q, k, v_sb, ready, qk_slot):
        s = self.scratch
        ib, bias, bfree = self.bias.next()
        iu, u, ufree = self.u_ring.next()
        toep = s["toeplitz"]
        landed = []
        start, width = (127, 2 * P) if g < 2 else (127 + P, P)
        for h in range(2):
            base = toep[g * NH + 2 * pair + h:g * NH + 2 * pair + h + 1, 0:1]
            landed.append(self.load(bias[:, h, 0:width], shifted(base, start, P, width),
                                    [bfree, self.toeplitz_stored]))
        yield
        state = {}

        def score(t):
            nk = 2 if (g == 0 and t > 0) or (g == 1 and t % 2) else 1
            k0 = (t + 1 - nk) * P
            off = (2 - nk) * P if g < 2 else 0
            i, sc, sfree = self.scores.next()
            m, st, mfree = self.stats.next()
            for h in range(2):
                rows = slice(h * HD, (h + 1) * HD)
                b = self.banks.take()
                bank = self.banks.banks[b]
                token = self.pe.put(lambda e, rows=rows, bank=bank: e.matmul(
                    bank[:, 0:nk * P], q[rows, t * P:(t + 1) * P], k[rows, k0:k0 + nk * P],
                    start=True, stop=True), [self.banks.free[b], ready])
                token2 = self.dve.put(lambda e, h=h, bank=bank: e.tensor_tensor_reduce(
                    sc[:, h, 0:nk * P], bank[:, 0:nk * P], bias[:, h, off:off + nk * P],
                    1.0, -3e38, ALU.add, ALU.max, st[:, h:h + 1]), [token, sfree, mfree, landed])
                self.banks.release(b, [token2])
            neg = self.dve.put(lambda e: e.tensor_scalar(st[:, 2:4], st[:, 0:2], -1.0, None, ALU.mult), [token2])
            keep = self.dve.put(lambda e: e.tensor_copy(u[:, t, :, HD + 1:HD + 2].rearrange("p h a -> p (h a)"),
                                                        st[:, 0:2]), [token2, ufree])
            for h in range(2):
                exp = self.act.put(lambda e, h=h: e.activation(sc[:, h, 0:nk * P], sc[:, h, 0:nk * P], ACT.Exp,
                                                               bias=st[:, 2 + h:3 + h]), [neg])
            self.stats.free[m] = [exp, keep]
            state[t] = [nk, i, sc, exp, keep]

        def turn(t):
            nk, i, sc, exp, keep = state[t]
            b, bank, token = self.transposes([sc[:, h, n * P:(n + 1) * P] for h in range(2) for n in range(nk)], [exp])
            self.scores.free[i] = [token]
            j, pt, pfree = self.turned.next()
            src = bank[:, 0:2 * nk * P].rearrange("p (h n q) -> p h n q", h=2, n=nk)
            if t % 2:
                put = self.act.put(lambda e: e.activation(pt[:, :, 0:nk, :], src, ACT.Copy), [token, pfree])
            else:
                put = self.dve.put(lambda e: e.tensor_copy(pt[:, :, 0:nk, :], src), [token, pfree])
            self.banks.release(b, [put])
            state[t] += [j, pt, put]

        def weigh(t):
            nk, _, _, _, keep, j, pt, put = state[t]
            b = self.banks.take()
            bank = self.banks.banks[b]
            for h in range(2):
                for n in range(nk):
                    kt = t + 1 - nk + n
                    token = self.pe.put(lambda e, h=h, n=n, kt=kt: e.matmul(
                        bank[:, h * (HD + 1):(h + 1) * (HD + 1)], pt[:, h, n, :], v_sb[:, kt, 2 * pair + h, :],
                        start=n == 0, stop=n == nk - 1), [self.banks.free[b], put] if h + n == 0 else (),
                        mark=h == 1 and n == nk - 1)
            self.turned.free[j] = [token]
            out = self.dve.put(lambda e: e.tensor_copy(
                u[:, t, :, 0:HD + 1], bank[:, 0:2 * (HD + 1)].rearrange("p (h d) -> p h d", h=2)), [token, ufree])
            self.banks.release(b, [out])
            return [out, keep]

        done = []
        for t in range(NT + 2):
            if t < NT:
                score(t)
            if 1 <= t <= NT:
                turn(t - 1)
            if t >= 2:
                done += weigh(t - 2)
            yield
        ring, slot = qk_slot
        ring.free[slot] = [self.pe.last()]
        self.bias.free[ib] = [self.dve.last()]
        out = []
        for dst, src in unit_stores(s["sums"][g], u, g, pair):
            out.append(self.store(dst, src, done))
        self.u_ring.free[iu] = out
        self.u_stored += out




    def first_mix_outputs(self, free):
        a, s = self.arg, self.scratch
        sums = self.place("sums", [P, NG, NH, HD + 2])
        msum = self.place("msum", [P, 2, NG, NH])
        o = self.place("o", [P, HALF])
        oT = (self.place("oT_hi", [P, 4, HALF], F32R), self.place("oT_lo", [P, 4, HALF], F32R))
        conv = self.place("cv", [P, KD, HALF])
        u = (self.place("u_hi", [P, KD, HALF], F32R), self.place("u_lo", [P, KD, HALF], F32R))
        at = self.cursor
        merged = (self.place("m_hi", [P, KD, HALF], F32R), self.place("m_lo", [P, KD, HALF], F32R))
        end = self.cursor
        self.cursor = at
        square = self.place("square", [P, KD, HALF])
        self.cursor = end
        mu, rs = self.place("mu", [P, HALF]), self.place("rs", [P, HALF])
        gates = Ring([self.place(f"sg{i}", [P, 2, HALF]) for i in range(2)], free)
        silu = Ring([self.place(f"silu{i}", [P, HALF]) for i in range(2)], free)
        gain, gain_ready = self.row_load("post", a["g_post_mix"], free)
        end = self.cursor
        stored = []
        sums_free, o_free, x_free, m_free = list(free), list(free), list(free), list(free)
        for half in range(2):
            oT_ready = []
            for t in range(4):
                tok = slice(half * HALF + t * P, half * HALF + (t + 1) * P)
                landed = [self.load(sums[:, g, :, :], s["sums"][g, tok, :].rearrange("p (h w) -> p h w", h=NH),
                                    [sums_free, self.u_stored], lane=self.sp) for g in range(NG)]
                top, e = msum[:, 0, 0, :], msum[:, 1, :, :]
                mx = sums[:, :, :, HD + 1]
                x = self.dve.put(lambda v: v.tensor_tensor(top, mx[:, 0, :], mx[:, 1, :], ALU.max), [landed, sums_free])
                x = self.dve.put(lambda v: v.tensor_tensor(top, top, mx[:, 2, :], ALU.max), [x])
                for g in range(NG):
                    y = self.dve.put(lambda v, g=g: v.tensor_tensor(e[:, g, :], mx[:, g, :], top, ALU.subtract), [x])
                x = self.act.put(lambda v: v.activation(e, e, ACT.Exp), [y])
                total = msum[:, 0, :, :]
                x = self.dve.put(lambda v: v.tensor_tensor(total, e, sums[:, :, :, HD], ALU.mult), [x, y])
                x = self.dve.put(lambda v: v.tensor_tensor(total[:, 0, :], total[:, 0, :], total[:, 1, :], ALU.add), [x])
                x = self.dve.put(lambda v: v.tensor_tensor(total[:, 0, :], total[:, 0, :], total[:, 2, :], ALU.add), [x])
                x = self.dve.put(lambda v: v.reciprocal(total[:, 0, :], total[:, 0, :]), [x])
                for g in range(NG):
                    y = self.dve.put(lambda v, g=g: v.tensor_tensor(e[:, g, :], e[:, g, :], total[:, 0, :], ALU.mult), [x])
                for g in range(NG):
                    part = sums[:, g, :, 0:HD]
                    weight = e[:, g, :].unsqueeze(2).to_broadcast([P, NH, HD])
                    z = self.dve.put(lambda v, part=part, weight=weight: v.tensor_tensor(part, part, weight, ALU.mult), [y])
                o3 = o[:, :].rearrange("p (h d) -> p h d", h=NH)
                x = self.dve.put(lambda v: v.tensor_tensor(o3, sums[:, 0, :, 0:HD], sums[:, 1, :, 0:HD], ALU.add), [z, o_free])
                x = self.dve.put(lambda v: v.tensor_tensor(o3, o3, sums[:, 2, :, 0:HD], ALU.add), [x])
                sums_free = [x]
                b, bank, turned = self.transposes([o[:, k * P:(k + 1) * P] for k in range(4)], [x])
                o_free = [turned]
                dst = slice(t * P, (t + 1) * P)
                parts = self.split(bank[:, :].rearrange("p (k t) -> p k t", k=4), oT[0][:, :, dst], oT[1][:, :, dst],
                                   [turned], x_free)
                self.banks.release(b, parts)
                oT_ready += parts
            landed = self.load(conv[:, :, :], s["conv"].rearrange("j p t -> p j t")[:, :, half * HALF:(half + 1) * HALF],
                               [x_free, self.conv_stored], lane=self.sp)
            b, y, done = self.into_bank([P, HALF], [(self.mean[:, :], conv[:, k, :]) for k in range(KD)],
                                        [landed, self.mean_ready])
            x = self.act.put(lambda v, y=y: v.activation(mu[:, :], y, ACT.Copy), [done, x_free])
            self.banks.release(b, [x])
            centred = self.dve.put(lambda v: v.tensor_tensor(conv[:, :, :], conv[:, :, :],
                                                             mu[:, :].unsqueeze(1).to_broadcast([P, KD, HALF]),
                                                             ALU.subtract), [x])
            x = self.act.put(lambda v: v.activation(square[:, :, :], conv[:, :, :], ACT.Square), [centred, m_free])
            b, y, done = self.into_bank([P, HALF], [(self.mean[:, :], square[:, k, :]) for k in range(KD)], [x])
            square_read = done
            x = self.dve.put(lambda v, y=y: v.tensor_scalar(rs[:, :], y, LN_EPS, None, ALU.add), [done, x_free])
            self.banks.release(b, [x])
            x = self.act.put(lambda v: v.activation(rs[:, :], rs[:, :], ACT.Sqrt), [x])
            x = self.dve.put(lambda v: v.reciprocal(rs[:, :], rs[:, :]), [x])
            u_ready = []
            for k in range(KD):
                scaled = self.dve.put(lambda v, k=k: v.tensor_tensor(conv[:, k, :], conv[:, k, :], rs[:, :], ALU.mult), [x])
                i, f, ffree = silu.next()
                act = self.act.put(lambda v, k=k, f=f: v.activation(
                    f[:, :], conv[:, k, :], ACT.Silu, bias=self.v_b_ln[:, k:k + 1], scale=self.v_g_ln[:, k:k + 1]),
                    [scaled, ffree])
                parts = self.split(f[:, :], u[0][:, k, :], u[1][:, k, :], [act], x_free)
                silu.free[i] = parts
                u_ready += parts
            conv_read = act
            m_ready = []
            for j in range(KD):
                i, sg, gfree = gates.next()
                cols = slice(half * HALF, (half + 1) * HALF)
                landed = [self.load(sg[:, n, :], s["gates"][n, j, :, cols], [gfree, self.gates_stored], lane=self.sp)
                          for n in range(2)]
                block = self.weights_take("conv_out")
                b1, y1, done1 = self.into_bank([P, HALF], self.column_terms(block, u, KD, slice(0, HALF)),
                                               [block[3], u_ready])
                self.weights_done(block, done1)
                block = self.weights_take("attn_out")
                b2, y2, done2 = self.into_bank([P, HALF], self.column_terms(block, oT, 4, slice(0, HALF)),
                                               [block[3], oT_ready])
                self.weights_done(block, done2)
                x = self.dve.put(lambda v, y1=y1, sg=sg, j=j: v.scalar_tensor_tensor(
                    sg[:, 1, :], y1, self.v_b_co[:, j:j + 1], sg[:, 1, :], ALU.add, ALU.mult), [done1, landed])
                self.banks.release(b1, [x])
                z = self.dve.put(lambda v, y2=y2, sg=sg: v.tensor_tensor(sg[:, 0, :], y2, sg[:, 0, :], ALU.mult), [done2])
                self.banks.release(b2, [z])
                x = self.dve.put(lambda v, sg=sg: v.tensor_tensor(sg[:, 0, :], sg[:, 0, :], sg[:, 1, :], ALU.add), [x, z])
                parts = self.split(sg[:, 0, :], merged[0][:, j, :], merged[1][:, j, :], [x], [m_free, square_read])
                gates.free[i] = parts
                m_ready += parts
                self.prefetch()
            x_free = [done1, done2]
            banks = self.project_rows("mix_out", merged, KD, m_ready)
            m_free = [banks[(3, 1)][1]]
            self.cursor = at - 3 * KD * HALF * 4
            self.phase += 1
            work = self.residual_work([conv_read, x_free])
            self.cursor = end
            done = self.add_residual(
                banks, lambda t, half=half: (a["x"][0, half * HALF + t * P:half * HALF + (t + 1) * P, :], ()),
                lambda t, half=half: s["x1"][half * HALF + t * P:half * HALF + (t + 1) * P, :], gain, work, (), gain_ready)
            x_free = x_free + done + [self.dve.last(), self.act.last()]
            stored += done
        return stored


    def feed_forward(self, free, source, target, gain_src, post_src, conv_gate, names, shift_row=None):
        halo = 2 if conv_gate else 0
        hi, lo = self.place("f_hi", [P, KD, HALF + halo], F32R), self.place("f_lo", [P, KD, HALF + halo], F32R)
        post, post_ready = post_src(free)
        floor = self.cursor
        stored = []
        x_free = list(free)
        edge = self.place("edge", [P, KF]) if conv_gate else None
        gbuf = Ring([self.place(f"g{i}", [P, HALF + 2]) for i in range(2)], free)
        tmp = Ring([self.place(f"t{i}", [P, HALF]) for i in range(2)], free)
        at = self.cursor
        edge_ready = []
        for half in range(2):
            self.phase += 1
            self.cursor = at
            gain, shift, gain_ready = gain_src(x_free)
            work = self.norm_work(x_free)

            def tile(t, half=half):
                r = half * HALF + t * P
                rows = P if t < 4 else 2
                src, loaded = source(r, rows)
                return rows, src, t * P, loaded
            tiles = 5 if conv_gate and half == 0 else 4
            h_ready = self.norm_to_columns(tile, tiles, hi, lo, gain, shift, work, x_free, gain_ready)
            norm_done = [self.pe.last(), self.act.last(), self.dve.last()]
            self.phase += 1
            self.cursor = at
            a_hi, a_lo = self.place("a_hi", [P, KF, HALF], F32R), self.place("a_lo", [P, KF, HALF], F32R)
            a_ready = []
            for j in range(KF):
                gate = self.weights_take(names[0])
                b, y, done = self.into_bank([P, HALF], self.column_terms(gate, (hi, lo), KD, slice(0, HALF)),
                                            [gate[3], h_ready])
                i, g, gfree = gbuf.next()
                n, f, ffree = tmp.next()
                if conv_gate:
                    taps = conv_gate(j)
                    put = self.act.put(lambda e, y=y, g=g: e.activation(g[:, 1:HALF + 1], y, ACT.Copy), [done, gfree])
                    self.banks.release(b, [put])
                    if half == 0:
                        b, y, done = self.into_bank([P, 2], self.column_terms(gate, (hi, lo), KD, slice(HALF, HALF + 2)))
                        zero = self.dve.put(lambda e, g=g: e.memset(g[:, 0:1], 0.0), [gfree])
                        side = self.dve.put(lambda e, g=g, y=y: e.tensor_copy(g[:, HALF + 1:HALF + 2], y[:, 0:1]),
                                            [done, gfree])
                        self.banks.release(b, [side])
                        keep = self.dve.put(lambda e, g=g, j=j: e.tensor_copy(edge[:, j:j + 1], g[:, HALF:HALF + 1]),
                                            [put, free])
                        edge_ready.append(keep)
                        sides = [zero, side, keep]
                    else:
                        zero = self.dve.put(lambda e, g=g: e.memset(g[:, HALF + 1:HALF + 2], 0.0), [gfree])
                        side = self.dve.put(lambda e, g=g, j=j: e.tensor_copy(g[:, 0:1], edge[:, j:j + 1]), [gfree, edge_ready])
                        sides = [zero, side]
                    x = self.dve.put(lambda e, f=f, g=g, taps=taps: e.tensor_scalar(
                        f[:, :], g[:, 0:HALF], taps[0], None, ALU.mult), [put, sides, ffree, self.vec_ready])
                    for q in (1, 2):
                        x = self.dve.put(lambda e, f=f, g=g, q=q, taps=taps: e.scalar_tensor_tensor(
                            f[:, :], g[:, q:q + HALF], taps[q], f[:, :], ALU.mult, ALU.add), [x])
                    silu = self.act.put(lambda e, f=f, g=g: e.activation(g[:, 0:HALF], f[:, :], ACT.Silu), [x])
                else:
                    silu = self.act.put(lambda e, y=y, g=g: e.activation(g[:, 0:HALF], y, ACT.Silu), [done, gfree])
                    self.banks.release(b, [silu])
                self.weights_done(gate, done)
                self.prefetch()
                up = self.weights_take(names[1])
                b, y, done = self.into_bank([P, HALF], self.column_terms(up, (hi, lo), KD, slice(0, HALF)), [up[3]])
                self.weights_done(up, done)
                mul = self.dve.put(lambda e, y=y, f=f, g=g: e.tensor_tensor(f[:, :], g[:, 0:HALF], y, ALU.mult),
                                   [silu, done, ffree])
                self.banks.release(b, [mul])
                gbuf.free[i] = [mul]
                parts = self.split(f[:, :], a_hi[:, j, :], a_lo[:, j, :], [mul], norm_done)
                tmp.free[n] = parts
                a_ready += parts
                self.prefetch()
            banks = self.project_rows(names[2], (a_hi, a_lo), KF, a_ready)
            read = [banks[(3, 1)][1], self.act.last(), self.dve.last()]
            self.phase += 1
            self.cursor = at
            work = self.residual_work(read)
            done = self.add_residual(
                banks, lambda t, half=half: source(half * HALF + t * P, P),
                lambda t, half=half: target(half * HALF + t * P), post, work, read, post_ready)
            stored += done
            x_free = [done, self.pe.last(), self.act.last(), self.dve.last()]
        return stored




    def second_block(self, floor, x2):
        a, s = self.arg, self.scratch
        self.cursor = floor
        free = self.begin_phase(floor)
        self.mod = self.place("mod", [P, 6 * KD, 2])
        self.gate_in = self.place("gate_in", [P, NT + CT, 16])
        self.beta = self.place("beta", [P, NT + CT, 8])
        self.decay = self.place("decay", [P, NT + CT, 8])
        self.modulation(free)
        floor = self.cursor
        free = self.begin_phase(floor)
        self.second_projections(free, x2)
        free = self.begin_phase(floor)
        o_sb = self.delta_rule(free)
        after_o = self.cursor
        free = self.begin_phase(after_o)
        x3 = self.second_mix_outputs(free, o_sb, x2)
        free = self.begin_phase(floor)

        def gains(free):
            gain, ready = self.modulated_row("gain", a["g_pre_ffn_2"], 4, 0, 1.0, free)
            shift, ready2 = self.modulated_row("shift", None, 3, 0, 0.0, free)
            return gain, shift, [ready, ready2]

        def taps(j):
            return [self.ffn_taps[:, n, j:j + 1] for n in range(3)]
        self.ffn_taps = self.place("ffn_taps", [P, 3, KF])
        rows = self.place("ffn_tap_rows", [3 * KF, P])
        landed = self.load(rows[:, :], a["conv_ffn_2"][0].rearrange("w (j p) -> (w j) p", p=P), free)
        b, bank, turned = self.transposes([rows[:, :]], [landed])
        put = self.dve.put(lambda e, bank=bank: e.tensor_copy(
            self.ffn_taps[:, :, :].rearrange("p w j -> p (w j)"), bank[:, :3 * KF]), [turned, free])
        self.banks.release(b, [put])
        self.vec_ready = [self.vec_ready, put]
        self.feed_forward(free, lambda r, n: (s["x3"][r:r + n, :], x3), lambda r: self.out[0, r:r + P, :],
                          gains, lambda free: self.modulated_row("post", a["g_post_ffn_2"], 5, 0, 0.0, free), taps,
                          ("up_gate", "up", "down"))

    def modulation(self, free):
        cs = self.place("cs", [P, KD, 2])
        x = self.act.put(lambda e: e.activation(cs[:, :, 0], self.v_c, ACT.Silu), [free, self.vec_ready])
        x = self.act.put(lambda e: e.activation(cs[:, :, 1], self.v_c_ctx, ACT.Silu), [free])
        b = self.banks.take()
        bank = self.banks.banks[b]
        for j in range(6 * KD):
            block = self.weights_take("mod")
            done = self.product(bank[:, 2 * j:2 * j + 2], [(block[1][:, k, :], cs[:, k, :]) for k in range(KD)],
                                [block[3], x, self.banks.free[b]])
            self.weights_done(block, done)
            self.prefetch()
        put = self.dve.put(lambda e: e.tensor_tensor(
            self.mod[:, :, :], bank[:, 0:12 * KD].rearrange("p (j n) -> p j n", n=2),
            self.v_b_mod.unsqueeze(2).to_broadcast([P, 6 * KD, 2]), ALU.add), [done, free])
        self.banks.release(b, [put])
        self.mod_ready = [put]

    def modulated_row(self, name, gain, index, column, plus, free):
        row = self.place(f"{name}{column}", [P, D])
        spread = self.place(f"{name}{column}_spread", [P, KD, P])
        g_ready = ()
        if gain is not None:
            g_ready = self.load(row[:, :], broadcast(gain, D), free, lane=self.sp)
        x = self.dve.put(lambda e: e.tensor_copy(
            spread[:, :, :], self.mod[:, index * KD:(index + 1) * KD, column].unsqueeze(2).to_broadcast([P, KD, P])),
            [free, self.mod_ready])
        done = []
        for h in range(2):
            b = self.banks.take()
            bank = self.banks.banks[b]
            for k in range(4):
                y = self.product(bank[:, k * P:(k + 1) * P], [(spread[:, 4 * h + k, :], self.ident[:, :])],
                                 [x, self.banks.free[b]])
            cols = slice(h * HALF, (h + 1) * HALF)
            if gain is None:
                put = self.dve.put(lambda e, bank=bank, cols=cols: e.tensor_copy(row[:, cols], bank[:, :]), [y, free])
            else:
                put = self.dve.put(lambda e, bank=bank, cols=cols: e.scalar_tensor_tensor(
                    row[:, cols], bank[:, :], plus, row[:, cols], ALU.add, ALU.mult), [y, g_ready])
            self.banks.release(b, [put])
            done.append(put)
        return row, done

    def second_projections(self, free, x2):
        a, s = self.arg, self.scratch
        x = (self.place("h_hi", [P, KD, S], F32R), self.place("h_lo", [P, KD, S], F32R))
        c = (self.place("c_hi", [P, KD, CTX], F32R), self.place("c_lo", [P, KD, CTX], F32R))
        floor = self.cursor
        ready = []
        for column, n, dst, source in ((0, NT, x, lambda t: (P, s["x2"][t * P:(t + 1) * P, :], t * P, x2)),
                                       (1, CT, c, lambda t: (P, a["ctx_2"][0, t * P:(t + 1) * P, :], t * P, ()))):
            self.phase += 1
            self.cursor = floor
            gain, r1 = self.modulated_row("gain", a["g_pre_mix_2"], 1, column, 1.0, free)
            shift, r2 = self.modulated_row("shift", None, 0, column, 0.0, free)
            work = self.norm_work(free)
            ready += self.norm_to_columns(source, n, dst[0], dst[1], gain, shift, work, free, [r1, r2])
            free = [self.pe.last(), self.act.last(), self.dve.last()]
        self.phase += 1
        self.cursor = floor
        W = S + CTX + 8
        C0 = S + 6
        ring = Ring([(self.place(f"pad{i}", [P, W]), self.place(f"acc{i}", [P, W - 4])) for i in range(2)], free)
        rows = Ring([self.place(f"rows{i}", [P, NT + CT, P]) for i in range(2)], free)
        for i, (pad, _) in enumerate(ring.slots):
            z = [self.dve.put(lambda e, pad=pad, c=c0, n=n: e.memset(pad[:, c:c + n], 0.0), free)
                 for c0, n in ((0, 2), (S + 2, 4), (W - 2, 2))]
            ring.free[i] = z
        work = []
        self.streams = [work]
        stored = []

        def convolve(j, i, pad, acc, put):
            width = S if j < 4 else W - 4
            col = 3 * 0
            token = self.dve.put(lambda e: e.tensor_scalar(acc[:, :width], pad[:, 0:width],
                                                           self.vec[:, 3, j:j + 1], None, ALU.mult), [put, self.vec_ready])
            for tap in range(1, CONV5):
                token = self.dve.put(lambda e, tap=tap: e.scalar_tensor_tensor(
                    acc[:, :width], pad[:, tap:tap + width], self.vec[:, 3, 12 * tap + j:12 * tap + j + 1],
                    acc[:, :width], ALU.mult, ALU.add), [token])
                if tap % 2 == 0:
                    yield
            token = self.act.put(lambda e: e.activation(acc[:, :width], acc[:, :width], ACT.Silu), [token])
            yield
            tiles = [t * P for t in range(NT)] + ([S + 4, S + 4 + P] if j >= 4 else [])
            r, row, rfree = rows.next()
            done = []
            for t0 in range(0, len(tiles), 4):
                part = tiles[t0:t0 + 4]
                b, bank, turned = self.transposes([acc[:, t:t + P] for t in part], [token])
                dst = row[:, t0:t0 + len(part), :].rearrange("p t c -> p (t c)")
                n = len(part) * P
                y = self.act.put(lambda e, dst=dst, bank=bank, n=n: e.activation(dst, bank[:, :n], ACT.Copy), [turned, rfree])
                self.banks.release(b, [y])
                done.append(y)
                yield
            ring.free[i] = [turned]
            n = len(tiles)
            out = self.store(s["qkv"].rearrange("t p c -> p t c")[:, 0:n, j * P:(j + 1) * P], row[:, 0:n, :], done)
            rows.free[r] = [out]
            stored.append(out)

        for j in range(12):
            i, (pad, acc), pfree = self.next_slot(ring)
            block = self.weights_take("qkv")
            put = []
            parts = [(x, slice(0, HALF), 2), (x, slice(HALF, S), 2 + HALF)] + ([(c, slice(0, CTX), C0)] if j >= 4 else [])
            for src, sl, at in parts:
                n = sl.stop - sl.start
                b, y, done = self.into_bank([P, n], self.column_terms(block, src, KD, sl), [block[3], ready])
                z = self.act.put(lambda e, y=y, at=at, n=n, pad=pad: e.activation(pad[:, at:at + n], y, ACT.Copy), [done, pfree])
                self.banks.release(b, [z])
                put.append(z)
                self.pump(2)
            self.weights_done(block, done)
            self.prefetch()
            ring.free[i] = None
            work.append(convolve(j, i, pad, acc, put))
        block = self.weights_take("dn_gates")
        b = self.banks.take()
        bank = self.banks.banks[b]
        _, whi, wlo, _, _ = block
        for t in range(NT + CT):
            src, tok = (x, slice(t * P, (t + 1) * P)) if t < NT else (c, slice((t - NT) * P, (t - NT + 1) * P))
            terms = []
            for k in range(KD):
                terms += [(src[0][:, k, tok], whi[:, k, :]), (src[1][:, k, tok], whi[:, k, :]), (src[0][:, k, tok], wlo[:, k, :])]
            done = self.product(bank[:, 16 * t:16 * t + 16], terms, [block[3], ready, self.banks.free[b]])
        self.weights_done(block, done)
        put = self.dve.put(lambda e: e.tensor_copy(self.gate_in[:, :, :].rearrange("p t c -> p (t c)"),
                                                   bank[:, 0:16 * (NT + CT)]), [done, free])
        self.banks.release(b, [put])
        self.delta_gates(put, free)
        self.finish_background()
        free2 = [self.pe.last(), self.act.last(), self.dve.last(), self.pool.last(), stored]
        self.phase += 1
        self.cursor = floor
        stage = Ring([self.place(f"zstage{i}", [P, HALF]) for i in range(3)], free2)
        blocks = [self.weights_take("z") for _ in range(4)]
        self.z_stored = []
        for t in range(NT):
            tok = slice(t * P, (t + 1) * P)
            terms = []
            for k in range(KD):
                _, whi, wlo, _, _ = blocks[k // 2]
                terms += [(x[0][:, k, tok], whi[:, k % 2, :]), (x[1][:, k, tok], whi[:, k % 2, :]), (x[0][:, k, tok], wlo[:, k % 2, :])]
            b, y, done = self.into_bank([P, HALF], terms, [[q[3] for q in blocks], ready])
            i, st, sfree = stage.next()
            z = self.act.put(lambda e, y=y, st=st: e.activation(st[:, :], y, ACT.Silu), [done, sfree])
            self.banks.release(b, [z])
            out = self.store(s["z"][tok, :], st[:, :], [z])
            stage.free[i] = [out]
            self.z_stored.append(out)
        for q in blocks:
            self.weights_done(q, done)
        self.pooling(x, ready, free2)
        self.qkv_stored = stored

    def delta_gates(self, put, free):
        a = self.arg
        n = NT + CT
        bias, lg = self.place("dt_row", [P, 8]), self.place("alog_row", [P, 8])
        pos, e, s2, q = (self.place(f"soft{i}", [P, n, 8]) for i in range(4))
        l1 = self.load(bias[:, :], broadcast(a["dt_bias_2"], 8), free, lane=self.sp)
        l2 = self.load(lg[:, :], broadcast(a["a_log_2"], 8), free, lane=self.sp)
        beta = self.act.put(lambda v: v.activation(self.beta[:, :, :], self.gate_in[:, :, 0:8], ACT.Sigmoid), [put, free])
        rate = self.act.put(lambda v: v.activation(lg[:, :], lg[:, :], ACT.Exp), [l2])
        av = self.gate_in[:, :, 8:16]
        x = self.dve.put(lambda v: v.tensor_tensor(av, av, bias[:, :].unsqueeze(1).to_broadcast([P, n, 8]), ALU.add),
                         [put, l1, beta])
        self.dve.put(lambda v: v.tensor_scalar(pos[:, :, :], av, 0.0, None, ALU.max), [x, free])
        x = self.dve.put(lambda v: v.tensor_scalar(e[:, :, :], av, -1.0, None, ALU.mult), [x])
        x = self.dve.put(lambda v: v.tensor_tensor(e[:, :, :], e[:, :, :], av, ALU.min), [x])
        x = self.act.put(lambda v: v.activation(e[:, :, :], e[:, :, :], ACT.Exp), [x])
        x = self.dve.put(lambda v: v.tensor_scalar(q[:, :, :], e[:, :, :], 2.0, None, ALU.add), [x])
        x = self.dve.put(lambda v: v.reciprocal(q[:, :, :], q[:, :, :]), [x])
        x = self.dve.put(lambda v: v.tensor_tensor(e[:, :, :], e[:, :, :], q[:, :, :], ALU.mult), [x])
        x = self.dve.put(lambda v: v.tensor_tensor(s2[:, :, :], e[:, :, :], e[:, :, :], ALU.mult), [x])
        x = self.dve.put(lambda v: v.tensor_scalar(q[:, :, :], s2[:, :, :], 1.0 / 19, None, ALU.mult), [x])
        for k in range(8, 0, -1):
            x = self.dve.put(lambda v, k=k: v.scalar_tensor_tensor(q[:, :, :], q[:, :, :], 1.0 / (2 * k + 1), s2[:, :, :],
                                                                   ALU.add, ALU.mult), [x])
        x = self.dve.put(lambda v: v.scalar_tensor_tensor(q[:, :, :], q[:, :, :], 1.0, e[:, :, :], ALU.add, ALU.mult), [x])
        x = self.dve.put(lambda v: v.scalar_tensor_tensor(q[:, :, :], q[:, :, :], 2.0, pos[:, :, :], ALU.mult, ALU.add), [x])
        x = self.dve.put(lambda v: v.scalar_tensor_tensor(self.decay[:, :, :], q[:, :, :], -1.0,
                                                          lg[:, :].unsqueeze(1).to_broadcast([P, n, 8]),
                                                          ALU.mult, ALU.mult), [x, rate])
        self.gates_ready = [x, beta]

    def pooling(self, x, ready, free):
        a, s = self.arg, self.scratch
        cols = [self.place(f"pc{i}", [P, GRID_H, GRID_W + 16]) for i in range(2)]
        rws = [self.place(f"pr{i}", [P, GRID_H + 16, GRID_W]) for i in range(2)]
        u = self.place("pu", [P, S])
        inv = self.place("pinv", [P, S])
        pw = self.place("pw", [P, P])
        y_sb = self.place("py", [P, S])
        self.pool_stored = []
        last = list(free)
        for g, window in enumerate(WINDOWS):
            lw = self.load(pw[:, :], a["pool_w_2"][0, g], [last], lane=self.sp)
            li = self.load(inv[:, :], broadcast(a["k_pool"][g:g + 1, :], S), [last], lane=self.sp)
            zeros = [self.dve.put(lambda e, r=r: e.memset(r[:, :, :], 0.0), last) for r in (cols[0], rws[0])]
            block = self.weights_take("pool")
            put = []
            for n in range(2):
                b, y, done = self.into_bank([P, HALF], self.column_terms(block, x, KD, slice(n * HALF, (n + 1) * HALF)),
                                            [block[3], ready])
                z = self.act.put(lambda e, y=y, n=n: e.activation(u[:, n * HALF:(n + 1) * HALF], y, ACT.Copy), [done, last])
                self.banks.release(b, [z])
                put.append(z)
            self.weights_done(block, done)
            self.prefetch()
            grid = u[:, :].rearrange("p (r c) -> p r c", c=GRID_W)
            tok = self.dve.put(lambda e: e.tensor_copy(cols[0][:, :, 8:8 + GRID_W], grid), [put, zeros])
            src = 0
            m = 1
            while m < window:
                reach = window // 2 - m
                lo_, n_ = 8 - reach, GRID_W + 2 * reach
                l_, r_ = (1, 0) if m == 1 else (m // 2, m // 2)
                tok = self.dve.put(lambda e, src=src, lo_=lo_, n_=n_, l_=l_, r_=r_: e.tensor_tensor(
                    cols[1 - src][:, :, lo_:lo_ + n_], cols[src][:, :, lo_ - l_:lo_ - l_ + n_],
                    cols[src][:, :, lo_ + r_:lo_ + r_ + n_], ALU.add), [tok])
                src, m = 1 - src, 2 * m
            tok = self.dve.put(lambda e, src=src: e.tensor_copy(rws[0][:, 8:8 + GRID_H, :], cols[src][:, :, 8:8 + GRID_W]), [tok])
            src, m = 0, 1
            while m < window:
                reach = window // 2 - m
                lo_, n_ = 8 - reach, GRID_H + 2 * reach
                l_, r_ = (1, 0) if m == 1 else (m // 2, m // 2)
                tok = self.dve.put(lambda e, src=src, lo_=lo_, n_=n_, l_=l_, r_=r_: e.tensor_tensor(
                    rws[1 - src][:, lo_:lo_ + n_, :], rws[src][:, lo_ - l_:lo_ - l_ + n_, :],
                    rws[src][:, lo_ + r_:lo_ + r_ + n_, :], ALU.add), [tok])
                src, m = 1 - src, 2 * m
            box = rws[src][:, 8:8 + GRID_H, :].rearrange("p r c -> p (r c)")
            tok = self.dve.put(lambda e, box=box: e.tensor_tensor(inv[:, :], box, inv[:, :], ALU.mult), [tok, li])
            tok = self.dve.put(lambda e: e.tensor_tensor(u[:, :], inv[:, :], u[:, :], ALU.subtract), [tok])
            outs = []
            for n in range(2):
                sl = slice(n * HALF, (n + 1) * HALF)
                b, y, done = self.into_bank([P, HALF], [(pw[:, :], u[:, sl])], [tok, lw])
                z = self.act.put(lambda e, y=y, sl=sl, g=g: e.activation(y_sb[:, sl], y, ACT.Copy,
                                                                        scale=self.v_pool[:, g:g + 1]), [done, last])
                self.banks.release(b, [z])
                outs.append(z)
            out = self.store(s["pooled"][g], y_sb[:, :], outs)
            self.pool_stored.append(out)
            last = [out, done, self.dve.last()]


    def delta_rule(self, free):
        a, s = self.arg, self.scratch
        o_sb = self.place("o_sum", [P, NT, DW])
        after_o = self.cursor
        kT = self.place("kT", [P, NT + CT, DW])
        qT = self.place("qT", [P, NT, DW])
        tri = self.place("tri", [P, 5, P])
        levels = self.place("levels", [P, 2, LEVELS, P])
        ones = self.place("ones", [P, P])
        ecol = self.place("ecol", [P, 4, NT + CT, DH])
        bcol = self.place("bcol", [P, 2, NT + CT, DH])
        floor = self.cursor
        consts = [self.load(tri[:, :, :].rearrange("p a b -> p (a b)"), a["k_tri"], free, lane=self.sp),
                  self.load(levels[:, :, :, :].rearrange("p a b c -> p (a b c)"), a["k_levels"], free, lane=self.sp),
                  self.dve.put(lambda e: e.memset(ones[:, :], 1.0), free)]
        b = self.banks.take()
        bank = self.banks.banks[b]
        n = (NT + CT) * DH
        for m, (t, d) in enumerate(((0, 0), (1, 1), (3, 0), (2, 1))):
            done = self.product(bank[:, m * n:(m + 1) * n].rearrange("p (t h) -> p t h", h=DH),
                                [(tri[:, t, :], self.decay[:, :, DH * d:DH * d + DH])],
                                [consts, self.gates_ready, self.banks.free[b]])
        x = self.act.put(lambda e, bank=bank: e.activation(ecol[:, :, :, :].rearrange("p a t h -> p (a t h)"),
                                                           bank[:, 0:4 * n], ACT.Exp), [done, free])
        self.banks.release(b, [x])
        for d in range(2):
            x2 = self.dve.put(lambda e, d=d: e.tensor_tensor(bcol[:, d, :, :], self.beta[:, :, DH * d:DH * d + DH],
                                                             ecol[:, d, :, :], ALU.mult), [x, free])
        cols_ready = [x, x2]
        ring = Ring([self.place(f"qkv{i}", [P, 3 * DW]) for i in range(2)], free)
        sq = self.place("sq", [P, 2 * DW])
        st = Ring([self.place(f"qst{i}", [P, 8]) for i in range(2)], free)
        turned_ready, k_stored = {}, {}
        sq_free = list(free)
        for t in range(NT + CT):
            c0, heads = (0, 8) if t < NT else (DW, 4)
            i, q, qfree = ring.next()
            j, r, rfree = st.next()
            landed = self.load(q[:, c0:2 * DW], s["qkv"][t, :, c0:2 * DW], [qfree, self.qkv_stored], lane=self.sp)
            w = heads * P
            qk3 = q[:, c0:2 * DW].rearrange("p (h d) -> p h d", d=P)
            x = self.dve.put(lambda e, q=q, c0=c0, w=w: e.tensor_tensor(sq[:, :w], q[:, c0:2 * DW], q[:, c0:2 * DW], ALU.mult),
                             [landed, sq_free])
            x = self.dve.put(lambda e, r=r, w=w, heads=heads: e.tensor_reduce(
                r[:, 0:heads], sq[:, :w].rearrange("p (h d) -> p h d", d=P), AX.X, ALU.add), [x, rfree])
            sq_free = [x]
            x = self.inverse_root(r[:, 0:heads], r[:, 0:heads], 1.0, RMS_EPS, [x])
            if t < NT:
                x = self.dve.put(lambda e, r=r: e.tensor_scalar(r[:, 0:4], r[:, 0:4], float(P) ** -0.5, None, ALU.mult), [x])
            x = self.dve.put(lambda e, qk3=qk3, r=r, heads=heads: e.tensor_tensor(
                qk3, qk3, r[:, 0:heads].unsqueeze(2).to_broadcast([P, heads, P]), ALU.mult), [x])
            st.free[j] = [x]
            out = self.store(s["qkv"][t, :, DW:2 * DW], q[:, DW:2 * DW], [x])
            k_stored[t] = out
            done = []
            for col, dst in ((0, qT), (DW, kT)):
                if col < c0:
                    continue
                b, bank, turned = self.transposes([q[:, col + h * P:col + (h + 1) * P] for h in range(DH)], [x])
                put = self.act.put(lambda e, dst=dst, bank=bank, t=t: e.activation(dst[:, t, :], bank[:, :], ACT.Copy),
                                   [turned, free])
                self.banks.release(b, [put])
                done.append(put)
            turned_ready[t] = done
            ring.free[i] = [out, turned]
        setup = [self.pe.last(), self.act.last(), self.dve.last(), list(k_stored.values())]
        self.phase += 1
        self.cursor = floor
        shape = [P, DH, P]
        state = [self.place(f"state{d}", shape) for d in range(2)]
        tmp = [{n: self.place(f"{n}{d}", shape) for n in ("A", "L", "C", "Y", "T", "W", "DT", "kbe", "vb")} for d in range(2)]
        kv = [Ring([self.place(f"kv{d}{i}", [P, 2 * DW]) for i in range(1)], setup) for d in range(2)]
        outs = [{n: self.place(f"{n}{d}", shape) for n in ("wT", "u", "kdec", "qdT", "attnT", "E", "vn")} for d in range(2)]
        state_ready = [self.dve.put(lambda e, st=st: e.memset(st[:, :, :], 0.0), setup) for st in state]
        tmp_free = [list(setup), list(setup)]
        outs_free = [list(setup), list(setup)]
        o_ready = {}
        order = [[NT, NT + 1] + list(range(NT)), [NT + 1, NT] + list(range(NT - 1, -1, -1))]
        prepared = [{}, {}]

        def heads(x):
            return x[:, :, :].rearrange("p h c -> p (h c)")

        def four(bank):
            return bank[:, :].rearrange("p (h c) -> p h c", h=DH)

        def wide(x):
            return x.unsqueeze(1).to_broadcast([P, DH, P])

        def each(fn, after):
            b = self.banks.take()
            bank = self.banks.banks[b]
            for h in range(DH):
                lhsT, rhs = fn(h)
                token = self.product(bank[:, h * P:(h + 1) * P], [(lhsT, rhs)], [after, self.banks.free[b]] if h == 0 else ())
            return b, bank, token

        def prepare(d, t):
            m, out = tmp[d], outs[d]
            is_x = t < NT
            tri_in, strict = (tri[:, 0, :], tri[:, 3, :]) if d == 0 else (tri[:, 1, :], tri[:, 2, :])
            free = tmp_free[d]
            i, kvt, kvfree = kv[d].next()
            landed = self.load(kvt[:, :], s["qkv"][t, :, DW:3 * DW], [kvfree, k_stored[t]], lane=self.sp)
            k3 = kvt[:, 0:DW].rearrange("p (h c) -> p h c", h=DH)
            v3 = kvt[:, DW:2 * DW].rearrange("p (h c) -> p h c", h=DH)

            def by_row(col):
                return col.unsqueeze(2).to_broadcast([P, DH, P])
            A = self.dve.put(lambda e: e.tensor_tensor(m["A"][:, :, :], wide(tri_in),
                                                       by_row(self.decay[:, t, DH * d:DH * d + DH]), ALU.mult),
                             [free, self.gates_ready, consts])
            b, bank, x = each(lambda h: (m["A"][:, h, :], strict), [A])
            D = self.act.put(lambda e, bank=bank: e.activation(heads(m["L"]), bank[:, :], ACT.Exp), [x, free])
            self.banks.release(b, [D])
            b, bank, x = each(lambda h: (kT[:, t, h * P:(h + 1) * P], kT[:, t, h * P:(h + 1) * P]), [turned_ready[t]])
            for h in range(DH):
                L = self.dve.put(lambda e, h=h, bank=bank: e.scalar_tensor_tensor(
                    m["L"][:, h, :], bank[:, h * P:(h + 1) * P], self.beta[:, t, DH * d + h:DH * d + h + 1], m["L"][:, h, :],
                    ALU.mult, ALU.mult), [x, D])
            self.banks.release(b, [L])
            kbe = self.pool.put(lambda e: e.tensor_tensor(m["kbe"][:, :, :], k3, by_row(bcol[:, d, t, :]), ALU.mult),
                                [landed, cols_ready, free])
            vb = self.pool.put(lambda e: e.tensor_tensor(m["vb"][:, :, :], v3,
                                                         by_row(self.beta[:, t, DH * d:DH * d + DH]), ALU.mult),
                               [landed, free])
            yield
            c = self.pool.put(lambda e: e.tensor_tensor(m["C"][:, :, :], m["L"][:, :, :], wide(levels[:, d, 0, :]), ALU.mult), [L, free])
            T = self.dve.put(lambda e: e.tensor_tensor(m["T"][:, :, :], wide(self.ident[:, :]), m["C"][:, :, :], ALU.subtract), [c, free])
            b, bank, x = self.transposes([m["C"][:, h, :] for h in range(DH)], [c])
            W = self.dve.put(lambda e, bank=bank: e.tensor_tensor(m["W"][:, :, :], wide(self.ident[:, :]), four(bank), ALU.subtract), [x, free])
            self.banks.release(b, [W])
            yield
            for lv in range(1, LEVELS):
                c = self.pool.put(lambda e, lv=lv: e.tensor_tensor(m["C"][:, :, :], m["L"][:, :, :],
                                                                   wide(levels[:, d, lv, :]), ALU.mult), [x, T])
                b, bank, x = each(lambda h: (m["C"][:, h, :], m["W"][:, h, :]), [c, W])
                Y = self.act.put(lambda e, bank=bank: e.activation(heads(m["Y"]), bank[:, :], ACT.Copy), [x, free, T])
                self.banks.release(b, [Y])
                yield
                b, bank, x = each(lambda h: (m["T"][:, h, :], m["Y"][:, h, :]), [Y, T])
                if lv < LEVELS - 1:
                    b2, bank2, x2 = each(lambda h: (m["Y"][:, h, :], m["T"][:, h, :]), [Y, T])
                W = self.dve.put(lambda e, bank=bank: e.tensor_tensor(heads(m["W"]), heads(m["W"]), bank[:, :], ALU.subtract), [x])
                self.banks.release(b, [W])
                if lv < LEVELS - 1:
                    T = self.dve.put(lambda e, bank=bank2: e.tensor_tensor(heads(m["T"]), heads(m["T"]), bank[:, :], ALU.subtract), [x2])
                    self.banks.release(b2, [T])
                    x = x2
                yield
            ofree = outs_free[d]
            if ofree is None:
                while outs_free[d] is None:
                    yield
                ofree = outs_free[d]
            b, bank, x = each(lambda h: (m["kbe"][:, h, :], m["W"][:, h, :]), [kbe, W])
            wT = self.act.put(lambda e, bank=bank: e.activation(heads(out["wT"]), bank[:, :], ACT.Copy), [x, ofree])
            self.banks.release(b, [wT])
            b, bank, x = each(lambda h: (m["W"][:, h, :], m["vb"][:, h, :]), [vb, W])
            u = self.act.put(lambda e, bank=bank: e.activation(heads(out["u"]), bank[:, :], ACT.Copy), [x, ofree])
            self.banks.release(b, [u])
            kdec = self.pool.put(lambda e: e.tensor_tensor(out["kdec"][:, :, :], k3, by_row(ecol[:, 2 + d, t, :]), ALU.mult), [ofree, kbe])
            kv[d].free[i] = [kdec, vb]
            yield
            b, bank, x = self.into_bank([P, HALF], [(ones[:, :], heads(m["A"]))], [A])
            E = self.act.put(lambda e, bank=bank: e.activation(heads(out["E"]), bank, ACT.Exp), [x, ofree])
            self.banks.release(b, [E])
            done = [wT, u, kdec, E]
            if is_x:
                qd = self.dve.put(lambda e: e.tensor_tensor(heads(out["qdT"]), qT[:, t, :], heads(out["E"]), ALU.mult), [E, ofree, turned_ready[t]])
                b, bank, x = self.into_bank([P, HALF], [(strict, heads(m["A"]))], [A])
                DT = self.act.put(lambda e, bank=bank: e.activation(heads(m["DT"]), bank, ACT.Exp), [x, free])
                self.banks.release(b, [DT])
                DT = self.dve.put(lambda e: e.tensor_tensor(m["DT"][:, :, :], m["DT"][:, :, :], wide(tri_in), ALU.mult), [DT])
                yield
                b, bank, x = each(lambda h: (kT[:, t, h * P:(h + 1) * P], qT[:, t, h * P:(h + 1) * P]), ())
                at = self.dve.put(lambda e, bank=bank: e.tensor_tensor(heads(out["attnT"]), heads(m["DT"]), bank[:, :], ALU.mult), [DT, x, ofree])
                self.banks.release(b, [at])
                done += [qd, at]
            tmp_free[d] = [self.pe.last(), self.act.last(), self.dve.last(), kbe, vb, c]
            outs_free[d] = None
            prepared[d][t] = done

        def recur(d, t):
            while t not in prepared[d]:
                yield
            ready = prepared[d][t]
            out, S_ = outs[d], state[d]
            is_x = t < NT
            if is_x:
                bo = self.banks.take()
                bank_o = self.banks.banks[bo]
            for n, c in enumerate((0, 1) if d == 0 else (1, 0)):
                R = slice(c * CHUNK, (c + 1) * CHUNK)
                last = c * CHUNK + (CHUNK - 1 if d == 0 else 0)
                b = self.banks.take()
                bank = self.banks.banks[b]
                for h in range(DH):
                    x = self.product(bank[R, h * P:(h + 1) * P], [(out["wT"][:, h, R], S_[:, h, :])],
                                     [ready, state_ready[d], self.banks.free[b]] if h == 0 else ())
                if is_x:
                    for h in range(DH):
                        xo = self.pe.put(lambda e, h=h, R=R: e.matmul(
                            bank_o[R, h * P:(h + 1) * P], out["qdT"][:, h, R], S_[:, h, :],
                            start=h == 0, stop=False, skip_group_check=True), [self.banks.free[bo]])
                vn = self.dve.put(lambda e, R=R, bank=bank: e.tensor_tensor(
                    out["vn"][R, :, :].rearrange("p h c -> p (h c)"), out["u"][R, :, :].rearrange("p h c -> p (h c)"),
                    bank[R, :], ALU.subtract), [x, outs_free_at[d]])
                self.banks.release(b, [vn])
                yield
                b = self.banks.take()
                bank = self.banks.banks[b]
                for h in range(DH):
                    x = self.product(bank[:, h * P:(h + 1) * P], [(out["kdec"][R, h, :], out["vn"][R, h, :])],
                                     [vn, self.banks.free[b]] if h == 0 else ())
                for h in range(DH):
                    st = self.dve.put(lambda e, h=h, bank=bank, last=last: e.scalar_tensor_tensor(
                        S_[:, h, :], S_[:, h, :], out["E"][:, h, last:last + 1], bank[:, h * P:(h + 1) * P],
                        ALU.mult, ALU.add), [x, xo if is_x else ()])
                self.banks.release(b, [st])
                state_ready[d] = [st]
                yield
            if is_x:
                for h in range(DH):
                    x = self.pe.put(lambda e, h=h: e.matmul(
                        bank_o[:, h * P:(h + 1) * P], out["attnT"][:, h, :], out["vn"][:, h, :],
                        start=False, stop=True, skip_group_check=True), [vn])
                if t not in o_ready:
                    o = self.act.put(lambda e: e.activation(o_sb[:, t, :], bank_o[:, :], ACT.Copy), [x, free_o])
                else:
                    o = self.dve.put(lambda e: e.tensor_tensor(o_sb[:, t, :], o_sb[:, t, :], bank_o[:, :], ALU.add),
                                     [x, o_ready[t]])
                o_ready[t] = [o]
                self.banks.release(bo, [o])
            outs_free_at[d] = [self.pe.last(), self.dve.last()]
            outs_free[d] = outs_free_at[d]

        free_o = free
        outs_free_at = [list(setup), list(setup)]
        self.streams = [[prepare(d, t) for t in order[d]] for d in range(2)] + \
                       [[recur(d, t) for t in order[d]] for d in range(2)]
        self.finish_background()
        self.o_ready = list(o_ready.values())
        self.cursor = after_o
        return o_sb

    def second_mix_outputs(self, free, o_sb, x2):
        a, s = self.arg, self.scratch
        gain, gain_ready = self.modulated_row("post", a["g_post_mix_2"], 2, 0, 0.0, free)
        norm = self.place("onorm", [P, P])
        nl = self.load(norm[:, :], broadcast(a["o_norm_2"], P), free, lane=self.sp)
        mix = (self.place("mix_hi", [P, KD, HALF], F32R), self.place("mix_lo", [P, KD, HALF], F32R))
        z = Ring([self.place(f"zrow{i}", [P, DW]) for i in range(2)], free)
        pl = Ring([self.place(f"prow{i}", [P, HALF]) for i in range(2)], free)
        sq, st = self.place("osq", [P, DW]), self.place("ost", [P, DH])
        work = self.residual_work(free)
        mix_free = list(free)
        stored = []
        for half in range(2):
            ready = []
            for g in range(4):
                i, q, qfree = pl.next()
                l = self.load(q[:, :], s["pooled"][g, :, half * HALF:(half + 1) * HALF], [qfree, self.pool_stored], lane=self.sp)
                parts = self.split(q[:, :], mix[0][:, 4 + g, :], mix[1][:, 4 + g, :], [l], mix_free)
                pl.free[i] = parts
                ready += parts
            for t in range(4):
                tile = half * 4 + t
                o = o_sb[:, tile, :]
                o3 = o.rearrange("p (h d) -> p h d", h=DH)
                i, zr, zfree = z.next()
                lz = self.load(zr[:, :], s["z"][tile * P:(tile + 1) * P, :], [zfree, self.z_stored], lane=self.sp)
                x = self.dve.put(lambda e, o=o: e.tensor_tensor(sq[:, :], o, o, ALU.mult), [self.o_ready, free])
                x = self.dve.put(lambda e: e.tensor_reduce(st[:, :], sq[:, :].rearrange("p (h d) -> p h d", h=DH), AX.X, ALU.add), [x])
                x = self.inverse_root(st[:, :], st[:, :], 1.0 / P, RMS_EPS, [x])
                x = self.dve.put(lambda e, o3=o3: e.tensor_tensor(o3, o3, st[:, :].unsqueeze(2).to_broadcast([P, DH, P]), ALU.mult), [x])
                x = self.dve.put(lambda e, o3=o3: e.tensor_tensor(o3, o3, norm[:, :].unsqueeze(1).to_broadcast([P, DH, P]), ALU.mult), [x, nl])
                x = self.dve.put(lambda e, o=o, zr=zr: e.tensor_tensor(o, o, zr[:, :], ALU.mult), [x, lz])
                z.free[i] = [x]
                b, bank, turned = self.transposes([o[:, k * P:(k + 1) * P] for k in range(4)], [x])
                dst = slice(t * P, (t + 1) * P)
                parts = self.split(bank[:, :].rearrange("p (k t) -> p k t", k=4), mix[0][:, 0:4, dst], mix[1][:, 0:4, dst],
                                   [turned], mix_free)
                self.banks.release(b, parts)
                ready += parts
            banks = self.project_rows("w_out", mix, KD, ready)
            mix_free = [banks[(3, 1)][1]]
            stored += self.add_residual(
                banks, lambda t, half=half: (s["x2"][half * HALF + t * P:half * HALF + (t + 1) * P, :], x2),
                lambda t, half=half: s["x3"][half * HALF + t * P:half * HALF + (t + 1) * P, :], gain, work, (), gain_ready)
        return stored



def broadcast(row, n):
    return bass.AP(tensor=row.tensor, offset=row.offset, ap=[[0, P], [1, n]])


def bank_view(bank, shape):
    return bank[:shape[0], :shape[1]]


def group_tokens(x, k, g, t):
    if g == 0:
        return x[:, k, t * P:(t + 1) * P]
    classes = CLASSES[g]
    first = t % (NT // classes) * P
    return x[:, k, :].rearrange("p (m c) -> p c m", c=classes)[:, t * classes // NT, first:first + P]


def class_order(dst, y, g, n):
    c = CLASSES[g]
    if c == 1:
        return dst[:, n * HALF:(n + 1) * HALF], y
    m = HALF // c
    return (dst[:, :].rearrange("p (c m) -> p m c", c=c)[:, n * m:(n + 1) * m, :],
            y.rearrange("p (m c) -> p m c", c=c))


def shifted(base, start, rows, cols):
    return bass.AP(tensor=base.tensor, offset=base.offset + start, ap=[[TOEP - 1, rows], [1, cols]])


def unit_stores(sums, u, g, pair):
    w = HD + 2
    cols = slice(2 * pair * w, (2 * pair + 2) * w)
    if g == 0:
        return [(sums.rearrange("(t p) w -> p t w", p=P)[:, :, cols], u[:, :, :, :].rearrange("p t h w -> p t (h w)"))]
    if g == 1:
        view = sums.rearrange("(h p c) w -> c p h w", h=2, c=4)
        return [(view[c][:, :, cols], u[:, 2 * c:2 * c + 2, :, :].rearrange("p t h w -> p t (h w)")) for c in range(4)]
    return [(sums.rearrange("(p t) w -> p t w", t=8)[:, :, cols], u[:, :, :, :].rearrange("p t h w -> p t (h w)"))]



def column_blocks(w, name, cols, k=KD, width=P):
    return [(name, w.rearrange("(k p) n -> p k n", p=P)[:, :, c:c + width], k, width, True) for c in cols]


def row_blocks(w, name, c0, k_all):
    return [(name, w.rearrange("(k p) n -> p k n", p=P)[:, k:k + 2, c0:c0 + HALF], 2, HALF, True)
            for k in range(0, k_all, 2)]


def first_plan(a):
    w, plan = a["w_in"][0], []

    def glu(j):
        return column_blocks(w, "glu_gate", [GLU0 + D + j * P]) + column_blocks(w, "glu_u", [GLU0 + j * P])
    plan += glu(0) + glu(1)
    for g in range(NG):
        base = g * NH * HD
        plan += row_blocks(w, "v", 2 * ATTN_W + base, KD)
        for pair in range(NH // 2):
            plan += column_blocks(w, "q", [base + pair * P]) + column_blocks(w, "k", [ATTN_W + base + pair * P])
            if pair % 2:
                plan += glu(2 + 2 * g + pair // 2)
    for j in range(KD):
        plan += column_blocks(w, "gate_attn", [GA0 + j * P]) + column_blocks(w, "gate_conv", [GC0 + j * P])
    for _ in range(2):
        for j in range(KD):
            plan += column_blocks(a["w_conv_out"][0], "conv_out", [j * P])
            plan += column_blocks(a["w_attn_out"][0], "attn_out", [j * P], k=4)
        for c in range(2):
            plan += row_blocks(a["w_mix_out"][0], "mix_out", c * HALF, KD)
    return plan + ffn_plan(a["w_ffn_in"][0], a["w_ffn_out"][0], ("ffn_gate", "ffn_up", "ffn_down"))


def second_plan(a):
    w = a["w_in_2"][0]
    mod = a["w_mod_2"][0].rearrange("(k p) n -> p k n", p=P)
    plan = [("mod", mod[:, :, j * P:(j + 1) * P], KD, P, False) for j in range(6 * KD)]
    plan += column_blocks(w, "qkv", [j * P for j in range(12)])
    plan += column_blocks(w, "dn_gates", [GATE0], width=16)
    plan += row_blocks(w, "z", 3 * DW, KD)
    plan += column_blocks(w, "pool", [POOL0 + g * P for g in range(4)])
    for _ in range(2):
        for c in range(2):
            plan += row_blocks(a["w_out_2"][0], "w_out", c * HALF, KD)
    return plan + ffn_plan(a["w_up_2"][0], a["w_down_2"][0], ("up_gate", "up", "down"))


def ffn_plan(w_in, w_out, names):
    plan = []
    for _ in range(2):
        for j in range(KF):
            plan += column_blocks(w_in, names[0], [j * P]) + column_blocks(w_in, names[1], [FFN + j * P])
        for c in range(2):
            plan += row_blocks(w_out, names[2], c * HALF, KF)
    return plan


def build(nc, arg, scratch, out, blocks=2):
    ctx = ExitStack()
    with ctx:
        p = Program(nc, ctx, arg, scratch, out)
        a, s = arg, scratch
        plan = first_plan(a)
        if blocks == 2:
            plan += second_plan(a)
        p.weights_begin(plan)
        p.prefetch()
        p.setup()
        floor = p.cursor
        free = p.begin_phase(floor)
        p.first_mix_projections(free)
        free = p.begin_phase(floor)
        x1 = p.first_mix_outputs(free)
        free = p.begin_phase(floor)

        def gains(rows_src):
            def get(free):
                row, ready = p.row_load("gain", rows_src, free)
                return row, None, ready
            return get
        target = s["x2"] if blocks == 2 else out[0]
        x2 = p.feed_forward(free, lambda r, n: (s["x1"][r:r + n, :], x1), lambda r: target[r:r + P, :],
                            gains(a["g_pre_ffn"]), lambda free: p.row_load("post", a["g_post_ffn"], free), None,
                            ("ffn_gate", "ffn_up", "ffn_down"))
        if blocks == 2:
            p.second_block(floor, x2)
        p.pool.put(lambda e: e.memset(p.mean[0:1, 0:1], 1.0 / D), [x.last() for x in p.misc])
        block = ctx.enter_context(nc.Block())
        block.sync(p.sp.play)
        block.gpsimd(p.pool.play)
        block.scalar(p.act.play)
        block.vector(p.dve.play)
        block.tensor(p.pe.play)


_OUTS = [((1, S, D), "float32")]
_SCRATCH = {
    "toeplitz": (NG * NH, P * TOEP), "sums": (NG, S, NH * (HD + 2)), "gates": (2, KD, P, S), "conv": (KD, P, S),
    "x1": (S, D), "x2": (S, D), "x3": (S, D), "qkv": ((NT + CT), P, 3 * DW), "z": (S, DW), "pooled": (4, P, S),
}


def kernel(**inputs):
    import concourse.bacc as _bacc
    from concourse.bass_utils import run_bass_kernel_spmd as _run

    nc = _bacc.Bacc("TRN2", target_bir_lowering=False, num_devices=1)
    arrays, arg = {}, {}
    for name, value in {**inputs, **constants()}.items():
        value = np.ascontiguousarray(value)
        arrays[f"in_{name}_dram"] = value
        arg[name] = nc.dram_tensor(f"in_{name}_dram", value.shape, mybir.dt.from_np(value.dtype),
                                   kind="ExternalInput").ap()
    scratch = {name: nc.dram_tensor(f"scratch_{name}", shape, F32, kind="Internal").ap()
               for name, shape in _SCRATCH.items()}
    outs = [nc.dram_tensor(f"out_{i}_dram", shape, mybir.dt.from_np(np.dtype(dtype)), kind="ExternalOutput").ap()
            for i, (shape, dtype) in enumerate(_OUTS)]
    build(nc, arg, scratch, outs[0])
    r = _run(nc, [arrays], core_ids=[0])
    return r.results[0]["out_0_dram"]
```

```python
from contextlib import ExitStack

import numpy as np

import concourse.bass as bass
from concourse import mybir

F32 = mybir.dt.float32
F32R = mybir.dt.float32r
ALU = mybir.AluOpType
ACT = mybir.ActivationFunctionType
AX = mybir.AxisListType

P = 128
S = 1024
D = 1024
KD = D // P
HALF = 512
NT = S // P
HD = 64
NH = 8
DILATION = (1, 4, 16)
CLASSES = (1, 4, 8)
NG = 3
ATTN_W = NG * NH * HD
FFN = 2816
KF = FFN // P
TAPS = 31
RMS_EPS = 1e-6
LN_EPS = 1e-5
BUCKETS, MAX_DISTANCE = 32, 2048
TOEP = 384
GLU0 = 3 * ATTN_W
GA0 = GLU0 + 2 * D
GC0 = GA0 + D

CTX = 256
CT = CTX // P
DH = 4
DW = 512
CHUNK = 64
CONV5 = 5
GRID_W = 64
GRID_H = S // GRID_W
WINDOWS = (2, 4, 8, 16)
GATE0 = 4 * DW
POOL0 = GATE0 + 4 * DH
POOL_AFTER = (3, 6, 9, 11)
LEVELS = 6



def rel_buckets(distance):
    exact = BUCKETS // 2
    d = np.maximum(distance, 0)
    df = np.maximum(d, 1).astype(np.float32)
    large = exact + (np.log(df / np.float32(exact)) / np.float32(np.log(MAX_DISTANCE / exact))
                     * (BUCKETS - exact)).astype(np.int32)
    return np.where(d < exact, d, np.minimum(large, BUCKETS - 1))


def constants():
    offset = 255 - np.arange(TOEP)
    onehot = np.zeros((BUCKETS, NG, TOEP), np.float32)
    invalid = np.zeros((NG, TOEP), np.float32)
    for g, (dil, classes) in enumerate(zip(DILATION, CLASSES)):
        step = dil // classes
        valid = (offset >= 0) & (offset <= 128 * step) & (offset % step == 0)
        b = rel_buckets(offset * classes)
        onehot[b[valid], g, np.flatnonzero(valid)] = 1.0
        invalid[g] = np.where(valid, 0.0, -1e30)
    i = np.arange(P)
    same = (i[:, None] // CHUNK) == (i[None, :] // CHUNK)
    upper_in = same & (i[:, None] <= i[None, :])
    lower_in = same & (i[:, None] >= i[None, :])
    upper_ex = same & (i[:, None] < i[None, :])
    lower_ex = same & (i[:, None] > i[None, :])
    tri = np.stack([upper_in, lower_in, upper_ex, lower_ex, same], 1).astype(np.float32)
    levels = np.zeros((P, 2, LEVELS, P), np.float32)
    for lv in range(LEVELS):
        b = 1 << lv
        pair = (i[:, None] // (2 * b)) == (i[None, :] // (2 * b))
        levels[:, 0, lv] = pair & ((i[:, None] // b) > (i[None, :] // b))
        levels[:, 1, lv] = pair & ((i[:, None] // b) < (i[None, :] // b))
    inv = np.zeros((len(WINDOWS), S), np.float32)
    for w, win in enumerate(WINDOWS):
        left, right = win // 2, win - 1 - win // 2

        def count(n):
            j = np.arange(n)
            return (np.clip(j + right + 1, 0, n) - np.clip(j - left, 0, n)).astype(np.float32)
        inv[w] = (1.0 / (count(GRID_H)[:, None] * count(GRID_W)[None, :])).reshape(-1)
    return {
        "k_onehot": onehot.reshape(BUCKETS, NG * TOEP),
        "k_invalid": invalid,
        "k_ident": np.eye(P, dtype=np.float32),
        "k_tri": tri.reshape(P, 5 * P),
        "k_levels": levels.reshape(P, 2 * LEVELS * P),
        "k_pool": inv,
    }



class Lane:

    def __init__(self, sem):
        self.sem, self.count, self.ops, self.waited = sem, 0, [], {}

    def put(self, fn, after=(), mark=True):
        waits = []
        for token in flat(after):
            if self.waited.get(token[0], 0) < token[1]:
                self.waited[token[0]] = token[1]
                waits.append(token)
        waits = [w for n, w in enumerate(waits) if all(v[0] != w[0] for v in waits[n + 1:])]
        if mark:
            self.count += 1
        self.ops.append((waits, fn, (self.sem, 1) if mark else None))
        return (self.sem, self.count)

    def put_dma(self, fn, counter, after=()):
        counter.count += 16
        self.put(fn, after, mark=False)
        waits, fn, _ = self.ops.pop()
        self.ops.append((waits, fn, (counter.sem, 16)))
        return (counter.sem, counter.count)

    def last(self):
        return (self.sem, self.count)

    def play(self, eng):
        for waits, fn, inc in self.ops:
            for sem, value in waits:
                eng.wait_ge(sem, value)
            ins = fn(eng)
            if inc:
                ins.then_inc(*inc)


class Counter:
    def __init__(self, sem):
        self.sem, self.count = sem, 0

    def last(self):
        return (self.sem, self.count)


def flat(tokens):
    if tokens is None:
        return []
    if isinstance(tokens, tuple) and len(tokens) == 2 and isinstance(tokens[1], int):
        return [tokens] if tokens[1] > 0 else []
    out = []
    for t in tokens:
        out += flat(t)
    return out


class Ring:

    def __init__(self, slots, free=()):
        self.slots, self.at = slots, -1
        self.free = [list(flat(free)) for _ in slots]

    def next(self):
        self.at = (self.at + 1) % len(self.slots)
        return self.at, self.slots[self.at], self.free[self.at]


class Banks:

    def __init__(self, banks):
        self.banks, self.free, self.idle = banks, [[] for _ in banks], list(range(len(banks)))

    def take(self):
        return self.idle.pop(0)

    def release(self, b, tokens):
        self.idle.append(b)
        self.free[b] = flat(tokens)


class Program:
    def __init__(self, nc, ctx, arg, scratch, out):
        self.nc, self.arg, self.scratch, self.out = nc, arg, scratch, out

        def sem(name):
            return ctx.enter_context(nc.semaphore(name))
        self.pe, self.act, self.dve = Lane(sem("s_pe")), Lane(sem("s_act")), Lane(sem("s_dve"))
        self.pool, self.sp = Lane(sem("s_pool")), Lane(sem("s_sp"))
        self.raw_counters = [Counter(sem(f"s_weights{i}")) for i in range(3)]
        self.queues = {lane: [0, [Counter(sem(f"s_{name}{i}")) for i in range(12)]]
                       for name, lane in (("dma_sp", self.sp), ("dma_pool", self.pool))}
        self.misc = [c for _, counters in self.queues.values() for c in counters]
        banks = [ctx.enter_context(nc.psum_tensor(f"bank{i}", [P, HALF], F32)) for i in range(8)]
        self.banks = Banks(banks)
        self.streams, self.turn_of = [], 0
        self.base = (nc.sbuf_base + 63) // 64 * 64
        self.limit = nc.sbuf_usable_end
        self.cursor = self.base
        self.phase = 0


    def place(self, name, shape, dtype=F32):
        size = int(np.prod(shape[1:])) * 4
        t = self.nc.alloc_sbuf_tensor_at(f"{name}_{self.phase}", shape, dtype, offset=self.cursor)
        self.cursor += (size + 31) // 32 * 32
        assert self.cursor <= self.limit, (name, self.cursor, self.limit)
        return t

    def begin_phase(self, floor):
        self.phase += 1
        self.cursor = floor
        return [x.last() for x in (self.pe, self.act, self.dve, self.pool, *self.misc)]


    def load(self, dst, src, after=(), lane=None):
        lane = lane or self.pool
        at, counters = self.queues[lane]
        c = counters[at]
        self.queues[lane][0] = (at + 1) % len(counters)
        return lane.put_dma(lambda e: e.dma_start(dst, src), c, after)

    store = load


    def weights_begin(self, plan):
        self.plan = plan
        self.raw_ring = Ring([self.place(f"raw{i}", [P, 1024]) for i in range(3)])
        self.split_ring = Ring([(self.place(f"whi{i}", [P, 1024], F32R), self.place(f"wlo{i}", [P, 1024], F32R))
                                for i in range(5)])
        self.ready, self.fetched, self.taken = [], 0, 0

    def fetch(self):
        name, src, k, n, split = self.plan[self.fetched]
        i, raw, free = self.raw_ring.next()
        view = raw[:, :k * n].rearrange("p (k n) -> p k n", k=k)
        landed = self.sp.put_dma(lambda e: e.dma_start(view, src), self.raw_counters[i], free)
        if not split:
            self.raw_ring.free[i] = None
            self.ready.append((name, view, None, landed, i))
        else:
            j, (hi, lo), sfree = self.split_ring.next()
            assert sfree is not None, name
            h, l = hi[:, :k * n], lo[:, :k * n]
            high = self.act.put(lambda e: e.activation(h, raw[:, :k * n], ACT.Copy), [landed, sfree])
            low = self.dve.put(lambda e: e.tensor_tensor(l, raw[:, :k * n], h.bitcast(F32), ALU.subtract),
                               [high, sfree])
            self.raw_ring.free[i] = [low]
            self.split_ring.free[j] = None
            self.ready.append((name, h.rearrange("p (k n) -> p k n", k=k),
                               l.rearrange("p (k n) -> p k n", k=k), [high, low], j))
        self.fetched += 1

    def weights_take(self, name):
        while self.fetched <= self.taken:
            self.fetch()
        self.prefetch()
        block = self.ready[self.taken]
        assert block[0] == name, (block[0], name)
        self.taken += 1
        return block

    def prefetch(self):
        while self.fetched < min(self.taken + 4, len(self.plan)):
            ring = self.raw_ring if not self.plan[self.fetched][4] else self.split_ring
            raw_next = self.raw_ring.free[(self.raw_ring.at + 1) % 3]
            if raw_next is None or ring.free[(ring.at + 1) % len(ring.slots)] is None:
                return
            self.fetch()

    def weights_done(self, block, token):
        ring = self.raw_ring if block[2] is None else self.split_ring
        ring.free[block[4]] = [token]


    def pump(self, n=1):
        for _ in range(n):
            busy = [x for x in self.streams if x]
            if not busy:
                return
            self.turn_of += 1
            work = busy[self.turn_of % len(busy)]
            if next(work[0], True):
                work.pop(0)

    def finish_background(self):
        while any(self.streams):
            self.pump()

    def next_slot(self, ring):
        while ring.free[(ring.at + 1) % len(ring.slots)] is None:
            self.pump()
        return ring.next()


    def product(self, out, terms, after=()):
        for n, (lhsT, rhs) in enumerate(terms):
            first, last = n == 0, n == len(terms) - 1
            token = self.pe.put(lambda e, a=lhsT, b=rhs, s=first, t=last: e.matmul(out, a, b, start=s, stop=t),
                                after if first else (), mark=last)
        return token

    def into_bank(self, shape, terms, after=()):
        b = self.banks.take()
        view = bank_view(self.banks.banks[b], shape)
        return b, view, self.product(view, terms, [self.banks.free[b], after])

    def split(self, src, hi, lo, after, free=()):
        high = self.act.put(lambda e: e.activation(hi, src, ACT.Copy), [after, free])
        low = self.dve.put(lambda e: e.tensor_tensor(lo, src, hi.bitcast(F32), ALU.subtract), [high, free])
        return [high, low]

    def transposes(self, pieces, after):
        b = self.banks.take()
        bank = self.banks.banks[b]
        for n, piece in enumerate(pieces):
            rows = piece.shape[0]
            width = int(np.prod(piece.shape[1:]))
            token = self.pe.put(
                lambda e, n=n, piece=piece, rows=rows, width=width: e.transpose(
                    bank[:width, n * P:n * P + rows], piece, self.ident[:rows, :rows]),
                [self.banks.free[b], after] if n == 0 else (), mark=n == len(pieces) - 1)
        return b, bank, token


    def inverse_root(self, dst, src, scale, eps, after):
        a = self.dve.put(lambda e: e.tensor_scalar(dst, src, scale, eps, ALU.mult, ALU.add), after)
        b = self.act.put(lambda e: e.activation(dst, dst, ACT.Sqrt), [a])
        return self.dve.put(lambda e: e.reciprocal(dst, dst), [b])

    def norm_steps(self, source, tiles, hi, lo, gain, shift, work, free, ready, done):
        normed = {}

        def rows_of(t):
            rows, src, col, loaded = source(t)
            i, x, xfree = work["x"].next()
            landed = self.load(x[:rows, :], src, [xfree, loaded], lane=self.sp)
            j, st, sfree = work["stat"].next()
            junk = work["junk"]
            sq = self.act.put(lambda e: e.activation(junk[:rows, :], x[:rows, :], ACT.Square,
                                                     accum_out=st[:rows, 0:1]), [landed, sfree, work["junk_free"]])
            work["junk_free"] = [sq]
            inv = self.inverse_root(st[:rows, 1:2], st[:rows, 0:1], 1.0 / D, RMS_EPS, [sq])
            scaled = self.dve.put(lambda e: e.tensor_scalar(x[:rows, :], x[:rows, :], st[:rows, 1:2], None, ALU.mult),
                                  [inv])
            work["stat"].free[j] = [scaled]
            work["x"].free[i] = None
            normed[t] = (rows, col, i, x, scaled)

        def turn(t, h):
            rows, col, i, x, scaled = normed[t]
            b, bank, turned = self.transposes([x[:rows, (4 * h + k) * P:(4 * h + k + 1) * P] for k in range(4)], [scaled])
            src4 = bank[:, :].rearrange("p (k t) -> p k t", k=4)[:, :, :rows]
            g4 = gain[:, 4 * h:4 * h + 4].unsqueeze(2).to_broadcast([P, 4, rows])
            y = self.dve.put(lambda e: e.tensor_tensor(src4, src4, g4, ALU.mult), [turned, ready])
            if shift is not None:
                s4 = shift[:, 4 * h:4 * h + 4].unsqueeze(2).to_broadcast([P, 4, rows])
                y = self.dve.put(lambda e: e.tensor_tensor(src4, src4, s4, ALU.add), [y])
            parts = self.split(src4, hi[:, 4 * h:4 * h + 4, col:col + rows], lo[:, 4 * h:4 * h + 4, col:col + rows],
                               [y], free)
            self.banks.release(b, parts)
            done.extend(parts)
            work["x"].free[i] = [turned]
        tiles = list(tiles)
        rows_of(tiles[0])
        yield
        for n, t in enumerate(tiles):
            if n + 1 < len(tiles):
                rows_of(tiles[n + 1])
            turn(t, 0)
            yield
            turn(t, 1)
            yield

    def norm_to_columns(self, source, tiles, hi, lo, gain, shift, work, free, ready=()):
        done = []
        for _ in self.norm_steps(source, tiles, hi, lo, gain, shift, work, free, ready, done):
            pass
        return done

    def row_work(self, free, x_buffers=2):
        return {"x": Ring([self.place(f"x{i}", [P, D]) for i in range(x_buffers)], free),
                "stat": Ring([self.place(f"stat{i}", [P, 3]) for i in range(2)], free),
                "junk": self.place("junk", [P, D]), "junk_free": list(flat(free))}


    def project_rows(self, name, x, k_all, x_ready, steps=1):
        out = {}
        for c in range(2):
            if c == 1:
                self.finish_background()
            held = [self.banks.take() for _ in range(4)]
            for k0 in range(0, k_all, 2):
                block = self.weights_take(name)
                _, whi, wlo, wready, _ = block
                for t in range(4):
                    tok = slice(t * P, (t + 1) * P)
                    bank = self.banks.banks[held[t]]
                    terms = []
                    for k in range(2):
                        terms += [(x[k0 + k][0][:, tok], whi[:, k, :]), (x[k0 + k][1][:, tok], whi[:, k, :]),
                                  (x[k0 + k][0][:, tok], wlo[:, k, :])]
                    for n, (a, w) in enumerate(terms):
                        first, last = k0 == 0 and n == 0, k0 == k_all - 2 and n == len(terms) - 1
                        token = self.pe.put(
                            lambda e, a=a, w=w, f=first, g=last, bank=bank: e.matmul(
                                bank[:, :], a, w, start=f, stop=g),
                            [wready, x_ready, self.banks.free[held[t]] if k0 == 0 else ()] if n == 0 else (),
                            mark=n == len(terms) - 1)
                    if k0 == k_all - 2:
                        out[(t, c)] = (held[t], token)
                self.weights_done(block, token)
                self.prefetch()
                if c == 0:
                    self.pump(steps)
        return out

    def add_residual(self, banks, source, target, gain, work, row_ready):
        stored = []
        for t in range(4):
            (b0, y0), (b1, y1) = banks[(t, 0)], banks[(t, 1)]
            bank0, bank1 = self.banks.banks[b0], self.banks.banks[b1]
            src, loaded = source(t)
            i, x, xfree = work["x"].next()
            landed = self.load(x[:, :], src, [xfree, loaded])
            j, st, sfree = work["stat"].next()
            junk = work["junk"]
            s0 = self.act.put(lambda e, b=bank0, st=st: e.activation(junk[:, :HALF], b[:, :], ACT.Square,
                                                                     accum_out=st[:, 0:1]),
                              [y0, sfree, work["junk_free"]])
            s1 = self.act.put(lambda e, b=bank1, st=st: e.activation(junk[:, HALF:], b[:, :], ACT.Square,
                                                                     accum_out=st[:, 1:2]), [y1, work["junk_free"]])
            work["junk_free"] = [s1]
            both = self.dve.put(lambda e, st=st: e.tensor_tensor(st[:, 0:1], st[:, 0:1], st[:, 1:2], ALU.add), [s0, s1])
            inv = self.inverse_root(st[:, 2:3], st[:, 0:1], 1.0 / D, RMS_EPS, [both])
            for c, (b, bank) in enumerate(((b0, bank0), (b1, bank1))):
                cols = slice(c * HALF, (c + 1) * HALF)
                scaled = self.dve.put(lambda e, bank=bank, st=st, cols=cols: e.scalar_tensor_tensor(
                    bank[:, :], bank[:, :], st[:, 2:3], gain[:, cols], ALU.mult, ALU.mult), [inv, row_ready])
                added = self.dve.put(lambda e, x=x, bank=bank, cols=cols: e.tensor_tensor(
                    x[:, cols], x[:, cols], bank[:, :], ALU.add), [scaled, landed])
                self.banks.release(b, [added])
            work["stat"].free[j] = [added]
            out = self.store(target(t), x[:, :], [added])
            work["x"].free[i] = [out]
            stored.append(out)
        return stored


    def setup(self):
        a, nc = self.arg, self.nc
        self.ident = self.place("ident", [P, P])
        self.mean = self.place("mean", [P, P])
        ident_ready = self.load(self.ident[:, :], a["k_ident"])
        self.mean_ready = self.pool.put(lambda e: e.memset(self.mean[:, :], 1.0 / D))
        sources = [[a["b_glu"], a["b_dw"], a["g_conv_ln"], a["b_conv_ln"], a["b_conv_out"],
                    a["pool_scale_2"], a["c_2"], a["b_mod_2"]],
                   [a["w_dw"][0, 0:15, :]], [a["w_dw"][0, 15:31, :]], [a["conv_qkv_2"][0],
                   a["g_pre_mix"], a["g_pre_ffn"], a["g_pre_mix_2"], a["g_pre_ffn_2"]]]
        self.vec = self.place("vec", [P, 4, P])
        self.mod = self.place("mod", [P, 6 * KD, 2])
        self.context = self.place("context", [P, KD, 2])
        self.gate_in = self.place("gate_in", [P, NT + CT, 16])
        self.beta = self.place("beta", [P, NT + CT, 8])
        self.decay = self.place("decay", [P, NT + CT, 8])
        self.mix_gain, self.ffn_gain = self.place("mix_gain", [P, 2, KD]), self.place("ffn_gain", [P, 1, KD])
        self.ffn_taps = self.place("ffn_taps", [P, 3, KF])
        floor = self.cursor
        rows = self.place("vec_rows", [P, 4, P])
        tap_rows = self.place("ffn_tap_rows", [3 * KF, P])
        counts = []
        for n, group in enumerate(sources):
            r = 0
            landed = []
            for src in group:
                flat_src = src.rearrange("a (j p) -> (a j) p", p=P)
                m = flat_src.shape[0]
                landed.append(self.load(rows[r:r + m, n, :], flat_src))
                counts.append((n, r, m))
                r += m
            if n == 0:
                c_ctx = a["c_ctx_2"].rearrange("(j p) -> j p", p=P)
                landed.append(self.load(rows[r:r + 8, n, :], c_ctx))
                counts.append((n, r, 8))
                r += 8
            b, bank, turned = self.transposes([rows[:r, n, :]], [landed, ident_ready])
            copied = self.dve.put(lambda e, bank=bank, n=n, r=r: e.tensor_copy(self.vec[:, n, :r], bank[:, :r]), [turned])
            self.banks.release(b, [copied])
            self.vec_ready = [copied]
        landed = self.load(tap_rows[:, :], a["conv_ffn_2"][0].rearrange("w (j p) -> (w j) p", p=P))
        b, bank, turned = self.transposes([tap_rows[:, :]], [landed])
        copied = self.dve.put(lambda e, bank=bank: e.tensor_copy(
            self.ffn_taps[:, :, :].rearrange("p w j -> p (w j)"), bank[:, :3 * KF]), [turned])
        self.banks.release(b, [copied])
        self.vec_ready = [copied]
        self.v_b_glu, self.v_b_dw, self.v_g_ln, self.v_b_ln, self.v_b_co, self.v_pool, self.v_c, self.v_b_mod, \
            self.v_c_ctx = (self.vec[:, 0, r:r + m] for _, r, m in counts[:9])
        self.v_g_pre_mix, self.v_g_pre_ffn, self.v_g_pre_mix_2, self.v_g_pre_ffn_2 = (
            self.vec[:, 3, CONV5 * 12 + n * KD:CONV5 * 12 + (n + 1) * KD] for n in range(4))
        self.act.put(lambda e: e.activation(self.context[:, :, 0], self.v_c, ACT.Silu), [self.vec_ready])
        self.context_ready = self.act.put(lambda e: e.activation(self.context[:, :, 1], self.v_c_ctx, ACT.Silu))
        self.mods, self.mod_ready = 0, []
        self.cursor = floor
        return ident_ready

    def dw_tap(self, chunk, tap):
        n, t = (1, tap) if tap < 15 else (2, tap - 15)
        return self.vec[:, n, t * KD + chunk:t * KD + chunk + 1]

    def row_load(self, name, src, after):
        row = self.place(name, [P, src.shape[-1]])
        return row, self.load(row[:, :], broadcast(src, src.shape[-1]), after, lane=self.sp)


    def first_mix_projections(self, free):
        a, s = self.arg, self.scratch
        hi, lo = self.place("h_hi", [P, KD, S], F32R), self.place("h_lo", [P, KD, S], F32R)
        floor = self.cursor
        work = self.row_work(free, 4)
        h_ready = self.norm_to_columns(lambda t: (P, a["x"][0, t * P:(t + 1) * P, :], t * P, ()), range(NT), hi, lo,
                                       self.v_g_pre_mix, None, work, free, self.vec_ready)
        norm_done = [x.last() for x in (self.pe, self.act, self.dve)]
        self.phase += 1
        self.cursor = floor
        free = norm_done
        setup = self.attention_setup(free)
        next(setup)
        self.conv_setup(free)
        stage = Ring([self.place(f"stage{i}", [P, HALF]) for i in range(3)], free)
        v_sb = self.place("v", [P, NT, NH, HD + 1])
        ones = self.pool.put(lambda e: e.memset(v_sb[:, :, :, HD:HD + 1], 1.0), free)
        qk = Ring([(self.place(f"q{i}", [P, S]), self.place(f"k{i}", [P, S])) for i in range(2)], free)
        self.v_free = list(free)
        attention, convolution = [], []
        self.streams = [attention, convolution]
        self.gates_stored, self.conv_stored, self.u_stored = [], [], []
        h = (hi, lo)

        def glu(j):
            i, (up, acc), cfree = self.next_slot(self.conv_ring)
            gate = self.weights_take("glu_gate")
            main = self.weights_take("glu_u")
            landed = []
            for n in range(2):
                sl = slice(n * HALF, (n + 1) * HALF)
                b, y, done = self.into_bank([P, HALF], self.column_terms(gate, h, KD, sl), [gate[3], h_ready])
                k, sg, sfree = self.sig_ring.next()
                sig = self.act.put(lambda e, y=y, sg=sg: e.activation(
                    sg[:, :], y, ACT.Sigmoid, bias=self.v_b_glu[:, KD + j:KD + j + 1]), [done, sfree, self.vec_ready])
                self.banks.release(b, [sig])
                if n:
                    self.weights_done(gate, done)
                b, y, done = self.into_bank([P, HALF], self.column_terms(main, h, KD, sl), [main[3]])
                put = self.dve.put(lambda e, y=y, sg=sg, n=n, up=up: e.scalar_tensor_tensor(
                    up[:, TAPS - 1 + n * HALF:TAPS - 1 + (n + 1) * HALF], y, self.v_b_glu[:, j:j + 1], sg[:, :],
                    ALU.add, ALU.mult), [done, sig, cfree])
                self.banks.release(b, [put])
                self.sig_ring.free[k] = [put]
                landed.append(put)
                if n:
                    self.weights_done(main, done)
                self.prefetch()
                self.pump(2)
            self.conv_ring.free[i] = None
            convolution.append(self.convolve(j, i, up, acc, landed))

        def gates(name, slot, j):
            block = self.weights_take(name)
            for n in range(2):
                b, y, done = self.into_bank([P, HALF], self.column_terms(block, h, KD, slice(n * HALF, (n + 1) * HALF)),
                                            [block[3], h_ready])
                i, st, sfree = stage.next()
                sig = self.act.put(lambda e, y=y, st=st: e.activation(st[:, :], y, ACT.Sigmoid), [done, sfree])
                self.banks.release(b, [sig])
                out = self.store(s["gates"][slot, j, :, n * HALF:(n + 1) * HALF], st[:, :], [sig])
                stage.free[i] = [out]
                self.gates_stored.append(out)
                if n:
                    self.weights_done(block, done)
                self.prefetch()
                self.pump(2)

        attention.append(setup)
        glu(0)
        glu(1)
        for g in range(NG):
            blocks = [self.weights_take("v") for _ in range(4)]
            landed = []
            for t in range(NT):
                terms = []
                for k in range(KD):
                    _, whi, wlo, _, _ = blocks[k // 2]
                    xs = [group_tokens(x, k, g, t) for x in (hi, lo)]
                    terms += [(xs[0], whi[:, k % 2, :]), (xs[1], whi[:, k % 2, :]), (xs[0], wlo[:, k % 2, :])]
                b, y, done = self.into_bank([P, HALF], terms, [[x[3] for x in blocks], h_ready])
                dst = v_sb[:, t, :, 0:HD]
                src = y.rearrange("p (h d) -> p h d", h=NH)
                if t % 2:
                    put = self.act.put(lambda e, dst=dst, src=src: e.activation(dst, src, ACT.Copy), [done, self.v_free])
                else:
                    put = self.dve.put(lambda e, dst=dst, src=src: e.tensor_copy(dst, src), [done, self.v_free])
                self.banks.release(b, [put])
                landed.append(put)
                if t >= NT - 1:
                    for x in blocks:
                        self.weights_done(x, done)
                self.pump()
            self.prefetch()
            v_ready = [landed, ones]
            for pair in range(NH // 2):
                i, (q, k), qfree = self.next_slot(qk)
                ready = []
                for name, dst, scale in (("q", q, HD ** -0.5), ("k", k, 1.0)):
                    block = self.weights_take(name)
                    for n in range(2):
                        b, y, done = self.into_bank([P, HALF],
                                                    self.column_terms(block, h, KD, slice(n * HALF, (n + 1) * HALF)),
                                                    [block[3], h_ready])
                        dv, sv = class_order(dst, y, g, n)
                        put = self.act.put(lambda e, dv=dv, sv=sv, scale=scale: e.activation(
                            dv, sv, ACT.Copy, scale=scale), [done, qfree])
                        self.banks.release(b, [put])
                        ready.append(put)
                        if n:
                            self.weights_done(block, done)
                        self.prefetch()
                        self.pump(2)
                qk.free[i] = None
                attention.append(self.attend(g, pair, q, k, v_sb, [ready, v_ready], (qk, i)))
                if pair % 2:
                    glu(2 + 2 * g + pair // 2)
                for name, slot, j in gates_behind(g, pair):
                    gates(name, slot, j)
            while attention:
                self.pump()
            self.v_free = [self.pe.last()]
        gates(*GATES[-1])
        self.finish_background()

    def column_terms(self, block, x, k_all, sl):
        _, whi, wlo, _, _ = block
        terms = []
        for k in range(k_all):
            terms += [(whi[:, k, :], x[0][:, k, sl]), (whi[:, k, :], x[1][:, k, sl]), (wlo[:, k, :], x[0][:, k, sl])]
        return terms


    def conv_setup(self, free):
        self.conv_ring = Ring([(self.place(f"u{i}", [P, TAPS - 1 + S]), self.place(f"conv{i}", [P, S]))
                               for i in range(2)], free)
        self.sig_ring = Ring([self.place(f"sig{i}", [P, HALF]) for i in range(2)], free)
        for i, (up, _) in enumerate(self.conv_ring.slots):
            zero = self.dve.put(lambda e, up=up: e.memset(up[:, 0:TAPS - 1], 0.0), free)
            self.conv_ring.free[i] = [zero]

    def convolve(self, j, i, up, acc, ready):
        token = self.dve.put(lambda e: e.tensor_scalar(acc[:, :], up[:, 0:S], self.dw_tap(j, 0),
                                                       self.v_b_dw[:, j:j + 1], ALU.mult, ALU.add), ready)
        for tap in range(1, TAPS):
            token = self.dve.put(lambda e, tap=tap: e.scalar_tensor_tensor(
                acc[:, :], up[:, tap:tap + S], self.dw_tap(j, tap), acc[:, :], ALU.mult, ALU.add), [token])
            if tap % 3 == 2:
                yield
        out = self.store(self.scratch["conv"][j], acc[:, :], [token])
        self.conv_ring.free[i] = [out, token]
        self.conv_stored.append(out)


    def attention_setup(self, free):
        a, s = self.arg, self.scratch
        table = self.place("table", [BUCKETS, NG * NH])
        self.bias = Ring([self.place(f"bias{i}", [P, 2, 2 * P]) for i in range(2)], free)
        self.scores = Ring([self.place(f"scores{i}", [P, 2, 2 * P]) for i in range(3)], free)
        self.turned = Ring([self.place(f"turned{i}", [P, 2, 2, P]) for i in range(2)], free)
        self.u_ring = Ring([self.place(f"uo{i}", [P, NT, 2, HD + 2]) for i in range(2)], free)
        self.stats = Ring([self.place(f"astat{i}", [P, 4]) for i in range(6)], free)
        onehot = self.bias.slots[0][0:BUCKETS, :, :].rearrange("p a b -> p (a b)")[:, 0:TOEP]
        vec = self.scores.slots[0][0:NG * NH, :, :].rearrange("p a b -> p (a b)")[:, 0:TOEP]
        invalid = self.scores.slots[1][0:NG * NH, :, :].rearrange("p a b -> p (a b)")[:, 0:TOEP]
        yield
        landed = self.load(table[:, :], a["rel_bias_table"], free)
        stored = []
        for g in range(NG):
            hot = self.load(onehot, a["k_onehot"][:, g * TOEP:(g + 1) * TOEP], [free, self.pe.last()])
            bad = self.load(invalid, bass.AP(tensor=a["k_invalid"].tensor, offset=g * TOEP,
                                             ap=[[0, NG * NH], [1, TOEP]]), [free, self.dve.last()])
            b, y, done = self.into_bank([NG * NH, TOEP], [(table[:, :], onehot)], [landed, hot])
            add = self.dve.put(lambda e, y=y: e.tensor_tensor(vec, y, invalid, ALU.add), [done, bad, stored])
            self.banks.release(b, [add])
            own = slice(g * NH, (g + 1) * NH)
            stored.append(self.store(s["toeplitz"][own, :].rearrange("h (r j) -> h r j", j=TOEP),
                                     vec[own, :].unsqueeze(1).to_broadcast([NH, P, TOEP]), [add]))
            yield
        self.toeplitz_stored = stored
        self.bias.free[0] = [done]
        self.scores.free = [[stored], [add], list(free)]

    def attend(self, g, pair, q, k, v_sb, ready, qk_slot):
        s = self.scratch
        ib, bias, bfree = self.bias.next()
        iu, u, ufree = self.u_ring.next()
        toep = s["toeplitz"]
        landed = []
        start, width = (127, 2 * P) if g < 2 else (127 + P, P)
        for h in range(2):
            base = toep[g * NH + 2 * pair + h:g * NH + 2 * pair + h + 1, 0:1]
            landed.append(self.load(bias[:, h, 0:width], shifted(base, start, P, width),
                                    [bfree, self.toeplitz_stored]))
        yield
        state = {}

        def score(t):
            nk = 2 if (g == 0 and t > 0) or (g == 1 and t % 2) else 1
            k0 = (t + 1 - nk) * P
            off = (2 - nk) * P if g < 2 else 0
            i, sc, sfree = self.scores.next()
            m, st, mfree = self.stats.next()
            for h in range(2):
                rows = slice(h * HD, (h + 1) * HD)
                b = self.banks.take()
                bank = self.banks.banks[b]
                token = self.pe.put(lambda e, rows=rows, bank=bank: e.matmul(
                    bank[:, 0:nk * P], q[rows, t * P:(t + 1) * P], k[rows, k0:k0 + nk * P],
                    start=True, stop=True), [self.banks.free[b], ready])
                token2 = self.dve.put(lambda e, h=h, bank=bank: e.tensor_tensor_reduce(
                    sc[:, h, 0:nk * P], bank[:, 0:nk * P], bias[:, h, off:off + nk * P],
                    1.0, -3e38, ALU.add, ALU.max, st[:, h:h + 1]), [token, sfree, mfree, landed])
                self.banks.release(b, [token2])
            neg = self.dve.put(lambda e: e.tensor_scalar(st[:, 2:4], st[:, 0:2], -1.0, None, ALU.mult), [token2])
            keep = self.dve.put(lambda e: e.tensor_copy(u[:, t, :, HD + 1:HD + 2].rearrange("p h a -> p (h a)"),
                                                        st[:, 0:2]), [token2, ufree])
            for h in range(2):
                exp = self.act.put(lambda e, h=h: e.activation(sc[:, h, 0:nk * P], sc[:, h, 0:nk * P], ACT.Exp,
                                                               bias=st[:, 2 + h:3 + h]), [neg])
            self.stats.free[m] = [exp, keep]
            state[t] = [nk, i, sc, exp, keep]

        def turn(t):
            nk, i, sc, exp, keep = state[t]
            b, bank, token = self.transposes([sc[:, h, n * P:(n + 1) * P] for h in range(2) for n in range(nk)], [exp])
            self.scores.free[i] = [token]
            j, pt, pfree = self.turned.next()
            src = bank[:, 0:2 * nk * P].rearrange("p (h n q) -> p h n q", h=2, n=nk)
            put = self.act.put(lambda e: e.activation(pt[:, :, 0:nk, :], src, ACT.Copy), [token, pfree])
            self.banks.release(b, [put])
            state[t] += [j, pt, put]

        def weigh(t):
            nk, _, _, _, keep, j, pt, put = state[t]
            b = self.banks.take()
            bank = self.banks.banks[b]
            for h in range(2):
                for n in range(nk):
                    kt = t + 1 - nk + n
                    token = self.pe.put(lambda e, h=h, n=n, kt=kt: e.matmul(
                        bank[:, h * (HD + 1):(h + 1) * (HD + 1)], pt[:, h, n, :], v_sb[:, kt, 2 * pair + h, :],
                        start=n == 0, stop=n == nk - 1), [self.banks.free[b], put] if h + n == 0 else (),
                        mark=h == 1 and n == nk - 1)
            self.turned.free[j] = [token]
            out = self.dve.put(lambda e: e.tensor_copy(
                u[:, t, :, 0:HD + 1], bank[:, 0:2 * (HD + 1)].rearrange("p (h d) -> p h d", h=2)), [token, ufree])
            self.banks.release(b, [out])
            return [out, keep]

        done = []
        for t in range(NT + 3):
            if t < NT:
                score(t)
            if 2 <= t < NT + 2:
                turn(t - 2)
            if t >= 3:
                done += weigh(t - 3)
            yield
        ring, slot = qk_slot
        ring.free[slot] = [self.pe.last()]
        self.bias.free[ib] = [self.dve.last()]
        out = []
        for dst, src in unit_stores(s["sums"][g], u, g, pair):
            out.append(self.store(dst, src, done))
        self.u_ring.free[iu] = out
        self.u_stored += out



    def first_mix_outputs(self, free):
        a, s = self.arg, self.scratch
        self.before_half = self.cursor
        self.post = gain = self.place("post", [P, D])
        self.work = work = self.row_work(free)
        self.work_size = self.cursor - self.before_half
        self.half = u = (self.place("half_hi", [P, KD, HALF + 2], F32R), self.place("half_lo", [P, KD, HALF + 2], F32R))
        self.after_half = end = self.cursor
        self.cursor = end - KD * (HALF + 2) * 4
        conv = self.place("conv", [P, KD, HALF + 2])
        assert self.cursor == end
        gain_ready = self.load(gain[:, :], broadcast(a["g_post_mix"], D), free)
        oT = [(self.place(f"oT{h}_hi", [P, 4, HALF], F32R), self.place(f"oT{h}_lo", [P, 4, HALF], F32R)) for h in range(2)]
        merged = (self.place("m_hi", [P, KD, HALF], F32R), self.place("m_lo", [P, KD, HALF], F32R))
        sums = self.place("sums", [P, NG, NH, HD + 2])
        msum = self.place("msum", [P, 2, NG, NH])
        o = self.place("o", [P, HALF])
        square = Ring([self.place(f"square{i}", [P, HALF]) for i in range(2)], free)
        mu, rs = self.place("mu", [P, HALF]), self.place("rs", [P, HALF])
        gates = Ring([self.place(f"sg{i}", [P, 2, HALF]) for i in range(2)], free)
        stored = []
        top, e, total = msum[:, 0, 0, :], msum[:, 1, :, :], msum[:, 0, :, :]
        mx = sums[:, :, :, HD + 1]
        o3 = o[:, :].rearrange("p (h d) -> p h d", h=NH)
        merge_free = [list(free), list(free)]

        def merge(half, ready):
            hi, lo = oT[half]
            for t in range(4):
                sums_free, o_free = merge_free
                tok = slice(half * HALF + t * P, half * HALF + (t + 1) * P)
                landed = [self.load(sums[:, g, :, :], s["sums"][g, tok, :].rearrange("p (h w) -> p h w", h=NH),
                                    [sums_free, self.u_stored], lane=self.sp) for g in range(NG)]
                x = self.dve.put(lambda v: v.tensor_tensor(top, mx[:, 0, :], mx[:, 1, :], ALU.max), [landed, sums_free])
                x = self.dve.put(lambda v: v.tensor_tensor(top, top, mx[:, 2, :], ALU.max), [x])
                y = self.dve.put(lambda v: v.tensor_tensor(e, mx, top.unsqueeze(1).to_broadcast([P, NG, NH]),
                                                           ALU.subtract), [x])
                x = self.act.put(lambda v: v.activation(e, e, ACT.Exp), [y])
                yield
                x = self.dve.put(lambda v: v.tensor_tensor(total, e, sums[:, :, :, HD], ALU.mult), [x, y])
                x = self.dve.put(lambda v: v.tensor_tensor(total[:, 0, :], total[:, 0, :], total[:, 1, :], ALU.add), [x])
                x = self.dve.put(lambda v: v.tensor_tensor(total[:, 0, :], total[:, 0, :], total[:, 2, :], ALU.add), [x])
                x = self.dve.put(lambda v: v.reciprocal(total[:, 0, :], total[:, 0, :]), [x])
                y = self.dve.put(lambda v: v.tensor_tensor(
                    e, e, total[:, 0, :].unsqueeze(1).to_broadcast([P, NG, NH]), ALU.mult), [x])
                for g in range(NG):
                    part = sums[:, g, :, 0:HD]
                    weight = e[:, g, :].unsqueeze(2).to_broadcast([P, NH, HD])
                    z = self.dve.put(lambda v, part=part, weight=weight: v.tensor_tensor(part, part, weight, ALU.mult), [y])
                x = self.dve.put(lambda v: v.tensor_tensor(o3, sums[:, 0, :, 0:HD], sums[:, 1, :, 0:HD], ALU.add), [z, o_free])
                x = self.dve.put(lambda v: v.tensor_tensor(o3, o3, sums[:, 2, :, 0:HD], ALU.add), [x])
                sums_free = [x]
                yield
                b, bank, turned = self.transposes([o[:, k * P:(k + 1) * P] for k in range(4)], [x])
                merge_free[:] = [sums_free, [turned]]
                dst = slice(t * P, (t + 1) * P)
                parts = self.split(bank[:, :].rearrange("p (k t) -> p k t", k=4), hi[:, :, dst], lo[:, :, dst],
                                   [turned], free)
                self.banks.release(b, parts)
                ready += parts
            yield

        def conv_norm(half, u_free, ready):
            landed = self.load(conv[:, :, 0:HALF], s["conv"].rearrange("j p t -> p j t")[:, :, half * HALF:(half + 1) * HALF],
                               [u_free, self.conv_stored], lane=self.sp)
            yield
            b, y, done = self.into_bank([P, HALF], [(self.mean[:, :], conv[:, k, 0:HALF]) for k in range(KD)],
                                        [landed, self.mean_ready])
            x = self.act.put(lambda v: v.activation(mu[:, :], y, ACT.Copy), [done, u_free])
            self.banks.release(b, [x])
            yield
            b = self.banks.take()
            bank = self.banks.banks[b]
            for k in range(KD):
                c = self.dve.put(lambda v, k=k: v.tensor_tensor(conv[:, k, 0:HALF], conv[:, k, 0:HALF], mu[:, :], ALU.subtract), [x])
                i, sq, sqfree = square.next()
                q = self.act.put(lambda v, k=k, sq=sq: v.activation(sq[:, :], conv[:, k, 0:HALF], ACT.Square), [c, sqfree])
                done = self.pe.put(lambda v, k=k, sq=sq: v.matmul(bank[:, :], self.mean[:, :], sq[:, :], start=k == 0,
                                                                  stop=k == KD - 1), [q, self.banks.free[b] if k == 0 else ()])
                square.free[i] = [done]
                if k % 4 == 3:
                    yield
            x = self.dve.put(lambda v: v.tensor_scalar(rs[:, :], bank[:, :], LN_EPS, None, ALU.add), [done, u_free])
            self.banks.release(b, [x])
            x = self.act.put(lambda v: v.activation(rs[:, :], rs[:, :], ACT.Sqrt), [x])
            x = self.dve.put(lambda v: v.reciprocal(rs[:, :], rs[:, :]), [x])
            for k in range(KD):
                scaled = self.dve.put(lambda v, k=k: v.tensor_tensor(conv[:, k, 0:HALF], conv[:, k, 0:HALF], rs[:, :], ALU.mult), [x])
                act = self.act.put(lambda v, k=k: v.activation(
                    conv[:, k, 0:HALF], conv[:, k, 0:HALF], ACT.Silu, bias=self.v_b_ln[:, k:k + 1], scale=self.v_g_ln[:, k:k + 1]),
                    [scaled])
                ready += self.split(conv[:, k, 0:HALF], u[0][:, k, 0:HALF], u[1][:, k, 0:HALF], [act], u_free)
                if k % 2:
                    yield

        oT_ready, u_ready = [[], []], [[], []]
        self.streams = [[conv_norm(0, free, u_ready[0])], [merge(0, oT_ready[0])]]
        self.finish_background()
        self.streams = [[merge(1, oT_ready[1])]]
        m_free = list(free)
        self.next_ready = []
        for half in range(2):
            m_ready = []
            for j in range(KD):
                i, sg, gfree = gates.next()
                cols = slice(half * HALF, (half + 1) * HALF)
                landed = [self.load(sg[:, n, :], s["gates"][n, j, :, cols], [gfree, self.gates_stored], lane=self.sp)
                          for n in range(2)]
                block = self.weights_take("conv_out")
                b1, y1, done1 = self.into_bank([P, HALF], self.column_terms(block, u, KD, slice(0, HALF)),
                                               [block[3], u_ready[half]])
                self.pump()
                self.weights_done(block, done1)
                block = self.weights_take("attn_out")
                b2, y2, done2 = self.into_bank([P, HALF], self.column_terms(block, oT[half], 4, slice(0, HALF)),
                                               [block[3], oT_ready[half]])
                self.pump()
                self.weights_done(block, done2)
                x = self.dve.put(lambda v, y1=y1, sg=sg, j=j: v.scalar_tensor_tensor(
                    sg[:, 1, :], y1, self.v_b_co[:, j:j + 1], sg[:, 1, :], ALU.add, ALU.mult), [done1, landed])
                self.banks.release(b1, [x])
                z = self.dve.put(lambda v, y2=y2, sg=sg: v.tensor_tensor(sg[:, 0, :], y2, sg[:, 0, :], ALU.mult), [done2])
                self.banks.release(b2, [z])
                x = self.dve.put(lambda v, sg=sg: v.tensor_tensor(sg[:, 0, :], sg[:, 0, :], sg[:, 1, :], ALU.add), [x, z])
                parts = self.split(sg[:, 0, :], merged[0][:, j, :], merged[1][:, j, :], [x], m_free)
                gates.free[i] = parts
                m_ready += parts
                self.prefetch()
                self.modulate()
            self.finish_background()
            if half == 0:
                self.streams = [[conv_norm(1, [done1, self.act.last(), self.dve.last()], u_ready[1])]]
            else:
                self.streams = [[self.norm_steps(
                    lambda t: (P, s["x1"][t * P:(t + 1) * P, :], t * P, stored[t]), range(4), u[0], u[1],
                    self.v_g_pre_ffn, None, work, [done1], self.vec_ready, self.next_ready)]]
            banks = self.project_rows("mix_out", chunks(merged, KD), KD, m_ready, steps=3)
            m_free = [banks[(3, 1)][1]]
            stored += self.add_residual(
                banks, lambda t, half=half: (a["x"][0, half * HALF + t * P:half * HALF + (t + 1) * P, :], ()),
                lambda t, half=half: s["x1"][half * HALF + t * P:half * HALF + (t + 1) * P, :], gain, work, gain_ready)
        return stored


    def feed_forward(self, free, source, target, gain, shift, gain_ready, post_ready, conv_gate, names, spare=(), then=None):
        (hi, lo), post, work = self.half, self.post, self.work
        hidden = []
        if spare:
            at, self.cursor = self.cursor, spare[0]
            while self.cursor + 4 * HALF * 2 <= spare[1]:
                j = len(hidden)
                hidden.append((self.place(f"a{j}_hi", [P, HALF], F32R), self.place(f"a{j}_lo", [P, HALF], F32R)))
            self.cursor = at
        edge = self.place("edge", [P, KF]) if conv_gate else None
        beside = self.place("beside", [P, KD, 4], F32R) if conv_gate else None
        gbuf = Ring([self.place(f"g{i}", [P, HALF + 2]) for i in range(2)], free)
        tmp = Ring([self.place(f"t{i}", [P, HALF]) for i in range(2)], free)
        for j in range(len(hidden), KF):
            hidden.append((self.place(f"a{j}_hi", [P, HALF], F32R), self.place(f"a{j}_lo", [P, HALF], F32R)))
        stored, edge_ready = [], []
        a_free = list(free)
        taps_ready = self.vec_ready

        def tile(t):
            src, loaded = source(t * P, P)
            return P, src, t * P - HALF, loaded

        def halo_tile(t):
            src, loaded = source(HALF, 2)
            return 2, src, 0, loaded
        h_ready = self.next_ready
        for half in range(2):
            a_ready = []
            for j in range(KF):
                gate = self.weights_take(names[0])
                b, y, done = self.into_bank([P, HALF], self.column_terms(gate, (hi, lo), KD, slice(0, HALF)),
                                            [gate[3], h_ready])
                up = self.weights_take(names[1])
                b_up, y_up, done_up = self.into_bank([P, HALF], self.column_terms(up, (hi, lo), KD, slice(0, HALF)), [up[3]])
                self.weights_done(up, done_up)
                if conv_gate and half == 0 and j == 0:
                    side_ready = self.norm_to_columns(halo_tile, [0], beside[:, :, 0:2], beside[:, :, 2:4], gain, shift,
                                                      work, free, gain_ready)
                i, g, gfree = gbuf.next()
                n, f, ffree = tmp.next()
                if conv_gate:
                    taps = conv_gate(j)
                    put = self.act.put(lambda e, y=y, g=g: e.activation(g[:, 1:HALF + 1], y, ACT.Copy), [done, gfree])
                    self.banks.release(b, [put])
                    if half == 0:
                        terms = [(gate[part][:, k, :], beside[:, k, :]) for k in range(KD) for part in (1, 2)]
                        b, y, done = self.into_bank([P, 4], terms, [side_ready])
                        zero = self.dve.put(lambda e, g=g: e.memset(g[:, 0:1], 0.0), [gfree])
                        side = self.dve.put(lambda e, g=g, y=y: e.tensor_reduce(g[:, HALF + 1:HALF + 2], y[:, 0:4:2],
                                                                                AX.X, ALU.add), [done, gfree])
                        self.banks.release(b, [side])
                        keep = self.dve.put(lambda e, g=g, j=j: e.tensor_copy(edge[:, j:j + 1], g[:, HALF:HALF + 1]),
                                            [put, free])
                        edge_ready.append(keep)
                        sides = [zero, side, keep]
                    else:
                        zero = self.dve.put(lambda e, g=g: e.memset(g[:, HALF + 1:HALF + 2], 0.0), [gfree])
                        side = self.dve.put(lambda e, g=g, j=j: e.tensor_copy(g[:, 0:1], edge[:, j:j + 1]), [gfree, edge_ready])
                        sides = [zero, side]
                    x = self.dve.put(lambda e, f=f, g=g, taps=taps: e.tensor_scalar(
                        f[:, :], g[:, 0:HALF], taps[0], None, ALU.mult), [put, sides, ffree, taps_ready])
                    for q in (1, 2):
                        x = self.dve.put(lambda e, f=f, g=g, q=q, taps=taps: e.scalar_tensor_tensor(
                            f[:, :], g[:, q:q + HALF], taps[q], f[:, :], ALU.mult, ALU.add), [x])
                    silu = self.act.put(lambda e, f=f, g=g: e.activation(g[:, 0:HALF], f[:, :], ACT.Silu), [x])
                else:
                    silu = self.act.put(lambda e, y=y, g=g: e.activation(g[:, 0:HALF], y, ACT.Silu), [done, gfree])
                    self.banks.release(b, [silu])
                self.weights_done(gate, done)
                self.prefetch()
                mul = self.dve.put(lambda e, y=y_up, f=f, g=g: e.tensor_tensor(f[:, :], g[:, 0:HALF], y, ALU.mult),
                                   [silu, done_up, ffree])
                self.banks.release(b_up, [mul])
                gbuf.free[i] = [mul]
                parts = self.split(f[:, :], hidden[j][0][:, :], hidden[j][1][:, :], [mul], a_free)
                tmp.free[n] = parts
                a_ready += parts
                self.prefetch()
                self.modulate()
            if half == 0:
                h_ready = []
                self.streams = [[self.norm_steps(tile, range(4, 8), hi, lo, gain, shift, work, [done_up], gain_ready, h_ready)]]
            elif then:
                self.streams = [[then([done_up], stored)]]
            banks = self.project_rows(names[2], hidden, KF, a_ready)
            a_free = [banks[(3, 1)][1]]
            stored += self.add_residual(
                banks, lambda t, half=half: source(half * HALF + t * P, P),
                lambda t, half=half: target(half * HALF + t * P), post, work, post_ready)
        return stored


    def second_block(self, floor, x2):
        a, s = self.arg, self.scratch
        self.cursor = self.after_half
        free = self.begin_phase(self.after_half)
        self.second_projections(free, x2)
        free = self.begin_phase(floor)
        o_sb = self.delta_rule(free)
        after_o = self.cursor
        free = self.begin_phase(after_o)
        self.second_mix_outputs(free, o_sb, x2)
        x3 = self.x3_stored
        free = self.begin_phase(self.after_half)
        self.feed_forward(free, lambda r, n: (s["x3"][r:r + n, :], x3[r // P]), lambda r: self.out[0, r:r + P, :],
                          self.ffn_gain[:, 0, :], self.mod[:, 3 * KD:4 * KD, 0], self.ffn_gain_ready,
                          self.post_ready, lambda j: [self.ffn_taps[:, n, j:j + 1] for n in range(3)],
                          ("up_gate", "up", "down"), spare=(floor, after_o))

    def modulate(self):
        if self.taken == len(self.plan) or self.plan[self.taken][0] != "mod":
            return
        j = self.mods
        self.mods += 1
        block = self.weights_take("mod")
        b, y, done = self.into_bank([P, 2], [(block[1][:, k, :], self.context[:, k, :]) for k in range(KD)],
                                    [block[3], self.context_ready])
        self.weights_done(block, done)
        put = self.dve.put(lambda e: e.tensor_tensor(
            self.mod[:, j, :], y, self.v_b_mod[:, j:j + 1].to_broadcast([P, 2]), ALU.add), [done])
        self.banks.release(b, [put])
        self.mod_ready = [put]

    def modulated_gain(self, col, gain, index, n):
        for m in range(n):
            put = self.dve.put(lambda e, m=m: e.scalar_tensor_tensor(
                col[:, m, :], self.mod[:, index * KD:(index + 1) * KD, m], 1.0, gain, ALU.add, ALU.mult),
                [self.mod_ready])
        return put

    def modulated_row(self, row, spread, gain, index, free):
        g_ready = self.load(row[:, :], broadcast(gain, D), free)
        x = self.dve.put(lambda e: e.tensor_copy(
            spread[:, :, :], self.mod[:, index * KD:(index + 1) * KD, 0].unsqueeze(2).to_broadcast([P, KD, P])),
            [free, self.mod_ready])
        done = []
        for h in range(2):
            b = self.banks.take()
            bank = self.banks.banks[b]
            for k in range(4):
                y = self.product(bank[:, k * P:(k + 1) * P], [(spread[:, 4 * h + k, :], self.ident[:, :])],
                                 [x, self.banks.free[b]])
            cols = slice(h * HALF, (h + 1) * HALF)
            put = self.dve.put(lambda e, bank=bank, cols=cols: e.tensor_tensor(
                row[:, cols], bank[:, :], row[:, cols], ALU.mult), [y, g_ready])
            self.banks.release(b, [put])
            done.append(put)
        return done

    def second_projections(self, free, x2):
        a, s = self.arg, self.scratch
        x = [self.half, (self.place("h_hi", [P, KD, HALF], F32R), self.place("h_lo", [P, KD, HALF], F32R))]
        c = (self.place("c_hi", [P, KD, CTX], F32R), self.place("c_lo", [P, KD, CTX], F32R))
        ready = list(self.next_ready)
        stage = Ring([self.place(f"zstage{i}", [P, HALF]) for i in range(2)], free)
        self.z_stored = []

        def project_z(half):
            blocks = [self.weights_take("z") for _ in range(4)]
            for t in range(4 * half, 4 * half + 4):
                src, tok = x[half], slice(t % 4 * P, (t % 4 + 1) * P)
                terms = []
                for k in range(KD):
                    _, whi, wlo, _, _ = blocks[k // 2]
                    terms += [(src[0][:, k, tok], whi[:, k % 2, :]), (src[1][:, k, tok], whi[:, k % 2, :]),
                              (src[0][:, k, tok], wlo[:, k % 2, :])]
                b, y, done = self.into_bank([P, HALF], terms, [[q[3] for q in blocks], ready])
                i, st, sfree = stage.next()
                z = self.act.put(lambda e, y=y, st=st: e.activation(st[:, :], y, ACT.Silu), [done, sfree])
                self.banks.release(b, [z])
                out = self.store(s["z"][t * P:(t + 1) * P, :], st[:, :], [z])
                stage.free[i] = [out]
                self.z_stored.append(out)
                self.pump(4 if half == 1 or t >= 2 else 1 - t)
            for q in blocks:
                self.weights_done(q, done)
            self.prefetch()

        late = []
        self.streams = [[
            self.norm_steps(lambda t: (P, a["ctx_2"][0, t * P:(t + 1) * P, :], t * P, ()), range(CT), c[0], c[1],
                            self.mix_gain[:, 1, :], self.mod[:, 0:KD, 1], self.work, free, self.mix_gain_ready, late),
            self.norm_steps(lambda t: (P, s["x2"][t * P:(t + 1) * P, :], t * P - HALF, x2[t]), range(4, 8),
                            x[1][0], x[1][1], self.mix_gain[:, 0, :], self.mod[:, 0:KD, 0], self.work, free,
                            self.mix_gain_ready, late)]]
        project_z(0)
        self.finish_background()
        ready = [ready, late]
        W = S + CTX + 8
        C0 = S + 6
        ring = Ring([(self.place(f"pad{i}", [P, W]), self.place(f"acc{i}", [P, W - 4])) for i in range(2)], free)
        rows = Ring([self.place(f"rows{i}", [P, NT + CT, P]) for i in range(2)], free)
        for i, (pad, _) in enumerate(ring.slots):
            z = [self.dve.put(lambda e, pad=pad, c=c0, n=n: e.memset(pad[:, c:c + n], 0.0), free)
                 for c0, n in ((0, 2), (S + 2, 4), (W - 2, 2))]
            ring.free[i] = z
        work = []
        boxes = []
        self.streams = [work, boxes]
        stored = []
        pool_step = self.pooling(x, ready, free)

        def convolve(j, i, pad, acc, put):
            width = S if j < 4 else W - 4
            token = self.dve.put(lambda e: e.tensor_scalar(acc[:, :width], pad[:, 0:width],
                                                           self.vec[:, 3, j:j + 1], None, ALU.mult), [put, self.vec_ready])
            for tap in range(1, CONV5):
                token = self.dve.put(lambda e, tap=tap: e.scalar_tensor_tensor(
                    acc[:, :width], pad[:, tap:tap + width], self.vec[:, 3, 12 * tap + j:12 * tap + j + 1],
                    acc[:, :width], ALU.mult, ALU.add), [token])
                if tap % 2 == 0:
                    yield
            token = self.act.put(lambda e: e.activation(acc[:, :width], acc[:, :width], ACT.Silu), [token])
            yield
            tiles = [t * P for t in range(NT)] + ([S + 4, S + 4 + P] if j >= 4 else [])
            r, row, rfree = rows.next()
            done = []
            for t0 in range(0, len(tiles), 4):
                part = tiles[t0:t0 + 4]
                b, bank, turned = self.transposes([acc[:, t:t + P] for t in part], [token])
                dst = row[:, t0:t0 + len(part), :].rearrange("p t c -> p (t c)")
                n = len(part) * P
                y = self.act.put(lambda e, dst=dst, bank=bank, n=n: e.activation(dst, bank[:, :n], ACT.Copy), [turned, rfree])
                self.banks.release(b, [y])
                done.append(y)
                yield
            ring.free[i] = [turned]
            n = len(tiles)
            out = self.store(s["qkv"].rearrange("t p c -> p t c")[:, 0:n, j * P:(j + 1) * P], row[:, 0:n, :], done)
            rows.free[r] = [out]
            stored.append(out)

        for j in range(12):
            i, (pad, acc), pfree = self.next_slot(ring)
            block = self.weights_take("qkv")
            put = []
            parts = [(x[0], slice(0, HALF), 2), (x[1], slice(0, HALF), 2 + HALF)] + \
                ([(c, slice(0, CTX), C0)] if j >= 4 else [])
            for src, sl, at in parts:
                n = sl.stop - sl.start
                b, y, done = self.into_bank([P, n], self.column_terms(block, src, KD, sl), [block[3], ready])
                z = self.act.put(lambda e, y=y, at=at, n=n, pad=pad: e.activation(pad[:, at:at + n], y, ACT.Copy), [done, pfree])
                self.banks.release(b, [z])
                put.append(z)
                self.pump(3)
            self.weights_done(block, done)
            self.prefetch()
            ring.free[i] = None
            work.append(convolve(j, i, pad, acc, put))
            if j in POOL_AFTER:
                boxes.append(pool_step(POOL_AFTER.index(j)))
        block = self.weights_take("dn_gates")
        b = self.banks.take()
        bank = self.banks.banks[b]
        _, whi, wlo, _, _ = block
        for t in range(NT + CT):
            src, tok = (x[t // 4] if t < NT else c), slice(t % 4 * P, (t % 4 + 1) * P)
            terms = []
            for k in range(KD):
                terms += [(src[0][:, k, tok], whi[:, k, :]), (src[1][:, k, tok], whi[:, k, :]), (src[0][:, k, tok], wlo[:, k, :])]
            done = self.product(bank[:, 16 * t:16 * t + 16], terms, [block[3], ready, self.banks.free[b]])
        self.weights_done(block, done)
        put = self.dve.put(lambda e: e.tensor_copy(self.gate_in[:, :, :].rearrange("p t c -> p (t c)"),
                                                   bank[:, 0:16 * (NT + CT)]), [done, free])
        self.banks.release(b, [put])
        self.delta_gates(put, free)
        project_z(1)
        self.finish_background()
        self.qkv_stored = stored

    def delta_gates(self, put, free):
        a = self.arg
        n = NT + CT
        at, self.cursor = self.cursor, self.before_half + self.work_size - 4 * n * 32 - 64
        bias, lg = self.place("dt_row", [P, 8]), self.place("alog_row", [P, 8])
        pos, e, s2, q = (self.place(f"soft{i}", [P, n, 8]) for i in range(4))
        assert self.cursor <= self.before_half + self.work_size
        self.cursor = at
        free = [free, self.pe.last(), self.act.last(), self.dve.last(), *(c.last() for c in self.misc)]
        l1 = self.load(bias[:, :], broadcast(a["dt_bias_2"], 8), free, lane=self.sp)
        l2 = self.load(lg[:, :], broadcast(a["a_log_2"], 8), free, lane=self.sp)
        beta = self.act.put(lambda v: v.activation(self.beta[:, :, :], self.gate_in[:, :, 0:8], ACT.Sigmoid), [put, free])
        rate = self.act.put(lambda v: v.activation(lg[:, :], lg[:, :], ACT.Exp), [l2])
        av = self.gate_in[:, :, 8:16]
        x = self.dve.put(lambda v: v.tensor_tensor(av, av, bias[:, :].unsqueeze(1).to_broadcast([P, n, 8]), ALU.add),
                         [put, l1, beta])
        self.dve.put(lambda v: v.tensor_scalar(pos[:, :, :], av, 0.0, None, ALU.max), [x, free])
        x = self.dve.put(lambda v: v.tensor_scalar(e[:, :, :], av, -1.0, None, ALU.mult), [x])
        x = self.dve.put(lambda v: v.tensor_tensor(e[:, :, :], e[:, :, :], av, ALU.min), [x])
        x = self.act.put(lambda v: v.activation(e[:, :, :], e[:, :, :], ACT.Exp), [x])
        x = self.dve.put(lambda v: v.tensor_scalar(q[:, :, :], e[:, :, :], 2.0, None, ALU.add), [x])
        x = self.dve.put(lambda v: v.reciprocal(q[:, :, :], q[:, :, :]), [x])
        x = self.dve.put(lambda v: v.tensor_tensor(e[:, :, :], e[:, :, :], q[:, :, :], ALU.mult), [x])
        x = self.dve.put(lambda v: v.tensor_tensor(s2[:, :, :], e[:, :, :], e[:, :, :], ALU.mult), [x])
        x = self.dve.put(lambda v: v.tensor_scalar(q[:, :, :], s2[:, :, :], 1.0 / 19, None, ALU.mult), [x])
        for k in range(8, 0, -1):
            x = self.dve.put(lambda v, k=k: v.scalar_tensor_tensor(q[:, :, :], q[:, :, :], 1.0 / (2 * k + 1), s2[:, :, :],
                                                                   ALU.add, ALU.mult), [x])
        x = self.dve.put(lambda v: v.scalar_tensor_tensor(q[:, :, :], q[:, :, :], 1.0, e[:, :, :], ALU.add, ALU.mult), [x])
        x = self.dve.put(lambda v: v.scalar_tensor_tensor(q[:, :, :], q[:, :, :], 2.0, pos[:, :, :], ALU.mult, ALU.add), [x])
        x = self.dve.put(lambda v: v.scalar_tensor_tensor(self.decay[:, :, :], q[:, :, :], -1.0,
                                                          lg[:, :].unsqueeze(1).to_broadcast([P, n, 8]),
                                                          ALU.mult, ALU.mult), [x, rate])
        self.gates_ready = [x, beta]

    def pooling(self, x, ready, free):
        a, s = self.arg, self.scratch
        at, self.cursor = self.cursor, self.before_half
        cols = [self.place(f"pc{i}", [P, GRID_H, GRID_W + 16]) for i in range(2)]
        u = self.place("pu", [P, S])
        pw = self.place("pw", [P, P])
        assert self.cursor <= self.before_half + self.work_size
        self.cursor = at
        free = [free, self.pe.last(), self.act.last(), self.dve.last(), *(c.last() for c in self.misc)]
        rws = [self.place(f"pr{i}", [P, GRID_H + 16, GRID_W]) for i in range(2)]
        inv = self.place("pinv", [P, S])
        y_sb = inv
        self.pool_stored = []
        state = {"last": list(free)}

        def step(g):
            while state["last"] is None:
                self.pump()
            last, state["last"] = state["last"], None
            lw = self.load(pw[:, :], a["pool_w_2"][0, g], [last], lane=self.sp)
            li = self.load(inv[:, :], broadcast(a["k_pool"][g:g + 1, :], S), [last], lane=self.sp)
            zeros = [self.dve.put(lambda e, r=r: e.memset(r[:, :, :], 0.0), last) for r in (cols[0], rws[0])]
            block = self.weights_take("pool")
            put = []
            for n in range(2):
                b, y, done = self.into_bank([P, HALF], self.column_terms(block, x[n], KD, slice(0, HALF)),
                                            [block[3], ready])
                z = self.act.put(lambda e, y=y, n=n: e.activation(u[:, n * HALF:(n + 1) * HALF], y, ACT.Copy), [done, last])
                self.banks.release(b, [z])
                put.append(z)
            self.weights_done(block, done)
            self.prefetch()
            return box(g, WINDOWS[g], last, lw, li, zeros, put)

        def box(g, window, last, lw, li, zeros, put):
            grid = u[:, :].rearrange("p (r c) -> p r c", c=GRID_W)
            tok = self.dve.put(lambda e: e.tensor_copy(cols[0][:, :, 8:8 + GRID_W], grid), [put, zeros])
            src = 0
            m = 1
            while m < window:
                reach = window // 2 - m
                lo_, n_ = 8 - reach, GRID_W + 2 * reach
                l_, r_ = (1, 0) if m == 1 else (m // 2, m // 2)
                tok = self.dve.put(lambda e, src=src, lo_=lo_, n_=n_, l_=l_, r_=r_: e.tensor_tensor(
                    cols[1 - src][:, :, lo_:lo_ + n_], cols[src][:, :, lo_ - l_:lo_ - l_ + n_],
                    cols[src][:, :, lo_ + r_:lo_ + r_ + n_], ALU.add), [tok])
                src, m = 1 - src, 2 * m
                yield
            tok = self.dve.put(lambda e, src=src: e.tensor_copy(rws[0][:, 8:8 + GRID_H, :], cols[src][:, :, 8:8 + GRID_W]), [tok])
            src, m = 0, 1
            while m < window:
                reach = window // 2 - m
                lo_, n_ = 8 - reach, GRID_H + 2 * reach
                l_, r_ = (1, 0) if m == 1 else (m // 2, m // 2)
                tok = self.dve.put(lambda e, src=src, lo_=lo_, n_=n_, l_=l_, r_=r_: e.tensor_tensor(
                    rws[1 - src][:, lo_:lo_ + n_, :], rws[src][:, lo_ - l_:lo_ - l_ + n_, :],
                    rws[src][:, lo_ + r_:lo_ + r_ + n_, :], ALU.add), [tok])
                src, m = 1 - src, 2 * m
                yield
            boxed = rws[src][:, 8:8 + GRID_H, :].rearrange("p r c -> p (r c)")
            tok = self.dve.put(lambda e, box=boxed: e.tensor_tensor(inv[:, :], box, inv[:, :], ALU.mult), [tok, li])
            tok = self.dve.put(lambda e: e.tensor_tensor(u[:, :], inv[:, :], u[:, :], ALU.subtract), [tok])
            outs = []
            for n in range(2):
                sl = slice(n * HALF, (n + 1) * HALF)
                b, y, done = self.into_bank([P, HALF], [(pw[:, :], u[:, sl])], [tok, lw])
                z = self.act.put(lambda e, y=y, sl=sl, g=g: e.activation(y_sb[:, sl], y, ACT.Copy,
                                                                        scale=self.v_pool[:, g:g + 1]), [done, last])
                self.banks.release(b, [z])
                outs.append(z)
            out = self.store(s["pooled"][g], y_sb[:, :], outs)
            self.pool_stored.append(out)
            state["last"] = [out, done, self.dve.last()]
        return step


    def delta_rule(self, free):
        a, s = self.arg, self.scratch
        o_sb = self.place("o_sum", [P, NT, DW])
        after_o = self.cursor
        kT = self.place("kT", [P, NT + CT, DW])
        qT = self.place("qT", [P, NT, DW])
        tri = self.place("tri", [P, 5, P])
        levels = self.place("levels", [P, 2, LEVELS, P])
        ones = self.place("ones", [P, P])
        ecol = self.place("ecol", [P, 4, NT + CT, DH])
        bcol = self.place("bcol", [P, 2, NT + CT, DH])
        floor = self.cursor
        consts = [self.load(tri[:, :, :].rearrange("p a b -> p (a b)"), a["k_tri"], free, lane=self.sp),
                  self.load(levels[:, :, :, :].rearrange("p a b c -> p (a b c)"), a["k_levels"], free, lane=self.sp),
                  self.dve.put(lambda e: e.memset(ones[:, :], 1.0), free)]
        b = self.banks.take()
        bank = self.banks.banks[b]
        n = (NT + CT) * DH
        for m, (t, d) in enumerate(((0, 0), (1, 1), (3, 0), (2, 1))):
            done = self.product(bank[:, m * n:(m + 1) * n].rearrange("p (t h) -> p t h", h=DH),
                                [(tri[:, t, :], self.decay[:, :, DH * d:DH * d + DH])],
                                [consts, self.gates_ready, self.banks.free[b]])
        x = self.act.put(lambda e, bank=bank: e.activation(ecol[:, :, :, :].rearrange("p a t h -> p (a t h)"),
                                                           bank[:, 0:4 * n], ACT.Exp), [done, free])
        self.banks.release(b, [x])
        for d in range(2):
            x2 = self.dve.put(lambda e, d=d: e.tensor_tensor(bcol[:, d, :, :], self.beta[:, :, DH * d:DH * d + DH],
                                                             ecol[:, d, :, :], ALU.mult), [x, free])
        cols_ready = [x, x2]
        ring = Ring([self.place(f"qkv{i}", [P, 3 * DW]) for i in range(2)], free)
        sq = self.place("sq", [P, 2 * DW])
        st = Ring([self.place(f"qst{i}", [P, 8]) for i in range(2)], free)
        turned_ready, k_stored = {}, {}
        sq_free = list(free)
        for t in range(NT + CT):
            c0, heads = (0, 8) if t < NT else (DW, 4)
            i, q, qfree = ring.next()
            j, r, rfree = st.next()
            landed = self.load(q[:, c0:2 * DW], s["qkv"][t, :, c0:2 * DW], [qfree, self.qkv_stored], lane=self.sp)
            w = heads * P
            qk3 = q[:, c0:2 * DW].rearrange("p (h d) -> p h d", d=P)
            x = self.dve.put(lambda e, q=q, c0=c0, w=w: e.tensor_tensor(sq[:, :w], q[:, c0:2 * DW], q[:, c0:2 * DW], ALU.mult),
                             [landed, sq_free])
            x = self.dve.put(lambda e, r=r, w=w, heads=heads: e.tensor_reduce(
                r[:, 0:heads], sq[:, :w].rearrange("p (h d) -> p h d", d=P), AX.X, ALU.add), [x, rfree])
            sq_free = [x]
            x = self.inverse_root(r[:, 0:heads], r[:, 0:heads], 1.0, RMS_EPS, [x])
            if t < NT:
                x = self.dve.put(lambda e, r=r: e.tensor_scalar(r[:, 0:4], r[:, 0:4], float(P) ** -0.5, None, ALU.mult), [x])
            x = self.dve.put(lambda e, qk3=qk3, r=r, heads=heads: e.tensor_tensor(
                qk3, qk3, r[:, 0:heads].unsqueeze(2).to_broadcast([P, heads, P]), ALU.mult), [x])
            st.free[j] = [x]
            out = self.store(s["qkv"][t, :, DW:2 * DW], q[:, DW:2 * DW], [x])
            k_stored[t] = out
            done = []
            for col, dst in ((0, qT), (DW, kT)):
                if col < c0:
                    continue
                b, bank, turned = self.transposes([q[:, col + h * P:col + (h + 1) * P] for h in range(DH)], [x])
                put = self.act.put(lambda e, dst=dst, bank=bank, t=t: e.activation(dst[:, t, :], bank[:, :], ACT.Copy),
                                   [turned, free])
                self.banks.release(b, [put])
                done.append(put)
            turned_ready[t] = done
            ring.free[i] = [out, turned]
        setup = [self.pe.last(), self.act.last(), self.dve.last(), list(k_stored.values())]
        self.phase += 1
        self.cursor = floor
        shape = [P, DH, P]
        state = [self.place(f"state{d}", shape) for d in range(2)]
        tmp = [{n: self.place(f"{n}{d}", shape) for n in ("A", "L", "C", "Y", "T", "W", "DT", "kbe", "vb")} for d in range(2)]
        kv = [Ring([self.place(f"kv{d}{i}", [P, 2 * DW]) for i in range(1)], setup) for d in range(2)]
        outs = [{n: self.place(f"{n}{d}", shape) for n in ("wT", "u", "kdec", "qdT", "attnT", "E", "vn")} for d in range(2)]
        state_ready = [self.dve.put(lambda e, st=st: e.memset(st[:, :, :], 0.0), setup) for st in state]
        tmp_free = [list(setup), list(setup)]
        outs_free = [list(setup), list(setup)]
        o_ready = {}
        order = [[NT, NT + 1] + list(range(NT)), [NT + 1, NT] + list(range(NT - 1, -1, -1))]
        prepared = [{}, {}]

        def heads(x):
            return x[:, :, :].rearrange("p h c -> p (h c)")

        def four(bank):
            return bank[:, :].rearrange("p (h c) -> p h c", h=DH)

        def wide(x):
            return x.unsqueeze(1).to_broadcast([P, DH, P])

        def each(fn, after):
            b = self.banks.take()
            bank = self.banks.banks[b]
            for h in range(DH):
                lhsT, rhs = fn(h)
                token = self.product(bank[:, h * P:(h + 1) * P], [(lhsT, rhs)], [after, self.banks.free[b]] if h == 0 else ())
            return b, bank, token

        def prepare(d, t):
            m, out = tmp[d], outs[d]
            is_x = t < NT
            tri_in, strict = (tri[:, 0, :], tri[:, 3, :]) if d == 0 else (tri[:, 1, :], tri[:, 2, :])
            free = tmp_free[d]
            i, kvt, kvfree = kv[d].next()
            landed = self.load(kvt[:, :], s["qkv"][t, :, DW:3 * DW], [kvfree, k_stored[t]], lane=self.sp)
            k3 = kvt[:, 0:DW].rearrange("p (h c) -> p h c", h=DH)
            v3 = kvt[:, DW:2 * DW].rearrange("p (h c) -> p h c", h=DH)

            def by_row(col):
                return col.unsqueeze(2).to_broadcast([P, DH, P])
            A = self.dve.put(lambda e: e.tensor_tensor(m["A"][:, :, :], wide(tri_in),
                                                       by_row(self.decay[:, t, DH * d:DH * d + DH]), ALU.mult),
                             [free, self.gates_ready, consts])
            b, bank, x = each(lambda h: (m["A"][:, h, :], strict), [A])
            D = self.act.put(lambda e, bank=bank: e.activation(heads(m["L"]), bank[:, :], ACT.Exp), [x, free])
            self.banks.release(b, [D])
            b, bank, x = each(lambda h: (kT[:, t, h * P:(h + 1) * P], kT[:, t, h * P:(h + 1) * P]), [turned_ready[t]])
            for h in range(DH):
                L = self.dve.put(lambda e, h=h, bank=bank: e.scalar_tensor_tensor(
                    m["L"][:, h, :], bank[:, h * P:(h + 1) * P], self.beta[:, t, DH * d + h:DH * d + h + 1], m["L"][:, h, :],
                    ALU.mult, ALU.mult), [x, D])
            self.banks.release(b, [L])
            kbe = self.pool.put(lambda e: e.tensor_tensor(m["kbe"][:, :, :], k3, by_row(bcol[:, d, t, :]), ALU.mult),
                                [landed, cols_ready, free])
            vb = self.pool.put(lambda e: e.tensor_tensor(m["vb"][:, :, :], v3,
                                                         by_row(self.beta[:, t, DH * d:DH * d + DH]), ALU.mult),
                               [landed, free])
            yield
            c = self.pool.put(lambda e: e.tensor_tensor(m["C"][:, :, :], m["L"][:, :, :], wide(levels[:, d, 0, :]), ALU.mult), [L, free])
            T = self.dve.put(lambda e: e.tensor_tensor(m["T"][:, :, :], wide(self.ident[:, :]), m["C"][:, :, :], ALU.subtract), [c, free])
            b, bank, x = self.transposes([m["C"][:, h, :] for h in range(DH)], [c])
            W = self.dve.put(lambda e, bank=bank: e.tensor_tensor(m["W"][:, :, :], wide(self.ident[:, :]), four(bank), ALU.subtract), [x, free])
            self.banks.release(b, [W])
            yield
            for lv in range(1, LEVELS):
                c = self.pool.put(lambda e, lv=lv: e.tensor_tensor(m["C"][:, :, :], m["L"][:, :, :],
                                                                   wide(levels[:, d, lv, :]), ALU.mult), [x, T])
                b, bank, x = each(lambda h: (m["C"][:, h, :], m["W"][:, h, :]), [c, W])
                Y = self.act.put(lambda e, bank=bank: e.activation(heads(m["Y"]), bank[:, :], ACT.Copy), [x, free, T])
                self.banks.release(b, [Y])
                yield
                b, bank, x = each(lambda h: (m["T"][:, h, :], m["Y"][:, h, :]), [Y, T])
                if lv < LEVELS - 1:
                    b2, bank2, x2 = each(lambda h: (m["Y"][:, h, :], m["T"][:, h, :]), [Y, T])
                W = self.dve.put(lambda e, bank=bank: e.tensor_tensor(heads(m["W"]), heads(m["W"]), bank[:, :], ALU.subtract), [x])
                self.banks.release(b, [W])
                if lv < LEVELS - 1:
                    T = self.dve.put(lambda e, bank=bank2: e.tensor_tensor(heads(m["T"]), heads(m["T"]), bank[:, :], ALU.subtract), [x2])
                    self.banks.release(b2, [T])
                    x = x2
                yield
            ofree = outs_free[d]
            if ofree is None:
                while outs_free[d] is None:
                    yield
                ofree = outs_free[d]
            b, bank, x = each(lambda h: (m["kbe"][:, h, :], m["W"][:, h, :]), [kbe, W])
            wT = self.act.put(lambda e, bank=bank: e.activation(heads(out["wT"]), bank[:, :], ACT.Copy), [x, ofree])
            self.banks.release(b, [wT])
            b, bank, x = each(lambda h: (m["W"][:, h, :], m["vb"][:, h, :]), [vb, W])
            u = self.act.put(lambda e, bank=bank: e.activation(heads(out["u"]), bank[:, :], ACT.Copy), [x, ofree])
            self.banks.release(b, [u])
            kdec = self.pool.put(lambda e: e.tensor_tensor(out["kdec"][:, :, :], k3, by_row(ecol[:, 2 + d, t, :]), ALU.mult), [ofree, kbe])
            kv[d].free[i] = [kdec, vb]
            yield
            b, bank, x = self.into_bank([P, HALF], [(ones[:, :], heads(m["A"]))], [A])
            E = self.act.put(lambda e, bank=bank: e.activation(heads(out["E"]), bank, ACT.Exp), [x, ofree])
            self.banks.release(b, [E])
            done = [wT, u, kdec, E]
            if is_x:
                qd = self.dve.put(lambda e: e.tensor_tensor(heads(out["qdT"]), qT[:, t, :], heads(out["E"]), ALU.mult), [E, ofree, turned_ready[t]])
                b, bank, x = self.into_bank([P, HALF], [(strict, heads(m["A"]))], [A])
                DT = self.act.put(lambda e, bank=bank: e.activation(heads(m["DT"]), bank, ACT.Exp), [x, free])
                self.banks.release(b, [DT])
                DT = self.dve.put(lambda e: e.tensor_tensor(m["DT"][:, :, :], m["DT"][:, :, :], wide(tri_in), ALU.mult), [DT])
                yield
                b, bank, x = each(lambda h: (kT[:, t, h * P:(h + 1) * P], qT[:, t, h * P:(h + 1) * P]), ())
                at = self.dve.put(lambda e, bank=bank: e.tensor_tensor(heads(out["attnT"]), heads(m["DT"]), bank[:, :], ALU.mult), [DT, x, ofree])
                self.banks.release(b, [at])
                done += [qd, at]
            tmp_free[d] = [self.pe.last(), self.act.last(), self.dve.last(), kbe, vb, c]
            outs_free[d] = None
            prepared[d][t] = done

        def recur(d, t):
            while t not in prepared[d]:
                yield
            ready = prepared[d][t]
            out, S_ = outs[d], state[d]
            is_x = t < NT
            if is_x:
                bo = self.banks.take()
                bank_o = self.banks.banks[bo]
            for n, c in enumerate((0, 1) if d == 0 else (1, 0)):
                R = slice(c * CHUNK, (c + 1) * CHUNK)
                last = c * CHUNK + (CHUNK - 1 if d == 0 else 0)
                b = self.banks.take()
                bank = self.banks.banks[b]
                for h in range(DH):
                    x = self.product(bank[R, h * P:(h + 1) * P], [(out["wT"][:, h, R], S_[:, h, :])],
                                     [ready, state_ready[d], self.banks.free[b]] if h == 0 else ())
                if is_x:
                    for h in range(DH):
                        xo = self.pe.put(lambda e, h=h, R=R: e.matmul(
                            bank_o[R, h * P:(h + 1) * P], out["qdT"][:, h, R], S_[:, h, :],
                            start=h == 0, stop=False, skip_group_check=True), [self.banks.free[bo]])
                vn = self.dve.put(lambda e, R=R, bank=bank: e.tensor_tensor(
                    out["vn"][R, :, :].rearrange("p h c -> p (h c)"), out["u"][R, :, :].rearrange("p h c -> p (h c)"),
                    bank[R, :], ALU.subtract), [x, outs_free_at[d]])
                self.banks.release(b, [vn])
                yield
                b = self.banks.take()
                bank = self.banks.banks[b]
                for h in range(DH):
                    x = self.product(bank[:, h * P:(h + 1) * P], [(out["kdec"][R, h, :], out["vn"][R, h, :])],
                                     [vn, self.banks.free[b]] if h == 0 else ())
                for h in range(DH):
                    st = self.dve.put(lambda e, h=h, bank=bank, last=last: e.scalar_tensor_tensor(
                        S_[:, h, :], S_[:, h, :], out["E"][:, h, last:last + 1], bank[:, h * P:(h + 1) * P],
                        ALU.mult, ALU.add), [x, xo if is_x else ()])
                self.banks.release(b, [st])
                state_ready[d] = [st]
                yield
            if is_x:
                for h in range(DH):
                    x = self.pe.put(lambda e, h=h: e.matmul(
                        bank_o[:, h * P:(h + 1) * P], out["attnT"][:, h, :], out["vn"][:, h, :],
                        start=False, stop=True, skip_group_check=True), [vn])
                if t not in o_ready:
                    o = self.act.put(lambda e: e.activation(o_sb[:, t, :], bank_o[:, :], ACT.Copy), [x, free_o])
                else:
                    o = self.dve.put(lambda e: e.tensor_tensor(o_sb[:, t, :], o_sb[:, t, :], bank_o[:, :], ALU.add),
                                     [x, o_ready[t]])
                o_ready[t] = [o]
                self.banks.release(bo, [o])
            outs_free_at[d] = [self.pe.last(), self.dve.last()]
            outs_free[d] = outs_free_at[d]

        free_o = free
        outs_free_at = [list(setup), list(setup)]
        self.streams = [[prepare(d, t) for t in order[d]] for d in range(2)] + \
                       [[recur(d, t) for t in order[d]] for d in range(2)]
        self.finish_background()
        self.o_ready = list(o_ready.values())
        self.cursor = after_o
        return o_sb

    def second_mix_outputs(self, free, o_sb, x2):
        a, s = self.arg, self.scratch
        self.post = self.place("post", [P, D])
        self.work = work = self.row_work(free)
        self.half = half_in = (self.place("half_hi", [P, KD, HALF + 2], F32R), self.place("half_lo", [P, KD, HALF + 2], F32R))
        self.after_half = self.cursor
        gain = self.place("mix_post", [P, D])
        spread = self.place("spread", [P, KD, P])
        gain_ready = self.modulated_row(gain, spread, a["g_post_mix_2"], 2, free)
        self.post_ready = self.modulated_row(self.post, spread, a["g_post_ffn_2"], 5, [free, gain_ready, self.pe.last()])
        norm = self.place("onorm", [P, P])
        nl = self.load(norm[:, :], broadcast(a["o_norm_2"], P), free)
        mix = [(self.place(f"mix{h}_hi", [P, KD, HALF], F32R), self.place(f"mix{h}_lo", [P, KD, HALF], F32R))
               for h in range(2)]
        z = Ring([self.place(f"zrow{i}", [P, DW]) for i in range(2)], free)
        pl = Ring([self.place(f"prow{i}", [P, HALF]) for i in range(2)], free)
        sq, st = self.place("osq", [P, DW]), self.place("ost", [P, DH])

        def rows(half, ready):
            hi, lo = mix[half]
            for t in range(4):
                i, q, qfree = pl.next()
                l = self.load(q[:, :], s["pooled"][t, :, half * HALF:(half + 1) * HALF], [qfree, self.pool_stored], lane=self.sp)
                parts = self.split(q[:, :], hi[:, 4 + t, :], lo[:, 4 + t, :], [l], free)
                pl.free[i] = parts
                ready += parts
                tile = half * 4 + t
                o = o_sb[:, tile, :]
                o3 = o.rearrange("p (h d) -> p h d", h=DH)
                i, zr, zfree = z.next()
                lz = self.load(zr[:, :], s["z"][tile * P:(tile + 1) * P, :], [zfree, self.z_stored], lane=self.sp)
                x = self.dve.put(lambda e, o=o: e.tensor_tensor(sq[:, :], o, o, ALU.mult), [self.o_ready, free])
                x = self.dve.put(lambda e: e.tensor_reduce(st[:, :], sq[:, :].rearrange("p (h d) -> p h d", h=DH), AX.X, ALU.add), [x])
                x = self.inverse_root(st[:, :], st[:, :], 1.0 / P, RMS_EPS, [x])
                x = self.dve.put(lambda e, o3=o3: e.tensor_tensor(o3, o3, st[:, :].unsqueeze(2).to_broadcast([P, DH, P]), ALU.mult), [x])
                x = self.dve.put(lambda e, o3=o3: e.tensor_tensor(o3, o3, norm[:, :].unsqueeze(1).to_broadcast([P, DH, P]), ALU.mult), [x, nl])
                x = self.dve.put(lambda e, o=o, zr=zr: e.tensor_tensor(o, o, zr[:, :], ALU.mult), [x, lz])
                z.free[i] = [x]
                yield
                b, bank, turned = self.transposes([o[:, k * P:(k + 1) * P] for k in range(4)], [x])
                dst = slice(t * P, (t + 1) * P)
                parts = self.split(bank[:, :].rearrange("p (k t) -> p k t", k=4), hi[:, 0:4, dst], lo[:, 0:4, dst],
                                   [turned], free)
                self.banks.release(b, parts)
                ready += parts
            yield

        ready = [[], []]
        self.streams = [[rows(0, ready[0])]]
        self.finish_background()
        self.streams = [[rows(1, ready[1])]]
        self.x3_stored = stored = []
        self.next_ready = []
        for half in range(2):
            banks = self.project_rows("w_out", chunks(mix[half], KD), KD, ready[half], steps=3)
            stored += self.add_residual(
                banks, lambda t, half=half: (s["x2"][half * HALF + t * P:half * HALF + (t + 1) * P, :], x2),
                lambda t, half=half: s["x3"][half * HALF + t * P:half * HALF + (t + 1) * P, :], gain, work, gain_ready)
            if half == 0:
                self.streams = [[self.norm_steps(
                    lambda t: (P, s["x3"][t * P:(t + 1) * P, :], t * P, stored[t]), range(4), half_in[0], half_in[1],
                    self.ffn_gain[:, 0, :], self.mod[:, 3 * KD:4 * KD, 0], work, free, self.ffn_gain_ready,
                    self.next_ready)]]

def chunks(parts, n):
    return [(parts[0][:, k, :], parts[1][:, k, :]) for k in range(n)]


def broadcast(row, n):
    return bass.AP(tensor=row.tensor, offset=row.offset, ap=[[0, P], [1, n]])


def bank_view(bank, shape):
    return bank[:shape[0], :shape[1]]


def group_tokens(x, k, g, t):
    if g == 0:
        return x[:, k, t * P:(t + 1) * P]
    classes = CLASSES[g]
    first = t % (NT // classes) * P
    return x[:, k, :].rearrange("p (m c) -> p c m", c=classes)[:, t * classes // NT, first:first + P]


def class_order(dst, y, g, n):
    c = CLASSES[g]
    if c == 1:
        return dst[:, n * HALF:(n + 1) * HALF], y
    m = HALF // c
    return (dst[:, :].rearrange("p (c m) -> p m c", c=c)[:, n * m:(n + 1) * m, :],
            y.rearrange("p (m c) -> p m c", c=c))


def shifted(base, start, rows, cols):
    return bass.AP(tensor=base.tensor, offset=base.offset + start, ap=[[TOEP - 1, rows], [1, cols]])


def unit_stores(sums, u, g, pair):
    w = HD + 2
    cols = slice(2 * pair * w, (2 * pair + 2) * w)
    if g == 0:
        return [(sums.rearrange("(t p) w -> p t w", p=P)[:, :, cols], u[:, :, :, :].rearrange("p t h w -> p t (h w)"))]
    if g == 1:
        view = sums.rearrange("(h p c) w -> c p h w", h=2, c=4)
        return [(view[c][:, :, cols], u[:, 2 * c:2 * c + 2, :, :].rearrange("p t h w -> p t (h w)")) for c in range(4)]
    return [(sums.rearrange("(p t) w -> p t w", t=8)[:, :, cols], u[:, :, :, :].rearrange("p t h w -> p t (h w)"))]



GATES = [(name, slot, j) for j in range(KD) for slot, name in enumerate(("gate_attn", "gate_conv"))]
GATES_BEHIND = (0, 1, 1, 3)


def gates_behind(g, pair):
    at = sum(GATES_BEHIND) * g + sum(GATES_BEHIND[:pair])
    return GATES[at:at + GATES_BEHIND[pair]]


def column_blocks(w, name, cols, k=KD, width=P):
    return [(name, w.rearrange("(k p) n -> p k n", p=P)[:, :, c:c + width], k, width, True) for c in cols]


def row_blocks(w, name, c0, k_all):
    return [(name, w.rearrange("(k p) n -> p k n", p=P)[:, k:k + 2, c0:c0 + HALF], 2, HALF, True)
            for k in range(0, k_all, 2)]


def first_plan(a):
    w, plan = a["w_in"][0], []

    def glu(j):
        return column_blocks(w, "glu_gate", [GLU0 + D + j * P]) + column_blocks(w, "glu_u", [GLU0 + j * P])
    plan += glu(0) + glu(1)
    for g in range(NG):
        base = g * NH * HD
        plan += row_blocks(w, "v", 2 * ATTN_W + base, KD)
        for pair in range(NH // 2):
            plan += column_blocks(w, "q", [base + pair * P]) + column_blocks(w, "k", [ATTN_W + base + pair * P])
            if pair % 2:
                plan += glu(2 + 2 * g + pair // 2)
            for name, slot, j in gates_behind(g, pair):
                plan += column_blocks(w, name, [(GA0, GC0)[slot] + j * P])
    name, slot, j = GATES[-1]
    plan += column_blocks(w, name, [(GA0, GC0)[slot] + j * P])
    mod = a["w_mod_2"][0].rearrange("(k p) n -> p k n", p=P)
    mods = [("mod", mod[:, :, j * P:(j + 1) * P], KD, P, False) for j in range(6 * KD)]
    for _ in range(2):
        for j in range(KD):
            plan += column_blocks(a["w_conv_out"][0], "conv_out", [j * P])
            plan += column_blocks(a["w_attn_out"][0], "attn_out", [j * P], k=4)
            plan.append(mods.pop(0))
        for c in range(2):
            plan += row_blocks(a["w_mix_out"][0], "mix_out", c * HALF, KD)
    return plan + ffn_plan(a["w_ffn_in"][0], a["w_ffn_out"][0], ("ffn_gate", "ffn_up", "ffn_down"), mods)


def second_plan(a):
    w = a["w_in_2"][0]
    plan = row_blocks(w, "z", 3 * DW, KD)
    for j in range(12):
        plan += column_blocks(w, "qkv", [j * P])
        if j in POOL_AFTER:
            plan += column_blocks(w, "pool", [POOL0 + POOL_AFTER.index(j) * P])
    plan += column_blocks(w, "dn_gates", [GATE0], width=16)
    plan += row_blocks(w, "z", 3 * DW, KD)
    for _ in range(2):
        for c in range(2):
            plan += row_blocks(a["w_out_2"][0], "w_out", c * HALF, KD)
    return plan + ffn_plan(a["w_up_2"][0], a["w_down_2"][0], ("up_gate", "up", "down"))


def ffn_plan(w_in, w_out, names, between=()):
    between = list(between)
    plan = []
    for _ in range(2):
        for j in range(KF):
            plan += column_blocks(w_in, names[0], [j * P]) + column_blocks(w_in, names[1], [FFN + j * P])
            if between:
                plan.append(between.pop(0))
        for c in range(2):
            plan += row_blocks(w_out, names[2], c * HALF, KF)
    return plan


def build(nc, arg, scratch, out, blocks=2):
    ctx = ExitStack()
    with ctx:
        p = Program(nc, ctx, arg, scratch, out)
        a, s = arg, scratch
        plan = first_plan(a)
        if blocks == 2:
            plan += second_plan(a)
        p.weights_begin(plan)
        p.prefetch()
        p.setup()
        floor = p.cursor
        free = p.begin_phase(floor)
        p.first_mix_projections(free)
        free = p.begin_phase(floor)
        x1 = p.first_mix_outputs(free)
        free = p.begin_phase(p.after_half)
        post_ready = p.load(p.post[:, :], broadcast(a["g_post_ffn"], D), free)
        target = s["x2"] if blocks == 2 else out[0]

        def then(half_free, stored):
            p.mix_gain_ready = p.modulated_gain(p.mix_gain, p.v_g_pre_mix_2, 1, 2)
            p.ffn_gain_ready = p.modulated_gain(p.ffn_gain, p.v_g_pre_ffn_2, 4, 1)
            p.next_ready = []
            return p.norm_steps(lambda t: (P, s["x2"][t * P:(t + 1) * P, :], t * P, stored[t]), range(4), p.half[0],
                                p.half[1], p.mix_gain[:, 0, :], p.mod[:, 0:KD, 0], p.work, half_free,
                                p.mix_gain_ready, p.next_ready)
        x2 = p.feed_forward(free, lambda r, n: (s["x1"][r:r + n, :], x1[r // P]), lambda r: target[r:r + P, :],
                            p.v_g_pre_ffn, None, p.vec_ready, post_ready, None, ("ffn_gate", "ffn_up", "ffn_down"),
                            then=then)
        if blocks == 2:
            p.second_block(floor, x2)
        p.pool.put(lambda e: e.memset(p.mean[0:1, 0:1], 1.0 / D), [x.last() for x in p.misc])
        block = ctx.enter_context(nc.Block())
        block.sync(p.sp.play)
        block.gpsimd(p.pool.play)
        block.scalar(p.act.play)
        block.vector(p.dve.play)
        block.tensor(p.pe.play)


_OUTS = [((1, S, D), "float32")]
_SCRATCH = {
    "toeplitz": (NG * NH, P * TOEP), "sums": (NG, S, NH * (HD + 2)), "gates": (2, KD, P, S), "conv": (KD, P, S),
    "x1": (S, D), "x2": (S, D), "x3": (S, D), "qkv": ((NT + CT), P, 3 * DW), "z": (S, DW), "pooled": (4, P, S),
}


def kernel(**inputs):
    import concourse.bacc as _bacc
    from concourse.bass_utils import run_bass_kernel_spmd as _run

    nc = _bacc.Bacc("TRN2", target_bir_lowering=False, num_devices=1)
    arrays, arg = {}, {}
    for name, value in {**inputs, **constants()}.items():
        value = np.ascontiguousarray(value)
        arrays[f"in_{name}_dram"] = value
        arg[name] = nc.dram_tensor(f"in_{name}_dram", value.shape, mybir.dt.from_np(value.dtype),
                                   kind="ExternalInput").ap()
    scratch = {name: nc.dram_tensor(f"scratch_{name}", shape, F32, kind="Internal").ap()
               for name, shape in _SCRATCH.items()}
    outs = [nc.dram_tensor(f"out_{i}_dram", shape, mybir.dt.from_np(np.dtype(dtype)), kind="ExternalOutput").ap()
            for i, (shape, dtype) in enumerate(_OUTS)]
    build(nc, arg, scratch, outs[0])
    r = _run(nc, [arrays], core_ids=[0])
    return r.results[0]["out_0_dram"]
```
